# Optimizing a Trainium2 kernel written in Bass

```python
import math
import jax, jax.numpy as jnp
from jax import lax
import numpy as np

D_MODEL = 1024
BATCH = 1
SEQ = 512
DEPTH = 1

N_Q_HEADS = 8
N_KV_HEADS = 2
HEAD_DIM = 64
ATTN_WIDTH = N_Q_HEADS * HEAD_DIM
WINDOW = 128
BLOCK = 128
CONV_WIDTH = D_MODEL - ATTN_WIDTH
CONV_K = 3
QKV_COLS = (N_Q_HEADS + 2 * N_KV_HEADS) * HEAD_DIM
IN_COLS = QKV_COLS + 3 * CONV_WIDTH
N_EXPERTS = 32
TOP_K = 4
D_FF = D_MODEL
SWIGLU_ALPHA = 1.702
SWIGLU_LIMIT = 7.0
MOE_BLOCK = 128
EPS = 1e-5

kernel_name = "hymba_conv_swa_sink_alibi_moe"

def rmsnorm(x, g):
    x32 = x.astype(jnp.float32)
    y = x32 * lax.rsqrt(jnp.mean(x32 * x32, axis=-1, keepdims=True) + EPS)
    return (y * g.astype(jnp.float32)).astype(x.dtype)

def alibi_slopes(n_heads):
    return jnp.exp2(-8.0 * jnp.arange(1, n_heads + 1, dtype=jnp.float32) / n_heads)

def sliding_window_attention(q, k, v, sinks):
    bsz, s_len = q.shape[0], q.shape[1]
    nb = s_len // BLOCK
    grp = N_Q_HEADS // N_KV_HEADS
    qb = q.reshape(bsz, nb, BLOCK, N_KV_HEADS, grp, HEAD_DIM)
    kb = k.reshape(bsz, nb, BLOCK, N_KV_HEADS, HEAD_DIM)
    vb = v.reshape(bsz, nb, BLOCK, N_KV_HEADS, HEAD_DIM)

    def band(t):
        prev = jnp.concatenate([jnp.zeros_like(t[:, :1]), t[:, :-1]], axis=1)
        return jnp.concatenate([prev, t], axis=2)

    kband, vband = band(kb), band(vb)
    scale = 1.0 / math.sqrt(HEAD_DIM)
    s = jnp.einsum('bnqhgd,bnshd->bnhgqs', qb, kband,
                   preferred_element_type=jnp.float32) * scale

    qi = jnp.arange(BLOCK)[:, None]
    kj = jnp.arange(2 * BLOCK)[None, :]
    dist = qi + BLOCK - kj
    kpos = jnp.arange(nb)[:, None, None] * BLOCK + kj[None] - BLOCK
    valid = (dist >= 0) & (dist < WINDOW) & (kpos >= 0)

    slopes = alibi_slopes(N_Q_HEADS).reshape(N_KV_HEADS, grp)
    s = s - slopes[:, :, None, None] * dist.astype(jnp.float32)
    s = jnp.where(valid[None, :, None, None], s, -jnp.inf)

    sink = sinks.astype(jnp.float32).reshape(N_KV_HEADS, grp)[None, None, :, :, None, None]
    sink = jnp.broadcast_to(sink, s.shape[:-1] + (1,))
    p = jax.nn.softmax(jnp.concatenate([s, sink], axis=-1), axis=-1)[..., :-1]
    o = jnp.einsum('bnhgqs,bnshd->bnqhgd', p.astype(v.dtype), vband)
    return o.reshape(bsz, s_len, ATTN_WIDTH)

def short_conv(b_gate, c_gate, x_in, conv_w):
    u = c_gate * x_in
    s_len = u.shape[1]
    u_pad = jnp.pad(u, ((0, 0), (CONV_K - 1, 0), (0, 0)))
    y = (conv_w[0] * u_pad[:, 0:s_len]
         + conv_w[1] * u_pad[:, 1:s_len + 1]
         + conv_w[2] * u_pad[:, 2:s_len + 2])
    return b_gate * y

def clamped_swiglu(hu):
    x_glu, x_lin = hu[..., :D_FF], hu[..., D_FF:]
    x_glu = jnp.minimum(x_glu, SWIGLU_LIMIT)
    x_lin = jnp.clip(x_lin, -SWIGLU_LIMIT, SWIGLU_LIMIT)
    return x_glu * jax.nn.sigmoid(SWIGLU_ALPHA * x_glu) * (x_lin + 1.0)

def moe(h, w_router, b_router, w1, b1, w2, b2):
    bsz, s_len, d = h.shape
    n_tok = bsz * s_len
    xt = h.reshape(n_tok, d)
    logits = (xt @ w_router + b_router).astype(jnp.float32)
    top_val, top_idx = lax.top_k(logits, TOP_K)
    gates = jax.nn.softmax(top_val, axis=-1).astype(h.dtype)

    nk = n_tok * TOP_K
    e_flat = top_idx.reshape(nk)
    tok_flat = jnp.arange(nk, dtype=jnp.int32) // TOP_K
    g_flat = gates.reshape(nk)
    order = jnp.argsort(e_flat)
    e_sorted, tok_sorted, g_sorted = e_flat[order], tok_flat[order], g_flat[order]

    counts = jnp.bincount(e_flat, length=N_EXPERTS)
    padded = (counts + MOE_BLOCK - 1) // MOE_BLOCK * MOE_BLOCK
    starts = jnp.cumsum(counts) - counts
    pstarts = jnp.cumsum(padded) - padded
    pends = pstarts + padded
    dest = pstarts[e_sorted] + (jnp.arange(nk, dtype=jnp.int32) - starts[e_sorted])

    n_rows = (nk + MOE_BLOCK - 1) // MOE_BLOCK * MOE_BLOCK + N_EXPERTS * MOE_BLOCK
    n_blocks = n_rows // MOE_BLOCK
    row_tok = jnp.full((n_rows,), n_tok, jnp.int32).at[dest].set(tok_sorted)
    row_gate = jnp.zeros((n_rows,), h.dtype).at[dest].set(g_sorted)
    blk_start = jnp.arange(n_blocks, dtype=jnp.int32) * MOE_BLOCK
    blk_expert = jnp.minimum(jnp.searchsorted(pends, blk_start, side='right'), N_EXPERTS - 1)

    x_pad = jnp.concatenate([xt, jnp.zeros((1, d), xt.dtype)], axis=0)
    x_rows = x_pad[row_tok].reshape(n_blocks, MOE_BLOCK, d)

    def expert_block(args):
        xb, e = args
        act = clamped_swiglu(xb @ w1[e] + b1[e])
        return act @ w2[e] + b2[e]

    y_rows = lax.map(expert_block, (x_rows, blk_expert)).reshape(n_rows, d)
    out = jax.ops.segment_sum(y_rows * row_gate[:, None], row_tok, num_segments=n_tok + 1)[:n_tok]
    return out.reshape(bsz, s_len, d)

def setup_inputs(seed: int = 0) -> dict:
    key = jax.random.key(seed)
    ks = jax.random.split(key, 16)
    f32 = jnp.float32
    nrm = lambda k, shape, scale: jax.random.normal(k, shape, f32) * scale
    return {
        'x': nrm(ks[0], (BATCH, SEQ, D_MODEL), 1.0),
        'g_mix': 1.0 + nrm(ks[1], (DEPTH, D_MODEL), 0.02),
        'w_in': nrm(ks[2], (DEPTH, D_MODEL, IN_COLS), D_MODEL ** -0.5),
        'conv_w': nrm(ks[3], (DEPTH, CONV_K, CONV_WIDTH), CONV_K ** -0.5),
        'sinks': nrm(ks[4], (DEPTH, N_Q_HEADS), 0.5),
        'g_attn_out': 1.0 + nrm(ks[5], (DEPTH, ATTN_WIDTH), 0.02),
        'g_conv_out': 1.0 + nrm(ks[6], (DEPTH, CONV_WIDTH), 0.02),
        'w_out': nrm(ks[7], (DEPTH, D_MODEL, D_MODEL), D_MODEL ** -0.5),
        'g_ffn': 1.0 + nrm(ks[8], (DEPTH, D_MODEL), 0.02),
        'w_router': nrm(ks[9], (DEPTH, D_MODEL, N_EXPERTS), D_MODEL ** -0.5),
        'b_router': nrm(ks[10], (DEPTH, N_EXPERTS), 0.01),
        'w1': nrm(ks[11], (DEPTH, N_EXPERTS, D_MODEL, 2 * D_FF), D_MODEL ** -0.5),
        'b1': nrm(ks[12], (DEPTH, N_EXPERTS, 2 * D_FF), 0.02),
        'w2': nrm(ks[13], (DEPTH, N_EXPERTS, D_FF, D_MODEL), D_FF ** -0.5),
        'b2': nrm(ks[14], (DEPTH, N_EXPERTS, D_MODEL), 0.02),
        'g_final': 1.0 + nrm(ks[15], (D_MODEL,), 0.02),
    }

def reference(x, g_mix, w_in, conv_w, sinks, g_attn_out, g_conv_out, w_out,
              g_ffn, w_router, b_router, w1, b1, w2, b2, g_final):
    bsz, s_len, _ = x.shape
    split_at = [ATTN_WIDTH, ATTN_WIDTH + N_KV_HEADS * HEAD_DIM, QKV_COLS,
                QKV_COLS + CONV_WIDTH, QKV_COLS + 2 * CONV_WIDTH]
    for l in range(DEPTH):
        h = rmsnorm(x, g_mix[l])
        p = h @ w_in[l]
        q, k, v, b_gate, c_gate, x_in = jnp.split(p, split_at, axis=-1)
        q = q.reshape(bsz, s_len, N_Q_HEADS, HEAD_DIM)
        k = k.reshape(bsz, s_len, N_KV_HEADS, HEAD_DIM)
        v = v.reshape(bsz, s_len, N_KV_HEADS, HEAD_DIM)
        attn = sliding_window_attention(q, k, v, sinks[l])
        conv = short_conv(b_gate, c_gate, x_in, conv_w[l])
        mix = jnp.concatenate([rmsnorm(attn, g_attn_out[l]),
                               rmsnorm(conv, g_conv_out[l])], axis=-1)
        x = x + mix @ w_out[l]
        h = rmsnorm(x, g_ffn[l])
        x = x + moe(h, w_router[l], b_router[l], w1[l], b1[l], w2[l], b2[l])
    return rmsnorm(x, g_final)


_drawn_inputs = setup_inputs


def setup_inputs(seed=0):
    import zlib

    import numpy as np

    out = dict(_drawn_inputs(seed))
    spreads = {}
    factors = {'b1': 6.77, 'b2': 7.859, 'g_final': 2.865}
    for name, (base, spread) in spreads.items():
        noise = np.random.default_rng([zlib.crc32(name.encode()), seed]).standard_normal(out[name].shape)
        drawn = base * np.exp(spread * noise) if base else spread * noise
        out[name] = __import__('jax').numpy.asarray(drawn.astype(out[name].dtype))
    for name, factor in factors.items():
        out[name] = (out[name] * factor).astype(out[name].dtype)
    return out
```

```python
from contextlib import ExitStack

import concourse.bass as bass
from concourse import mybir

F32 = mybir.dt.float32
F32R = mybir.dt.float32r
BF16 = mybir.dt.bfloat16
I32 = mybir.dt.int32
U32 = mybir.dt.uint32
ALU = mybir.AluOpType
ACT = mybir.ActivationFunctionType
AX_X = mybir.AxisListType.X

P = 128
D = 1024
SEQ = 512
TB = SEQ // P
KT = D // P
HEADS, KV_HEADS, HD = 8, 2, 64
GRP = HEADS // KV_HEADS
AW = HEADS * HD
CW = D - AW
CT = CW // P
CONV_K = 3
QKV = (HEADS + 2 * KV_HEADS) * HD
CONV_COLS = 3 * CW
E = 32
TOPK = 4
FF = 1024
STEPS = 4
FC = FF // STEPS
FK = FC // P
PIECES = 4
PK = KT // PIECES
PIECE = PK * 2 * FC
ALPHA = 1.702
LIMIT = 7.0
EPS = 1e-5
NEG = -1e30
UNUSED = 1 << 20
ROWS = SEQ * TOPK
LIST_BLOCKS = SEQ // P
MAX_OVERFLOW = ROWS // (P + 1)
OVF_ROWS = 16


def head_place(h):
    return (h % 2) * (HEADS // 2) + h // 2


def place_head(at):
    return (at % (HEADS // 2)) * 2 + at // (HEADS // 2)


def layer_kernel(nc, x, g_mix, w_in, conv_w, sinks, g_attn_out, g_conv_out, w_out,
                 g_ffn, w_router, b_router, w1, b1, w2, b2, g_final, out):
    ctx = ExitStack()
    with ctx:
        def sb(name, shape, dt=F32):
            return ctx.enter_context(nc.sbuf_tensor(name, shape, dt))

        def sb_r(name, shape, offset):
            return nc.alloc_sbuf_tensor_at(name, shape, F32R, offset=offset)

        def sem(name):
            return ctx.enter_context(nc.semaphore(name))

        h2_dram = nc.dram_tensor("h2_rows", (SEQ, D), F32).ap()
        list_dram = nc.dram_tensor("slot_list", (SEQ * E, 2), I32).ap()
        y_dram = nc.dram_tensor("expert_rows", (ROWS, D), F32).ap()

        ovf_dram = nc.dram_tensor("overflow_table", (OVF_ROWS, 4), I32).ap()

        X = sb("X", [P, TB, D])
        gain_a = sb("gain_a", [P, D])
        gain_ffn = sb("gain_ffn", [P, D])
        gain_attn = sb("gain_attn", [P, AW])
        ring1 = sb("ring1", [P, STEPS * KT * 2 * FC])
        w1_lo = sb_r("w1_lo", [P, STEPS, PIECES, PIECE], nc.sbuf_base - STEPS * KT * 2 * FC * 4)
        ring2 = sb("ring2", [P, STEPS * FK * D])
        xnT = sb("xnT", [P, KT, SEQ])
        normed = sb("normed", [P, 2, D])
        scores = sb("scores", [P, HEADS, 2 * P])
        probsT = sb("probsT", [P, HEADS, 2, P])
        blockT_hi = sb_r("blockT_hi", [P, 2, KT, P], nc.sbuf_base - HEADS * 2 * P * 4)
        mixer = sb("mixer", [P, PIECES * PIECE + 2 * KT * P])
        w1_hi = sb_r("w1_hi", [P, PIECES, PIECE], nc.sbuf_base - (PIECES * PIECE + 2 * KT * P) * 4)
        blockT_lo = sb_r("blockT_lo", [P, 2, KT, P], nc.sbuf_base - 2 * KT * P * 4)
        u_pad = sb("u_pad", [P, SEQ + CONV_K - 1])
        conv_y = sb("conv_y", [P, SEQ])
        attn_o = sb("attn_o", [P, AW])
        bias_split = sb("bias_split", [3 * E, 2 * FF + D], BF16)
        expert_sel = sb("expert_sel", [3 * E, E], BF16)
        bias_sel = sb("bias_sel", [3 * E, 2, P], BF16)
        ident = sb("ident", [P, P])
        earlier = sb("earlier", [P, P], BF16)
        ones_bf = sb("ones_bf", [P, P], BF16)
        ones_col = sb("ones_col", [P, 1])
        ones_row = sb("ones_row", [1, P])
        upto = sb("upto", [E, E], BF16)
        ident_bf = sb("ident_bf", [E, E], BF16)
        iota_e = sb("iota_e", [P, TOPK, E])
        iota_o = sb("iota_o", [OVF_ROWS, 1])
        eps_col = sb("eps_col", [P, 1])
        w_rt = sb("w_rt", [P, KT, E])
        b_rt = sb("b_rt", [1, E])
        conv_wc = sb("conv_wc", [P, CONV_K, CT])
        g_conv = sb("g_conv", [P, CT])
        sink_b = sb("sink_b", [P, HEADS])
        stat = sb("stat", [P, 80])
        r_conv = sb("r_conv", [P, TB])
        smax = sb("smax", [P, 6, HEADS])
        esink = sb("esink", [P, HEADS])
        logit = sb("logit", [P, 2, E])
        top8 = sb("top8", [P, 2, 8])
        top8_i = sb("top8_i", [P, 2, 8], U32)
        top_e = sb("top_e", [P, 2, TOPK])
        top_x = sb("top_x", [P, 2, TOPK])
        rt_small = sb("rt_small", [P, 2, 4])
        onehot = sb("onehot", [P, 2, TOPK, E])
        chosen = sb("chosen", [P, TB, E], BF16)
        chosen_cum = sb("chosen_cum", [P, TB + 1, E], BF16)
        rankrow = sb("rankrow", [P, 2, E])
        row_f = sb("row_f", [P, 2, TOPK])
        row_i = sb("row_i", [P, TB, TOPK], I32)
        entry = sb("entry", [P, TB, TOPK, 2], I32)
        slots = sb("slots", [P, LIST_BLOCKS, E, 2], I32)
        slot_tok = sb("slot_tok", [P, LIST_BLOCKS * E], I32)
        cur_slot = sb("cur_slot", [P, 2, 2], I32)
        cur_tok = sb("cur_tok", [P, 2, 1], I32)
        ovf_f = sb("ovf_f", [OVF_ROWS, 6])
        ovf_m = sb("ovf_m", [OVF_ROWS, 3, E])
        ovf_nb = sb("ovf_nb", [E, 4])
        ovf_nb16 = sb("ovf_nb16", [E, OVF_ROWS], BF16)
        ovf_tab = sb("ovf_tab", [OVF_ROWS, 4], I32)
        ovf_row = sb("ovf_row", [1, OVF_ROWS * 4], I32)

        ps = ctx.enter_context(nc.psum_tensor("ps", [P, 8, 512], F32))

        w_conv_sb = ring1[:, 0:KT * CONV_COLS].rearrange("p (k c) -> p k c", k=KT)
        spare = KT * CONV_COLS
        alibi = ring1[:, spare:spare + HEADS * 2 * P].rearrange("p (h s) -> p h s", h=HEADS)
        bias_raw = ring1[0:3 * E, spare + HEADS * 2 * P:spare + HEADS * 2 * P + 2 * FF]
        w_qkv_sb = ring2[:, 0:KT * QKV].rearrange("p (k c) -> p k c", k=KT)
        w_out_sb = ring2[:, :].rearrange("p (k n) -> p k n", k=KT)
        ring1_v = ring1[:, :].rearrange("p (s k h c) -> p s k h c", s=STEPS, k=KT, h=2)
        ring2_v = ring2[:, :].rearrange("p (s k n) -> p s k n", s=STEPS, k=FK)
        list_fill = slots[:, :, :, :].rearrange("p b e w -> p (b e w)")
        conv_sq = normed[:, :, :].rearrange("p a (c t) -> p (a c) t", c=2)
        qT = mixer[:, 0:4 * SEQ].rearrange("p (a t) -> p a t", a=HEADS // 2)
        kT = mixer[:, 4 * SEQ:6 * SEQ].rearrange("p (g t) -> p g t", g=KV_HEADS)
        v_sb = mixer[:, 6 * SEQ:7 * SEQ].rearrange("p (t d) -> p t d", t=TB)
        c_gate = mixer[:, 7 * SEQ:8 * SEQ]
        convT = mixer[:, 8 * SEQ:12 * SEQ].rearrange("p (c t) -> p c t", c=CT)
        attnT = qT
        picked = attn_o[:, 0:TOPK * E].rearrange("p (k e) -> p k e", k=TOPK)
        gathered = scores[:, :, :].rearrange("p (b c) s -> p b (c s)", b=2)
        gated_y = normed
        step_v = xnT[:, :, :].rearrange("p k t -> p (k t)")
        glu_c = step_v[:, 0:2 * FC].rearrange("p (b c) -> p b c", b=2)
        lin_c = step_v[:, 2 * FC:4 * FC].rearrange("p (b c) -> p b c", b=2)
        sig = step_v[:, 4 * FC:6 * FC].rearrange("p (b c) -> p b c", b=2)
        prod = step_v[:, 6 * FC:8 * FC].rearrange("p (b c) -> p b c", b=2)
        act_v = step_v[:, 8 * FC:10 * FC].rearrange("p (b c) -> p b c", b=2)
        actT = step_v[:, 10 * FC:12 * FC].rearrange("p (b k t) -> p b k t", b=2, k=FK)
        y_rows = ring1[:, :].rearrange("p (t k n) -> p t k n", t=TB, k=TOPK)

        X_SUM, X_STD, X_R, O_SUM, O_STD, O_R, C_STD, H_SUM, H_STD, H_R, F_SUM, F_STD, F_R = range(0, 13 * TB, TB)

        B_H, B_Y, B_T, B_X = 0, 2, 4, 5
        ps_y = ps[:, B_Y:B_Y + 2, :].rearrange("p b n -> p (b n)")

        x_in = [sem(f"x_in{t}") for t in range(TB)]
        gains_in, small_in = sem("gains_in"), sem("small_in")
        qkv_in, conv_in, wout_in = sem("qkv_in"), sem("conv_in"), sem("wout_in")
        bias1_in, bias2_in, gfinal_in = sem("bias1_in"), sem("bias2_in"), sem("gfinal_in")
        w1_in = [sem(f"w1_in{j}") for j in range(STEPS)]
        w2_in = [sem(f"w2_in{j}") for j in range(STEPS)]
        dve_step, act_step, pool_step = sem("dve_step"), sem("act_step"), sem("pool_step")
        consts_ready, alibi_ready, biases_ready = sem("consts_ready"), sem("alibi_ready"), sem("biases_ready")
        std_ready, xn_ready, xn_turned = sem("std_ready"), sem("xn_ready"), sem("xn_turned")
        xnT_a, xnT_b = sem("xnT_a"), sem("xnT_b")
        k_ready, k_doubled = sem("k_ready"), sem("k_doubled")
        proj_done, proj_act, proj_dve = sem("proj_done"), sem("proj_act"), sem("proj_dve")
        scores_done, scores_read = sem("scores_done"), sem("scores_read")
        negmax_ready, exp_done = sem("negmax_ready"), sem("exp_done")
        convproj_done, c_ready, conv_read = sem("convproj_done"), sem("c_ready"), sem("conv_read")
        convy_ready, sq_ready, convT_ready = sem("convy_ready"), sem("sq_ready"), sem("convT_ready")
        probs_turned, pT_act, pT_dve = sem("probs_turned"), sem("pT_act"), sem("pT_dve")
        pv_done, o_ready, ostd_ready, on_ready = sem("pv_done"), sem("o_ready"), sem("ostd_ready"), sem("on_ready")
        o_turned, attnT_ready = sem("o_turned"), sem("attnT_ready")
        csum_done, cstd_ready, rconv_ready = sem("csum_done"), sem("cstd_ready"), sem("rconv_ready")
        oproj_done, x2_ready, std2_ready, h2_ready = sem("oproj_done"), sem("x2_ready"), sem("std2_ready"), sem("h2_ready")
        h2_turned, h2_stored = sem("h2_turned"), sem("h2_stored")
        h2T_a, h2T_b = sem("h2T_a"), sem("h2T_b")
        logits_done, logits_read, negtop_ready, gexp_ready = sem("logits_done"), sem("logits_read"), sem("negtop_ready"), sem("gexp_ready")
        chosen_ready, rank_done, entries_ready = sem("chosen_ready"), sem("rank_done"), sem("entries_ready")
        counts_done, nb_ready, prefix_done, ovf_ready, ovf_in = sem("counts_done"), sem("nb_ready"), sem("prefix_done"), sem("ovf_ready"), sem("ovf_in")
        ovf_stored = sem("ovf_stored")
        list_filled, list_written, slots_in, tok_ready = sem("list_filled"), sem("list_written"), sem("slots_in"), sem("tok_ready")
        cur_copied, cur_ready = sem("cur_copied"), sem("cur_ready")
        rows_in = [sem(f"rows_in{b}") for b in range(2)]
        rows_cleared = sem("rows_cleared")
        rows_turned, rows_hi, rows_lo = sem("rows_turned"), sem("rows_hi"), sem("rows_lo")
        hi_ready, lo_ready, w1_used, slot_ready = sem("hi_ready"), sem("lo_ready"), sem("w1_used"), sem("slot_ready")
        h_read, glu_ready, sig_ready = sem("h_read"), sem("glu_ready"), sem("sig_ready")
        prod_ready, actv_ready, act_turned, actT_ready = sem("prod_ready"), sem("actv_ready"), sem("act_turned"), sem("actT_ready")
        w2_done, y_ready = sem("w2_done"), sem("y_ready")
        scatter_begun = sem("scatter_begun")
        y_out = [sem(f"y_out{b}") for b in range(2)]
        rows_ovf, y_ovf = sem("rows_ovf"), sem("y_ovf")
        all_scattered = sem("all_scattered")
        yrow_in = [sem(f"yrow_in{t}") for t in range(TB)]
        sum_ready, fstd_ready, fin_ready, out_written = sem("sum_ready"), sem("fstd_ready"), sem("fin_ready"), sem("out_written")
        dve_final, act_final = sem("dve_final"), sem("act_final")

        def raw_piece(j, q):
            return ring1_v[:, j, q * PK:(q + 1) * PK, :, :].rearrange("p k h c -> p (k h c)")

        block = ctx.enter_context(nc.Block())

        def expert_blocks(eng, run):
            run(0, 0)
            run(1, 1)
            with eng.Fori(2, E - 2, 2) as i:
                run(i, 0)
                run(i + 1, 1)
            run(E - 2, 0)
            run(E - 1, 1)

        def overflow_blocks(eng, run):
            eng.wait_ge(ovf_in, 16)
            n_ovf = eng.value_load(ovf_row[0:1, 2:3], min_val=0, max_val=MAX_OVERFLOW)
            with eng.Fori(0, MAX_OVERFLOW) as o:
                with eng.If(n_ovf > o):
                    run(o, o + E)

        @block.sync
        def _(sp):
            with nc.allow_non_contiguous_dma(reason="small parameter columns"):
                for t in range(TB):
                    sp.dma_start(X[:, t, :], x[0, t * P:(t + 1) * P, :]).then_inc(x_in[t], 16)
                    if t == 0:
                        sp.dma_start(gain_a[:, :], g_mix[0].partition_broadcast(P)).then_inc(gains_in, 16)
                w_in_v = w_in[0].rearrange("(k p) c -> p k c", p=P)
                for k in range(0, KT, 2):
                    sp.dma_start(w_qkv_sb[:, k:k + 2, :], w_in_v[:, k:k + 2, 0:QKV]).then_inc(qkv_in, 16)
                for odd in range(2):
                    sp.dma_start(sink_b[:, odd * HEADS // 2:(odd + 1) * HEADS // 2],
                                 sinks[0].rearrange("(a b) -> b a", b=2)[odd].partition_broadcast(P)).then_inc(small_in, 16)
                sp.dma_start(gain_attn[:, :], g_attn_out[0].partition_broadcast(P)).then_inc(small_in, 16)
                sp.dma_start(conv_wc[:, :, :], conv_w[0].rearrange("w (c p) -> p w c", p=P)).then_inc(small_in, 16)
                sp.dma_start(g_conv[:, :], g_conv_out[0].rearrange("(c p) -> p c", p=P)).then_inc(small_in, 16)
                for k in range(KT):
                    sp.dma_start(w_conv_sb[:, k, :], w_in_v[:, k, QKV:]).then_inc(conv_in, 16)
                sp.dma_start(gain_ffn[:, :], g_ffn[0].partition_broadcast(P)).then_inc(small_in, 16)
                sp.dma_start(w_rt[:, :, :], w_router[0].rearrange("(k p) e -> p k e", p=P)).then_inc(small_in, 16)
                sp.dma_start(b_rt[:, :], b_router).then_inc(small_in, 16)
            for g in range(3):
                sp.dma_start(bias_raw[g * E:(g + 1) * E, :], b1[0]).then_inc(bias1_in, 16)
            sp.wait_ge(xn_ready, TB)
            sp.dma_start(gain_a[:, :], g_final.partition_broadcast(P)).then_inc(gfinal_in, 16)
            sp.wait_ge(k_ready, 2)
            sp.dma_start(kT[HD:P, 0, :], kT[0:HD, 0, :]).then_inc(k_doubled, 16)
            sp.dma_start(kT[0:HD, 1, :], kT[HD:P, 1, :]).then_inc(k_doubled, 16)
            sp.wait_ge(proj_done, 6)
            w_out_v = w_out[0].rearrange("(k p) n -> p k n", p=P)
            for k in range(0, KT, 2):
                sp.dma_start(w_out_sb[:, k:k + 2, :], w_out_v[:, k:k + 2, :]).then_inc(wout_in, 16)
            sp.wait_ge(biases_ready, 1)
            for g in range(3):
                sp.dma_start(bias_raw[g * E:(g + 1) * E, 0:D], b2[0]).then_inc(bias2_in, 16)

            def load_w1(j, e):
                src = w1[0, e].rearrange("(k p) (h c) -> p k h c", p=P, h=2)
                for h in range(2):
                    sp.dma_start(ring1_v[:, j, :, h, :], src[:, :, h, j * FC:(j + 1) * FC]).then_inc(w1_in[j], 16)

            def load_w2(j, e):
                src = w2[0, e].rearrange("(s k p) n -> p s k n", p=P, k=FK)
                sp.dma_start(ring2_v[:, j, :, :], src[:, j, :, :]).then_inc(w2_in[j], 16)

            def load(i, _parity):
                for j in range(STEPS):
                    if isinstance(i, int) and i == 0:
                        if j == 0:
                            sp.wait_ge(convproj_done, CT)
                        if j == STEPS - 1:
                            sp.wait_ge(scores_read, TB)
                            sp.wait_ge(biases_ready, 2)
                        load_w1(j, i)
                        continue
                    sp.wait_ge(w1_used, ((i - 1) * STEPS + j + 1) * PIECES)
                    load_w1(j, i)
                    sp.wait_ge(w2_done, (i - 1) * STEPS + j + 1)
                    load_w2(j, i)
                if isinstance(i, int) and i == 0:
                    sp.wait_ge(oproj_done, TB)
                    for j in range(STEPS):
                        load_w2(j, i)

            expert_blocks(sp, load)

            def load_overflow(o, i):
                e = sp.value_load(ovf_row[0:1, bass.ds(o * 4, 1)], min_val=0, max_val=E - 1)
                for j in range(STEPS):
                    sp.wait_ge(w1_used, ((i - 1) * STEPS + j + 1) * PIECES)
                    load_w1(j, e)
                    sp.wait_ge(w2_done, (i - 1) * STEPS + j + 1)
                    load_w2(j, e)

            overflow_blocks(sp, load_overflow)

            sp.wait_ge(all_scattered, 1)
            y_dram_v = y_dram.rearrange("(t p k) n -> t p k n", p=P, k=TOPK)
            for t in range(TB):
                sp.dma_start(y_rows[:, t, :, :], y_dram_v[t]).then_inc(yrow_in[t], 16)
            for t in range(TB):
                sp.wait_ge(fin_ready, t + 1)
                sp.dma_start(out[0, t * P:(t + 1) * P, :], y_rows[:, t, 0, :]).then_inc(out_written, 16)
            sp.wait_ge(out_written, 16 * TB)

        @block.tensor
        def _(pe):
            mm = pe.matmul

            def turn_rows(src, bank):
                for k in range(KT):
                    ins = pe.transpose(ps[:, bank + k // 4, (k % 4) * P:(k % 4 + 1) * P],
                                       src[:, k * P:(k + 1) * P], ident[:, :])
                return ins

            pe.wait_ge(consts_ready, 1)
            for t in range(TB):
                pe.wait_ge(xn_ready, t + 1)
                if t >= 2:
                    pe.wait_ge(xnT_a, t - 1)
                    pe.wait_ge(xnT_b, t - 1)
                turn_rows(normed[:, t % 2, :], 2 * (t % 2)).then_inc(xn_turned, 1)

            pe.wait_ge(xnT_a, TB)
            pe.wait_ge(xnT_b, TB)
            pe.wait_ge(qkv_in, 16 * KT // 2)
            for n in range(GRP + 1):
                if n == 4:
                    pe.wait_ge(proj_dve, 1)
                for k in range(KT):
                    c0 = AW if n == 0 else (n - 1) * P
                    lhs = w_qkv_sb[:, k, c0:c0 + P]
                    ins = mm(ps[:, 4 + n % 4, :], lhs, xnT[:, k, :], start=(k == 0), stop=(k == KT - 1))
                ins.then_inc(proj_done, 1)
            pe.wait_ge(proj_act, 1)
            for t in range(TB):
                for k in range(KT):
                    ins = mm(ps[:, 5, t * P:(t + 1) * P], xnT[:, k, t * P:(t + 1) * P],
                             w_qkv_sb[:, k, AW + P:QKV], start=(k == 0), stop=(k == KT - 1))
            ins.then_inc(proj_done, 1)

            def turn_o(n):
                pe.wait_ge(on_ready, n + 1)
                if n >= 1:
                    pe.wait_ge(attnT_ready, n)
                for c in range(AW // P):
                    ins = pe.transpose(ps[:, 7, c * P:(c + 1) * P], attn_o[:, c * P:(c + 1) * P], ident[:, :])
                ins.then_inc(o_turned, 1)

            for n in range(TB):
                k0 = 0 if n else 1
                if n == 0:
                    pe.wait_ge(proj_dve, 3)
                    pe.wait_ge(proj_act, 2)
                    pe.wait_ge(k_doubled, 32)
                else:
                    pe.wait_ge(conv_read, n)
                for h in range(HEADS):
                    g, half, at = h // GRP, (h % 2) * HD, head_place(h)
                    ins = mm(ps[:, at // 2, (at % 2) * 2 * P + k0 * P:(at % 2 + 1) * 2 * P],
                             qT[half:half + HD, h // 2, n * P:(n + 1) * P],
                             kT[half:half + HD, g, (n - 1 + k0) * P:(n + 1) * P], start=True, stop=True)
                ins.then_inc(scores_done, 1)
                if n >= 1:
                    turn_o(n - 1)
                if n == 0:
                    pe.wait_ge(conv_in, 16 * KT)
                pe.wait_ge(scores_read, n + 1)
                for part in range(3):
                    for k in range(KT):
                        c0 = part * CW + n * P
                        ins = mm(ps[:, part, :], w_conv_sb[:, k, c0:c0 + P], xnT[:, k, :],
                                 start=(k == 0), stop=(k == KT - 1))
                ins.then_inc(convproj_done, 1)
                pe.wait_ge(exp_done, n + 1)
                if n == 0:
                    pe.wait_ge(proj_dve, 3)
                    pe.wait_ge(proj_act, 3)
                for c in range(GRP):
                    q = GRP * n + c
                    if q >= 2:
                        pe.wait_ge(pT_dve if c % 2 else pT_act, q // 2)
                    for h in (2 * c, 2 * c + 1):
                        for kb in range(k0, 2):
                            ins = pe.transpose(ps[:, 4 + c % 2, ((h % 2) * 2 + kb) * P:((h % 2) * 2 + kb + 1) * P],
                                               scores[:, h, kb * P:(kb + 1) * P], ident[:, :])
                    ins.then_inc(probs_turned, 1)
                pe.wait_ge(pT_act, 2 * (n + 1))
                pe.wait_ge(pT_dve, 2 * (n + 1))
                if n >= 1:
                    pe.wait_ge(o_ready, n)
                for h in range(HEADS):
                    g = h // GRP
                    for kb in range(k0, 2):
                        ins = mm(ps[:, 6, h * HD:(h + 1) * HD], probsT[:, head_place(h), kb, :],
                                 v_sb[:, n - 1 + kb, g * HD:(g + 1) * HD], start=(kb == k0), stop=(kb == 1))
                ins.then_inc(pv_done, 1)
            turn_o(TB - 1)

            pe.wait_ge(sq_ready, CT)
            pe.wait_ge(o_ready, TB)
            for t in range(TB):
                for c in range(CT):
                    ins = mm(ps[:, 6, t:t + 1], conv_sq[:, c, t * P:(t + 1) * P], ones_col[:, :],
                             start=(c == 0), stop=(c == CT - 1))
            ins.then_inc(csum_done, 1)

            def out_proj(t):
                g = 4 * (t % 2)
                if t == 0:
                    pe.wait_ge(wout_in, 16 * KT // 2)
                    pe.wait_ge(attnT_ready, TB)
                    pe.wait_ge(convT_ready, CT)
                    pe.wait_ge(conv_read, CT)
                if t == 1:
                    pe.wait_ge(cstd_ready, 1)
                    pe.wait_ge(pT_dve, 2 * TB)
                if t >= 2:
                    pe.wait_ge(h2T_a, t - 1)
                    pe.wait_ge(h2T_b, t - 1)
                    pe.wait_ge(entries_ready, t - 1)
                for half, src in enumerate((attnT, convT)):
                    for c in range(CT):
                        for n in range(2):
                            ins = mm(ps[:, g + 2 * half + n, :], src[:, c, t * P:(t + 1) * P],
                                     w_out_sb[:, half * CT + c, n * 512:(n + 1) * 512],
                                     start=(c == 0), stop=(c == CT - 1))
                ins.then_inc(oproj_done, 1)

            def route(t):
                g = 4 * (t % 2)
                pe.wait_ge(h2_ready, t + 1)
                pe.wait_ge(x2_ready, t + 1)
                turn_rows(normed[:, t % 2, :], g).then_inc(h2_turned, 1)
                pe.wait_ge(h2T_a, t + 1)
                pe.wait_ge(h2T_b, t + 1)
                if t == 0:
                    pe.wait_ge(small_in, 16 * 8)
                mm(ps[:, g + 2, 0:E], ones_row[:, :], b_rt[:, :], start=True, stop=False)
                for k in range(KT):
                    ins = mm(ps[:, g + 2, 0:E], xnT[:, k, t * P:(t + 1) * P], w_rt[:, k, :],
                             start=False, stop=(k == KT - 1))
                ins.then_inc(logits_done, 1)

            def rank(t):
                g = 4 * (t % 2)
                pe.wait_ge(chosen_ready, t + 1)
                if t == 0:
                    pe.wait_ge(consts_ready, 2)
                ins = mm(ps[:, g + 3, 0:E], earlier[:, :], chosen[:, t, :], start=True, stop=(t == 0))
                if t:
                    ins = mm(ps[:, g + 3, 0:E], ones_bf[:, :], chosen_cum[:, t, :], start=False, stop=True)
                ins.then_inc(rank_done, 1)

            for t in range(0, TB, 2):
                out_proj(t)
                out_proj(t + 1)
                route(t)
                route(t + 1)
                rank(t)
                rank(t + 1)
            pe.wait_ge(entries_ready, TB - 1)
            mm(ps[0:E, 0, 0:1], chosen_cum[:, TB, :], ones_bf[:, 0:1], start=True, stop=True).then_inc(counts_done, 1)
            pe.wait_ge(nb_ready, 1)
            mm(ps[0:OVF_ROWS, 1, 0:E], ovf_nb16[:, :], upto[:, :], start=True, stop=True)
            mm(ps[0:OVF_ROWS, 1, E:2 * E], ovf_nb16[:, :], ident_bf[:, :], start=True, stop=True).then_inc(prefix_done, 1)

            def turn_block(i, parity):
                pe.wait_ge(rows_in[parity], 16 * (i // 2 + 1) if isinstance(i, int) else half_up(i, parity) * 16)
                if not (isinstance(i, int) and i == 0):
                    pe.wait_ge(rows_lo, i * 2)
                turn_rows(gathered[:, parity, :], B_X).then_inc(rows_turned, 1)

            def half_up(i, parity):
                return (i + 2 - parity) // 2

            def w1_step(i, j, parity):
                s = i * STEPS + j
                if j == 0:
                    pe.wait_ge(rows_lo, (i + 1) * 2)
                    pe.wait_ge(cur_ready, i + 1)
                if not isinstance(s, int) or s >= 2:
                    pe.wait_ge(h_read, s - 1)
                h = ps[:, B_H + j % 2, :]
                mm(h, bias_sel[:, parity, :], bias_split[:, 0:2 * FF].rearrange("p (h c) -> p h c", h=2)[:, :, j * FC:(j + 1) * FC],
                   start=True, stop=False)
                for q in range(PIECES):
                    pe.wait_ge(lo_ready, s * PIECES + q + 1)
                    for k in range(q * PK, (q + 1) * PK):
                        cols = slice((k % PK) * 2 * FC, (k % PK + 1) * 2 * FC)
                        x_hi, x_lo = blockT_hi[:, parity, k, :], blockT_lo[:, parity, k, :]
                        mm(h, x_hi, w1_hi[:, q, cols], start=False, stop=False)
                        mm(h, x_hi, w1_lo[:, j, q, cols], start=False, stop=False)
                        ins = mm(h, x_lo, w1_hi[:, q, cols], start=False, stop=(k == KT - 1))
                    ins.then_inc(w1_used, 1)

            def turn_act(i, j):
                s = i * STEPS + j
                pe.wait_ge(actv_ready, s + 1)
                if not isinstance(s, int) or s >= 1:
                    pe.wait_ge(actT_ready, s)
                for k in range(FK):
                    ins = pe.transpose(ps[:, B_T, k * P:(k + 1) * P], act_v[:, j % 2, k * P:(k + 1) * P], ident[:, :])
                ins.then_inc(act_turned, 1)

            def w2_step(i, j, parity):
                s = i * STEPS + j
                pe.wait_ge(actT_ready, s + 1)
                pe.wait_ge(w2_in[j], (i + 1) * 16)
                if j == 0:
                    if not (isinstance(i, int) and i == 0):
                        pe.wait_ge(y_ready, i)
                    for n in range(2):
                        mm(ps[:, B_Y + n, :], bias_sel[:, parity, :], bias_split[:, 2 * FF + n * 512:2 * FF + (n + 1) * 512],
                           start=True, stop=False)
                for k in range(FK):
                    for n in range(2):
                        ins = mm(ps[:, B_Y + n, :], actT[:, j % 2, k, :], ring2_v[:, j, k, n * 512:(n + 1) * 512],
                                 start=False, stop=(j == STEPS - 1 and k == FK - 1))
                ins.then_inc(w2_done, 1)

            def compute(i, parity):
                first = isinstance(i, int) and i == 0
                last = isinstance(i, int) and i == E - 1
                w1_step(i, 0, parity)
                if not first:
                    turn_act(i - 1, 3)
                    w2_step(i - 1, 2, 1 - parity)
                w1_step(i, 1, parity)
                turn_act(i, 0)
                if not first:
                    w2_step(i - 1, 3, 1 - parity)
                w1_step(i, 2, parity)
                turn_act(i, 1)
                w2_step(i, 0, parity)
                if not last:
                    turn_block(i + 1, 1 - parity)
                w1_step(i, 3, parity)
                turn_act(i, 2)
                w2_step(i, 1, parity)

            def drain(i, parity):
                turn_act(i, 3)
                w2_step(i, 2, parity)
                w2_step(i, 3, parity)

            pe.wait_ge(biases_ready, 2)
            pe.wait_ge(ovf_ready, 1)
            turn_block(0, 0)
            expert_blocks(pe, compute)
            drain(E - 1, 1)

            def overflow(o, i):
                pe.wait_ge(rows_ovf, (o + 1) * 16)
                pe.wait_ge(rows_lo, i * 2)
                turn_rows(gathered[:, 0, :], B_X).then_inc(rows_turned, 1)
                for j in range(STEPS):
                    w1_step(i, j, 0)
                    if j >= 1:
                        turn_act(i, j - 1)
                    if j >= 2:
                        w2_step(i, j - 2, 0)
                drain(i, 0)

            overflow_blocks(pe, overflow)

        @block.vector
        def _(dve):
            v = nc.vector
            chain = [0]

            def then(ins):
                chain[0] += 1
                ins.then_inc(dve_step, 1)
                dve.wait_ge(dve_step, chain[0])

            def norm(src, dst, gain, std_col, r_col, done):
                then(v.reciprocal(stat[:, r_col:r_col + 1], stat[:, std_col:std_col + 1]))
                return v.scalar_tensor_tensor(out=dst, in0=src, scalar=stat[:, r_col:r_col + 1], in1=gain,
                                              op0=ALU.mult, op1=ALU.mult).then_inc(done, 1)

            def xnT_half(t, bank, done):
                return v.tensor_copy(xnT[:, 4:8, t * P:(t + 1) * P],
                                     ps[:, bank, :].rearrange("p (k t) -> p k t", k=4)).then_inc(done, 1)

            v.memset(u_pad[:, 0:CONV_K - 1], 0.0)
            then(v.memset(chosen_cum[:, 0, :], 0.0))

            dve.wait_ge(gains_in, 16)
            for t in range(TB):
                dve.wait_ge(std_ready, t + 1)
                if t >= 2:
                    dve.wait_ge(xn_turned, t - 1)
                norm(X[:, t, :], normed[:, t % 2, :], gain_a[:, :], X_STD + t, X_R + t, xn_ready)
                if t >= 1:
                    dve.wait_ge(xn_turned, t)
                    xnT_half(t - 1, 2 * ((t - 1) % 2) + 1, xnT_b)
            dve.wait_ge(xn_turned, TB)
            xnT_half(TB - 1, 2 * ((TB - 1) % 2) + 1, xnT_b)

            dve.wait_ge(proj_done, 1)
            v.tensor_copy(kT[0:HD, 0, :], ps[0:HD, 4, :]).then_inc(k_ready, 1)
            v.tensor_copy(kT[HD:P, 1, :], ps[HD:P, 4, :]).then_inc(k_ready, 1)
            dve.wait_ge(k_ready, 2)
            dve.sem_inc(proj_dve, 1)
            dve.wait_ge(proj_done, 3)
            v.tensor_copy(qT[:, 1, :], ps[:, 6, :]).then_inc(proj_dve, 1)
            dve.wait_ge(proj_done, 5)
            v.tensor_copy(qT[:, 3, :], ps[:, 4, :]).then_inc(proj_dve, 1)

            dve.wait_ge(alibi_ready, 1)
            dve.wait_ge(small_in, 16 * 8)
            for n in range(TB):
                k0 = 0 if n else 1
                s0 = k0 * P
                dve.wait_ge(scores_done, n + 1)
                if n >= 1:
                    dve.wait_ge(probs_turned, GRP * n)
                then(v.scalar_tensor_tensor(out=scores[:, :, s0:], in0=ps[:, 0:4, :].rearrange("p b (h s) -> p (b h) s", h=2)[:, :, s0:],
                                            scalar=HD ** -0.5, in1=alibi[:, :, s0:], op0=ALU.mult, op1=ALU.add))
                dve.sem_inc(scores_read, 1)
                then(v.tensor_reduce(smax[:, 0, :], scores[:, :, s0:], AX_X, ALU.max))
                then(v.tensor_tensor(smax[:, 1, :], smax[:, 0, :], sink_b[:, :], ALU.max))
                then(v.tensor_scalar(smax[:, 2, :], smax[:, 1, :], -1.0, None, ALU.mult))
                v.tensor_tensor(smax[:, 3, :], smax[:, 2, :], sink_b[:, :], ALU.add).then_inc(negmax_ready, 1)
                dve.wait_ge(exp_done, n + 1)
                then(v.tensor_tensor(smax[:, 5, :], smax[:, 4, :], esink[:, :], ALU.add))
                then(v.reciprocal(smax[:, 5, :], smax[:, 5, :]))
                dve.wait_ge(c_ready, n + 1)
                then(v.tensor_tensor(u_pad[:, CONV_K - 1:], c_gate, ps[:, 2, :], ALU.mult))
                if n >= 1:
                    dve.wait_ge(sq_ready, n)
                then(v.tensor_scalar(conv_y[:, :], u_pad[:, 0:SEQ], conv_wc[:, 0, n:n + 1], None, ALU.mult))
                for w in range(1, CONV_K):
                    then(v.scalar_tensor_tensor(out=conv_y[:, :], in0=u_pad[:, w:w + SEQ], scalar=conv_wc[:, w, n:n + 1],
                                                in1=conv_y[:, :], op0=ALU.mult, op1=ALU.add))
                then(v.tensor_tensor(conv_y[:, :], conv_y[:, :], ps[:, 0, :], ALU.mult))
                dve.sem_inc(conv_read, 1)
                dve.sem_inc(convy_ready, 1)
                v.tensor_scalar(convT[:, n, :], conv_y[:, :], g_conv[:, n:n + 1], None, ALU.mult).then_inc(convT_ready, 1)
                for c in (1, 3):
                    dve.wait_ge(probs_turned, GRP * n + c + 1)
                    if c == 1 and n >= 1:
                        dve.wait_ge(pv_done, n)
                    v.tensor_copy(probsT[:, 2 * c:2 * c + 2, k0:2, :],
                                  ps[:, 5, :].rearrange("p (h k t) -> p h k t", h=2, k=2)[:, :, k0:2, :]).then_inc(pT_dve, 1)
                dve.wait_ge(pv_done, n + 1)
                if n >= 1:
                    dve.wait_ge(o_turned, n)
                v.tensor_tensor(attn_o[:, :].rearrange("p (a b d) -> p a b d", b=2, d=HD), ps[:, 6, :].rearrange("p (a b d) -> p a b d", b=2, d=HD),
                                smax[:, 5, :].rearrange("p (b a) -> p a b", b=2).unsqueeze(3).to_broadcast([P, HEADS // 2, 2, HD]), ALU.mult).then_inc(o_ready, 1)
                dve.wait_ge(ostd_ready, n + 1)
                norm(attn_o[:, :], attn_o[:, :], gain_attn[:, :], O_STD + n, O_R + n, on_ready)

            dve.wait_ge(consts_ready, 2)
            dve.wait_ge(cstd_ready, 1)
            then(v.reciprocal(r_conv[:, :], stat[:, C_STD:C_STD + TB]))

            def residual(t):
                g = 4 * (t % 2)
                dve.wait_ge(oproj_done, t + 1)
                xt = X[:, t, :]
                then(v.tensor_tensor(xt, ps[:, g:g + 2, :].rearrange("p b n -> p (b n)"), xt, ALU.add))
                v.scalar_tensor_tensor(out=xt, in0=ps[:, g + 2:g + 4, :].rearrange("p b n -> p (b n)"), scalar=r_conv[:, t:t + 1],
                                       in1=xt, op0=ALU.mult, op1=ALU.add).then_inc(x2_ready, 1)
                dve.wait_ge(std2_ready, t + 1)
                if t >= 2:
                    dve.wait_ge(h2_turned, t - 1)
                    dve.wait_ge(h2_stored, 16 * t)
                norm(xt, normed[:, t % 2, :], gain_ffn[:, :], H_STD + t, H_R + t, h2_ready)

            def select(t):
                b = t % 2
                dve.wait_ge(logits_done, t + 1)
                then(v.tensor_copy(logit[:, b, :], ps[:, 4 * b + 2, 0:E]))
                then(v.max(top8[:, b, :], logit[:, b, :]))
                v.tensor_scalar(rt_small[:, b, 0:1], top8[:, b, 0:1], -1.0, None, ALU.mult).then_inc(negtop_ready, 1)
                then(v.max_index(top8_i[:, b, :], top8[:, b, :], logit[:, b, :]))
                then(v.tensor_copy(top_e[:, b, :], top8_i[:, b, 0:TOPK]))
                then(v.tensor_tensor(onehot[:, b, :, :], iota_e[:, :, :], top_e[:, b, :].unsqueeze(2).to_broadcast([P, TOPK, E]), ALU.is_equal))
                with nc.allow_low_precision(reason="sums of zeros and ones, at most 4"):
                    then(v.tensor_reduce(chosen[:, t, :], onehot[:, b, :, :].rearrange("p k e -> p e k"), AX_X, ALU.add))
                    v.tensor_tensor(chosen_cum[:, t + 1, :], chosen_cum[:, t, :], chosen[:, t, :], ALU.add).then_inc(chosen_ready, 1)
                dve.wait_ge(gexp_ready, t + 1)
                then(v.reciprocal(rt_small[:, b, 2:3], rt_small[:, b, 1:2]))
                then(v.tensor_scalar(entry[:, t, :, 1:2].bitcast(F32), top_x[:, b, :].unsqueeze(2), rt_small[:, b, 2:3], None, ALU.mult))

            def place(t):
                b = t % 2
                dve.wait_ge(rank_done, t + 1)
                then(v.scalar_tensor_tensor(out=rankrow[:, b, :], in0=ps[:, 4 * b + 3, 0:E], scalar=float(E), in1=iota_e[:, 0, :],
                                            op0=ALU.mult, op1=ALU.add))
                then(v.tensor_tensor(picked[:, :, :], onehot[:, b, :, :], rankrow[:, b, :].unsqueeze(1).to_broadcast([P, TOPK, E]), ALU.mult))
                then(v.tensor_reduce(row_f[:, b, :], picked[:, :, :], AX_X, ALU.add))
                v.tensor_copy(row_i[:, t, :], row_f[:, b, :]).then_inc(entries_ready, 1)

            for t in range(0, TB, 2):
                for u in (t, t + 1):
                    residual(u)
                for u in (t, t + 1):
                    dve.wait_ge(h2_turned, u + 1)
                    xnT_half(u, 4 * (u % 2) + 1, h2T_b)
                select(t)
                select(t + 1)
                place(t)
                place(t + 1)

            dve.wait_ge(counts_done, 1)
            then(v.tensor_copy(ovf_nb[:, 0:1], ps[0:E, 0, 0:1]))
            then(v.tensor_scalar(ovf_nb[:, 1:2], ovf_nb[:, 0:1], float(P), None, ALU.is_gt))
            for n in range(2, LIST_BLOCKS):
                then(v.tensor_scalar(ovf_nb[:, 2:3], ovf_nb[:, 0:1], float(n * P), None, ALU.is_gt))
                then(v.tensor_tensor(ovf_nb[:, 1:2], ovf_nb[:, 1:2], ovf_nb[:, 2:3], ALU.add))
            v.tensor_copy(ovf_nb16[:, :], ovf_nb[:, 1:2].to_broadcast([E, OVF_ROWS])).then_inc(nb_ready, 1)
            dve.wait_ge(prefix_done, 1)
            then(v.tensor_copy(ovf_m[:, 0:2, :].rearrange("p a e -> p (a e)"), ps[0:OVF_ROWS, 1, 0:2 * E]))
            dve.sem_inc(ovf_ready, 1)
            then(v.tensor_scalar(ovf_m[:, 2, :], ovf_m[:, 0, :], iota_o[:, 0:1], None, ALU.is_le))
            then(v.tensor_reduce(ovf_f[:, 0:1], ovf_m[:, 2, :], AX_X, ALU.add))
            then(v.tensor_scalar(ovf_f[:, 0:1], ovf_f[:, 0:1], float(E - 1), None, ALU.min))
            then(v.tensor_tensor(ovf_m[:, 1, :], ovf_m[:, 1, :], ovf_m[:, 2, :], ALU.mult))
            then(v.tensor_reduce(ovf_f[:, 1:2], ovf_m[:, 1, :], AX_X, ALU.add))
            then(v.tensor_tensor(ovf_f[:, 2:3], iota_o[:, :], ovf_f[:, 1:2], ALU.subtract))
            then(v.tensor_scalar(ovf_f[:, 2:3], ovf_f[:, 2:3], 1.0, float(E), ALU.add, ALU.mult))
            then(v.tensor_tensor(ovf_f[:, 1:2], ovf_f[:, 2:3], ovf_f[:, 0:1], ALU.add))
            then(v.tensor_scalar(ovf_f[:, 1:2], ovf_f[:, 1:2], float(LIST_BLOCKS * E - 1), 0.0, ALU.min, ALU.max))
            v.tensor_copy(ovf_f[:, 2:3], ovf_m[:, 0, E - 1:E])
            then(v.memset(ovf_f[:, 3:4], 0.0))
            v.tensor_copy(ovf_tab[:, :], ovf_f[:, 0:4]).then_inc(ovf_ready, 1)
            dve.wait_ge(slots_in, 16)
            v.tensor_scalar(slot_tok[:, :].unsqueeze(2), slots[:, :, :, :].rearrange("p b e w -> p (b e) w")[:, :, 0:1],
                            2, None, ALU.logical_shift_right).then_inc(tok_ready, 1)

            def low_rows(i, parity):
                for b in range(2):
                    dve.wait_ge(rows_hi, i * 2 + b + 1)
                    half = slice(4 * b, 4 * b + 4)
                    v.tensor_tensor(blockT_lo[:, parity, half, :], ps[:, B_X + b, :].rearrange("p (k t) -> p k t", k=4),
                                    blockT_hi[:, parity, half, :].bitcast(F32), ALU.subtract).then_inc(rows_lo, 1)

            def low_piece(i, j, q):
                dve.wait_ge(hi_ready, (i * STEPS + j) * PIECES + q + 1)
                v.tensor_tensor(w1_lo[:, j, q, :], raw_piece(j, q), w1_hi[:, q, :].bitcast(F32), ALU.subtract).then_inc(lo_ready, 1)

            def swiglu(i, j, after):
                if after:
                    for q in range(PIECES - 1):
                        low_piece(*after, q)
                s = i * STEPS + j
                b = j % 2
                h = ps[:, B_H + b, :]
                dve.wait_ge(w1_used, (s + 1) * PIECES)
                v.tensor_scalar(glu_c[:, b, :], h[:, 0:FC], LIMIT, None, ALU.min).then_inc(glu_ready, 1)
                v.tensor_scalar(lin_c[:, b, :], h[:, FC:2 * FC], LIMIT, -LIMIT, ALU.min, ALU.max).then_inc(h_read, 1)
                if after:
                    low_piece(*after, PIECES - 1)
                dve.wait_ge(glu_ready, s + 1)
                dve.wait_ge(h_read, s + 1)
                v.scalar_tensor_tensor(out=prod[:, b, :], in0=lin_c[:, b, :], scalar=1.0, in1=glu_c[:, b, :],
                                       op0=ALU.add, op1=ALU.mult).then_inc(prod_ready, 1)
                dve.wait_ge(prod_ready, s + 1)
                dve.wait_ge(sig_ready, s + 1)
                if not isinstance(s, int) or s >= 2:
                    dve.wait_ge(act_turned, s - 1)
                v.tensor_tensor(act_v[:, b, :], prod[:, b, :], sig[:, b, :], ALU.mult).then_inc(actv_ready, 1)

            def elementwise(i, parity):
                last = isinstance(i, int) and i == E - 1
                for j in range(STEPS):
                    swiglu(i, j, (i, j + 1) if j < STEPS - 1 else None if last else (i + 1, 0))
                    if j == 2 and not last:
                        if not (isinstance(i, int) and i == 0):
                            dve.wait_ge(w1_used, i * STEPS * PIECES)
                        low_rows(i + 1, 1 - parity)

            dve.wait_ge(ovf_in, 16)
            for q in range(PIECES):
                low_piece(0, 0, q)
            low_rows(0, 0)
            expert_blocks(dve, elementwise)

            def overflow(o, i):
                low_rows(i, 0)
                for q in range(PIECES):
                    low_piece(i, 0, q)
                for j in range(STEPS):
                    swiglu(i, j, (i, j + 1) if j < STEPS - 1 else None)

            overflow_blocks(dve, overflow)

            dve.wait_ge(gfinal_in, 16)
            for t in range(TB):
                dve.wait_ge(yrow_in[t], 16)
                y = y_rows[:, t, :, :]
                v.tensor_tensor(y[:, 0, :], y[:, 0, :], y[:, 1, :], ALU.add).then_inc(sum_ready, 1)
                v.tensor_tensor(y[:, 2, :], y[:, 2, :], y[:, 3, :], ALU.add).then_inc(sum_ready, 1)
                dve.wait_ge(sum_ready, 4 * t + 2)
                v.tensor_tensor(y[:, 0, :], y[:, 0, :], y[:, 2, :], ALU.add).then_inc(sum_ready, 1)
                dve.wait_ge(sum_ready, 4 * t + 3)
                v.tensor_tensor(X[:, t, :], X[:, t, :], y[:, 0, :], ALU.add).then_inc(sum_ready, 1)
                dve.wait_ge(fstd_ready, t + 1)
                v.reciprocal(stat[:, F_R + t:F_R + t + 1], stat[:, F_STD + t:F_STD + t + 1]).then_inc(dve_final, 1)
                dve.wait_ge(dve_final, t + 1)
                v.scalar_tensor_tensor(out=y[:, 0, :], in0=X[:, t, :], scalar=stat[:, F_R + t:F_R + t + 1], in1=gain_a[:, :],
                                       op0=ALU.mult, op1=ALU.mult).then_inc(fin_ready, 1)

        @block.scalar
        def _(act):
            a = nc.scalar
            chain = [0]

            def then(ins):
                chain[0] += 1
                ins.then_inc(act_step, 1)
                act.wait_ge(act_step, chain[0])

            def row_std(src, junk, n, total, col, done):
                then(a.activation(junk, src, ACT.Square, accum_out=stat[:, total:total + 1]))
                a.activation(stat[:, col:col + 1], stat[:, total:total + 1], ACT.Sqrt, scale=1.0 / n, bias=eps_col[:, :]).then_inc(done, 1)

            def xnT_half(t, bank, done):
                a.activation(xnT[:, 0:4, t * P:(t + 1) * P], ps[:, bank, :].rearrange("p (k t) -> p k t", k=4),
                             ACT.Copy).then_inc(done, 1)

            act.wait_ge(consts_ready, 1)
            waste = scores[:, 0:4, :].rearrange("p h s -> p (h s)")
            for t in range(TB):
                act.wait_ge(x_in[t], 16)
                row_std(X[:, t, :], waste, D, X_SUM + t, X_STD + t, std_ready)
                if t >= 1:
                    act.wait_ge(xn_turned, t)
                    xnT_half(t - 1, 2 * ((t - 1) % 2), xnT_a)
            act.wait_ge(xn_turned, TB)
            xnT_half(TB - 1, 2 * ((TB - 1) % 2), xnT_a)

            act.wait_ge(proj_done, 2)
            a.activation(qT[:, 0, :], ps[:, 5, :], ACT.Copy).then_inc(proj_act, 1)
            act.wait_ge(proj_done, 4)
            a.activation(qT[:, 2, :], ps[:, 7, :], ACT.Copy).then_inc(proj_act, 1)
            act.wait_ge(proj_done, 6)
            a.activation(v_sb[:, :, :], ps[:, 5, :].rearrange("p (t d) -> p t d", t=TB), ACT.Copy).then_inc(proj_act, 1)

            for n in range(TB):
                k0 = 0 if n else 1
                act.wait_ge(negmax_ready, n + 1)
                for h in range(HEADS):
                    a.activation(scores[:, h, k0 * P:], scores[:, h, k0 * P:], ACT.Exp, bias=smax[:, 2, h:h + 1],
                                 accum_out=smax[:, 4, h:h + 1])
                a.activation(esink[:, :], smax[:, 3, :], ACT.Exp).then_inc(exp_done, 1)
                act.wait_ge(convproj_done, n + 1)
                if n >= 1:
                    act.wait_ge(conv_read, n)
                a.activation(c_gate, ps[:, 1, :], ACT.Copy).then_inc(c_ready, 1)
                for c in (0, 2):
                    act.wait_ge(probs_turned, GRP * n + c + 1)
                    if c == 0 and n >= 1:
                        act.wait_ge(pv_done, n)
                    a.activation(probsT[:, 2 * c:2 * c + 2, k0:2, :],
                                 ps[:, 4, :].rearrange("p (h k t) -> p h k t", h=2, k=2)[:, :, k0:2, :], ACT.Copy).then_inc(pT_act, 1)
                act.wait_ge(convy_ready, n + 1)
                a.activation(conv_sq[:, n, :], conv_y[:, :], ACT.Square).then_inc(sq_ready, 1)
                act.wait_ge(o_ready, n + 1)
                row_std(attn_o[:, :], c_gate, AW, O_SUM + n, O_STD + n, ostd_ready)
                act.wait_ge(o_turned, n + 1)
                a.activation(attnT[:, :, n * P:(n + 1) * P], ps[:, 7, :].rearrange("p (c t) -> p c t", c=AW // P),
                             ACT.Copy).then_inc(attnT_ready, 1)

            act.wait_ge(csum_done, 1)
            a.activation(stat[:, C_STD:C_STD + TB], ps[:, 6, 0:TB], ACT.Sqrt, scale=1.0 / CW, bias=eps_col[:, :]).then_inc(cstd_ready, 1)
            for t in range(0, TB, 2):
                for u in (t, t + 1):
                    act.wait_ge(x2_ready, u + 1)
                    row_std(X[:, u, :], waste, D, H_SUM + u, H_STD + u, std2_ready)
                    act.wait_ge(h2_ready, u + 1)
                    act.dma_start(h2_dram[u * P:(u + 1) * P, :], normed[:, u % 2, :]).then_inc(h2_stored, 16)
                for u in (t, t + 1):
                    act.wait_ge(h2_turned, u + 1)
                    xnT_half(u, 4 * (u % 2), h2T_a)
                for u in (t, t + 1):
                    act.wait_ge(negtop_ready, u + 1)
                    b = u % 2
                    a.activation(top_x[:, b, :], top8[:, b, 0:TOPK], ACT.Exp, bias=rt_small[:, b, 0:1],
                                 accum_out=rt_small[:, b, 1:2]).then_inc(gexp_ready, 1)

            def high_rows(i, parity):
                act.wait_ge(rows_turned, i + 1)
                for b in range(2):
                    a.activation(blockT_hi[:, parity, 4 * b:4 * b + 4, :], ps[:, B_X + b, :].rearrange("p (k t) -> p k t", k=4),
                                 ACT.Copy).then_inc(rows_hi, 1)

            def high_piece(i, j, q):
                n = (i * STEPS + j) * PIECES + q
                act.wait_ge(w1_in[j], (i + 1) * 32)
                if not isinstance(n, int) or n >= PIECES:
                    act.wait_ge(w1_used, n - PIECES + 1)
                a.activation(w1_hi[:, q, :], raw_piece(j, q), ACT.Copy).then_inc(hi_ready, 1)

            def turned_act(i, j):
                s = i * STEPS + j
                act.wait_ge(act_turned, s + 1)
                if not isinstance(s, int) or s >= 2:
                    act.wait_ge(w2_done, s - 1)
                a.activation(actT[:, j % 2, :, :], ps[:, B_T, 0:FC].rearrange("p (k t) -> p k t", k=FK),
                             ACT.Copy).then_inc(actT_ready, 1)

            def sigmoid(i, j):
                s = i * STEPS + j
                act.wait_ge(glu_ready, s + 1)
                if not isinstance(s, int) or s >= 2:
                    act.wait_ge(actv_ready, s - 1)
                a.activation(sig[:, j % 2, :], glu_c[:, j % 2, :], ACT.Sigmoid, scale=ALPHA).then_inc(sig_ready, 1)

            def result(i, parity):
                act.wait_ge(w2_done, (i + 1) * STEPS)
                act.wait_ge(slot_ready, i + 1)
                if isinstance(i, int):
                    if i >= 2:
                        act.wait_ge(y_out[parity], 16 * (i // 2))
                else:
                    act.wait_ge(y_out[parity], (i - parity) // 2 * 16)
                a.activation(gated_y[:, parity, :], ps_y, ACT.Copy,
                             scale=cur_slot[:, parity, 1:2].bitcast(F32)).then_inc(y_ready, 1)

            def step(i, j, before, after):
                if after:
                    for q in range(PIECES - 1):
                        high_piece(*after, q)
                if before:
                    turned_act(*before)
                sigmoid(i, j)
                if after:
                    high_piece(*after, PIECES - 1)

            def evacuate(i, parity):
                first = isinstance(i, int) and i == 0
                last = isinstance(i, int) and i == E - 1
                for j in range(STEPS):
                    step(i, j, (i, j - 1) if j else None if first else (i - 1, STEPS - 1),
                         (i, j + 1) if j < STEPS - 1 else None if last else (i + 1, 0))
                    if j == 1 and not first:
                        result(i - 1, 1 - parity)
                    if j == 2 and not last:
                        if not first:
                            act.wait_ge(w1_used, i * STEPS * PIECES)
                        high_rows(i + 1, 1 - parity)

            for q in range(PIECES):
                high_piece(0, 0, q)
            act.wait_ge(h2_stored, 16 * TB)
            high_rows(0, 0)
            expert_blocks(act, evacuate)
            turned_act(E - 1, 3)
            result(E - 1, 1)

            def overflow(o, i):
                high_rows(i, 0)
                for q in range(PIECES):
                    high_piece(i, 0, q)
                for j in range(STEPS):
                    step(i, j, (i, j - 1) if j else None, (i, j + 1) if j < STEPS - 1 else None)
                turned_act(i, STEPS - 1)
                act.wait_ge(w2_done, (i + 1) * STEPS)
                act.wait_ge(slot_ready, i + 1)
                act.wait_ge(y_out[0], 16 * E // 2)
                a.activation(gated_y[:, 0, :], ps_y, ACT.Copy, scale=cur_slot[:, 0, 1:2].bitcast(F32)).then_inc(y_ready, 1)

            overflow_blocks(act, overflow)

            for t in range(TB):
                act.wait_ge(sum_ready, 4 * t + 4)
                a.activation(y_rows[:, t, 1, :], X[:, t, :], ACT.Square, accum_out=stat[:, F_SUM + t:F_SUM + t + 1]).then_inc(act_final, 1)
                act.wait_ge(act_final, t + 1)
                a.activation(stat[:, F_STD + t:F_STD + t + 1], stat[:, F_SUM + t:F_SUM + t + 1], ACT.Sqrt, scale=1.0 / D, bias=eps_col[:, :]).then_inc(fstd_ready, 1)

        @block.gpsimd
        def _(pool):
            g = nc.gpsimd
            chain = [0]

            def then(ins):
                chain[0] += 1
                ins.then_inc(pool_step, 1)
                pool.wait_ge(pool_step, chain[0])

            def keep_unless_zero(view, base, pattern, mult, fill):
                return g.affine_select(out=view, in_=view, compare_op=ALU.not_equal, fill=fill, base=base,
                                       pattern=pattern, channel_multiplier=mult)

            g.memset(eps_col[:, :], EPS)
            g.memset(ones_col[:, :], 1.0)
            g.memset(ones_row[:, :], 1.0)
            g.memset(ones_bf[:, :], 1.0)
            g.memset(earlier[:, :], 1.0)
            g.memset(upto[:, :], 1.0)
            g.memset(ident_bf[:, :], 0.0)
            g.memset(expert_sel[:, :], 0.0)
            then(g.memset(ident[:, :], 0.0))
            then(keep_unless_zero(ident[:, :], 0, [[-1, P]], 1, 1.0))
            pool.sem_inc(consts_ready, 1)
            g.iota(alibi[:, 0, :], [[1, 2 * P]], base=-P, channel_multiplier=-1, allow_small_or_imprecise_dtypes=True)
            then(g.memset(list_fill, UNUSED))
            then(g.affine_select(out=alibi[:, 0, :], in_=alibi[:, 0, :], compare_op=ALU.is_ge, fill=NEG, base=P,
                                 pattern=[[-1, 2 * P]], channel_multiplier=1))
            then(g.affine_select(out=alibi[:, 0, :], in_=alibi[:, 0, :], compare_op=ALU.is_gt, fill=NEG, base=0,
                                 pattern=[[1, 2 * P]], channel_multiplier=-1))
            for h in range(HEADS - 1, -1, -1):
                then(g.tensor_scalar(alibi[:, h, :], alibi[:, 0, :], 2.0 ** (-8.0 * (place_head(h) + 1) / HEADS), None, ALU.mult))
            pool.sem_inc(alibi_ready, 1)
            g.dma_start(list_dram.rearrange("(p r) w -> p (r w)", p=P), list_fill).then_inc(list_filled, 16)
            then(keep_unless_zero(ident_bf[:, :], 0, [[-1, E]], 1, 1.0))
            then(g.affine_select(out=earlier[:, :], in_=earlier[:, :], compare_op=ALU.is_gt, fill=0.0, base=0,
                                 pattern=[[1, P]], channel_multiplier=-1))
            then(g.affine_select(out=upto[:, :], in_=upto[:, :], compare_op=ALU.is_ge, fill=0.0, base=0,
                                 pattern=[[1, E]], channel_multiplier=-1))
            for s in range(3):
                then(keep_unless_zero(expert_sel[:, :], -s * E, [[-1, E]], 1, 1.0))
            g.iota(iota_e[:, :, :], [[0, TOPK], [1, E]], base=0, channel_multiplier=0, allow_small_or_imprecise_dtypes=True)
            g.iota(iota_o[:, :], [[0, 1]], base=0, channel_multiplier=1, allow_small_or_imprecise_dtypes=True)
            then(g.iota(entry[:, :, :, 0:1], [[P * TOPK, TB], [1, TOPK], [0, 1]], base=0, channel_multiplier=TOPK))
            pool.sem_inc(consts_ready, 1)

            def split(cols, n):
                raw = bias_raw[:, 0:n]
                for s in range(3):
                    for q in range(s, 3):
                        then(g.tensor_copy(bias_split[q * E:(q + 1) * E, cols:cols + n], raw[q * E:(q + 1) * E, :]))
                    if s < 2:
                        for q in range(s + 1, 3):
                            then(g.tensor_tensor(raw[q * E:(q + 1) * E, :], raw[q * E:(q + 1) * E, :],
                                                 bias_split[q * E:(q + 1) * E, cols:cols + n], ALU.subtract))

            pool.wait_ge(bias1_in, 48)
            split(0, 2 * FF)
            pool.sem_inc(biases_ready, 1)
            pool.wait_ge(bias2_in, 48)
            split(2 * FF, D)
            pool.sem_inc(biases_ready, 1)

            pool.wait_ge(list_filled, 16)
            for t in range(TB):
                pool.wait_ge(entries_ready, t + 1)
                for k in range(TOPK):
                    g.indirect_dma_start(list_dram, bass.IndirectOffsetOnAxis(row_i[:, t, k:k + 1], 0), entry[:, t, k, :], None,
                                         bounds_check=SEQ * E - 1, oob_is_err=False).then_inc(list_written, 16)
            pool.wait_ge(list_written, 16 * TB * TOPK)
            g.dma_start(slots[:, :, :, :].rearrange("p b e w -> p b (e w)"),
                        list_dram.rearrange("(b p e) w -> p b (e w)", p=P, e=E)).then_inc(slots_in, 16)
            pool.wait_ge(ovf_ready, 2)
            g.dma_start(ovf_dram, ovf_tab[:, :]).then_inc(ovf_stored, 16)
            pool.wait_ge(ovf_stored, 16)
            g.dma_start(ovf_row[0:1, :], ovf_dram.rearrange("(a o) w -> a (o w)", a=1)).then_inc(ovf_in, 16)
            pool.wait_ge(probs_turned, GRP * TB)
            pool.wait_ge(std2_ready, TB)
            g.memset(gathered[:, :, :], 0.0).then_inc(rows_cleared, 1)
            pool.wait_ge(slots_in, 16)
            pool.wait_ge(tok_ready, 1)
            pool.wait_ge(rows_cleared, 1)

            last_token, last_row = pool.to_reg(SEQ - 1), pool.to_reg(ROWS - 1)
            slots_flat = slots[:, :, :, :].rearrange("p b e w -> p (b e) w")

            def fetch(i, parity, expert, column, done):
                g.tensor_copy(cur_tok[:, parity, :], slot_tok[:, bass.ds(column, 1)])
                g.tensor_copy(bias_sel[:, parity, :], expert_sel[:, bass.ds(expert, 1)].to_broadcast([3 * E, P])).then_inc(cur_copied, 1)
                pool.wait_ge(cur_copied, i + 1)
                pool.sem_inc(cur_ready, 1)
                g.indirect_dma_start(gathered[:, parity, :], None, h2_dram, bass.IndirectOffsetOnAxis(cur_tok[:, parity, :], 0),
                                     bounds_check=last_token, oob_is_err=False).then_inc(done, 16)

            def prepare(i, parity):
                if not isinstance(i, int) or i >= 2:
                    pool.wait_ge(rows_turned, i - 1)
                    pool.wait_ge(w1_used, (i - 1) * STEPS * PIECES)
                fetch(i, parity, i, i, rows_in[parity])

            def take_slots(parity, column):
                g.tensor_copy(cur_slot[:, parity, :].unsqueeze(1), slots_flat[:, bass.ds(column, 1), :]).then_inc(slot_ready, 1)

            def scatter(i, parity, done):
                pool.wait_ge(slot_ready, i + 1)
                pool.wait_ge(y_ready, i + 1)
                pool.sem_inc(scatter_begun, 1)
                g.indirect_dma_start(y_dram, bass.IndirectOffsetOnAxis(cur_slot[:, parity, 0:1], 0), gated_y[:, parity, :], None,
                                     bounds_check=last_row, oob_is_err=False).then_inc(done, 16)

            def move(i, parity):
                if isinstance(i, int) and i == 0:
                    prepare(0, 0)
                if not (isinstance(i, int) and i == E - 1):
                    prepare(i + 1, 1 - parity)
                if not isinstance(i, int):
                    pool.wait_ge(y_out[parity], (i - parity) // 2 * 16)
                elif i >= 2:
                    pool.wait_ge(y_out[parity], 16 * (i // 2))
                take_slots(parity, i)
                if not (isinstance(i, int) and i == 0):
                    scatter(i - 1, 1 - parity, y_out[1 - parity])

            pool.wait_ge(h2_stored, 16 * TB)
            expert_blocks(pool, move)
            scatter(E - 1, 1, y_out[1])
            for b in range(2):
                pool.wait_ge(y_out[b], 16 * E // 2)

            def overflow(o, i):
                e = pool.value_load(ovf_row[0:1, bass.ds(o * 4, 1)], min_val=0, max_val=E - 1)
                column = pool.value_load(ovf_row[0:1, bass.ds(o * 4 + 1, 1)], min_val=0, max_val=LIST_BLOCKS * E - 1)
                fetch(i, 0, e, column, rows_ovf)
                take_slots(0, column)
                scatter(i, 0, y_ovf)
                pool.wait_ge(y_ovf, (o + 1) * 16)

            overflow_blocks(pool, overflow)
            pool.sem_inc(all_scattered, 1)


_INS = ["x", "g_mix", "w_in", "conv_w", "sinks", "g_attn_out", "g_conv_out", "w_out",
        "g_ffn", "w_router", "b_router", "w1", "b1", "w2", "b2", "g_final"]


def kernel(**inputs):
    import numpy as _np
    import concourse.bacc as _bacc
    from concourse import mybir as _mybir
    from concourse.bass_utils import run_bass_kernel_spmd as _run

    nc = _bacc.Bacc("TRN2", target_bir_lowering=False, num_devices=1)
    arrays, args = {}, []
    for name in _INS:
        a = _np.ascontiguousarray(inputs[name])
        arrays[f"in_{name}"] = a
        args.append(nc.dram_tensor(f"in_{name}", a.shape, _mybir.dt.from_np(a.dtype), kind="ExternalInput").ap())
    args.append(nc.dram_tensor("out", (1, SEQ, D), F32, kind="ExternalOutput").ap())
    layer_kernel(nc, *args)
    r = _run(nc, [arrays], core_ids=[0])
    return r.results[0]["out"]
```

```python
from contextlib import ExitStack

import concourse.bass as bass
from concourse import mybir

F32 = mybir.dt.float32
F32R = mybir.dt.float32r
BF16 = mybir.dt.bfloat16
I32 = mybir.dt.int32
U32 = mybir.dt.uint32
ALU = mybir.AluOpType
ACT = mybir.ActivationFunctionType
AX_X = mybir.AxisListType.X

P = 128
D = 1024
SEQ = 512
TB = SEQ // P
KT = D // P
HEADS, KV_HEADS, HD = 8, 2, 64
GRP = HEADS // KV_HEADS
AW = HEADS * HD
CW = D - AW
CT = CW // P
CONV_K = 3
QKV = (HEADS + 2 * KV_HEADS) * HD
CONV_COLS = 3 * CW
QKV_TILES = QKV // P
E = 32
TOPK = 4
FF = 1024
STEPS = 4
FC = FF // STEPS
FK = FC // P
PIECES = 4
PK = KT // PIECES
PIECE = PK * 2 * FC
ALPHA = 1.702
LIMIT = 7.0
EPS = 1e-5
NEG = -1e30
UNUSED = 1 << 20
ROWS = SEQ * TOPK
LIST_BLOCKS = SEQ // P
MAX_OVERFLOW = ROWS // (P + 1)
OVF_ROWS = 16
W_OUT_LATE = (3, 4, 5)
W_OUT_EARLY = tuple(k for k in range(KT) if k not in W_OUT_LATE)


def head_place(h):
    return (h % 2) * (HEADS // 2) + h // 2


def place_head(at):
    return (at % (HEADS // 2)) * 2 + at // (HEADS // 2)


def layer_kernel(nc, x, g_mix, w_in, conv_w, sinks, g_attn_out, g_conv_out, w_out,
                 g_ffn, w_router, b_router, w1, b1, w2, b2, g_final, out):
    ctx = ExitStack()
    with ctx:
        def sb(name, shape, dt=F32):
            return ctx.enter_context(nc.sbuf_tensor(name, shape, dt))

        def sb_r(name, shape, offset):
            return nc.alloc_sbuf_tensor_at(name, shape, F32R, offset=offset)

        def sem(name):
            return ctx.enter_context(nc.semaphore(name))

        h2_dram = nc.dram_tensor("h2_rows", (SEQ, D), F32).ap()
        list_dram = nc.dram_tensor("slot_list", (SEQ * E, 2), I32).ap()
        y_dram = nc.dram_tensor("expert_rows", (ROWS, D), F32).ap()

        ovf_dram = nc.dram_tensor("overflow_table", (OVF_ROWS, 4), I32).ap()

        X = sb("X", [P, TB, D])
        xnT_lo = sb_r("xnT_lo", [P, TB, KT, P], nc.sbuf_base - TB * D * 4)
        gain_a = sb("gain_a", [P, D])
        gain_ffn = sb("gain_ffn", [P, D])
        ring1 = sb("ring1", [P, STEPS * KT * 2 * FC])
        w1_lo = sb_r("w1_lo", [P, STEPS, PIECES, PIECE], nc.sbuf_base - STEPS * KT * 2 * FC * 4)
        ring2 = sb("ring2", [P, STEPS * FK * D])
        ring2_r = sb_r("ring2_r", [P, STEPS * FK * D], nc.sbuf_base - STEPS * FK * D * 4)
        xnT = sb("xnT", [P, KT, SEQ])
        xnT_hi = sb_r("xnT_hi", [P, KT, SEQ], nc.sbuf_base - KT * SEQ * 4)
        normed = sb("normed", [P, 2, D])
        scores = sb("scores", [P, HEADS, 2 * P])
        probsT = sb("probsT", [P, HEADS, 2, P])
        blockT_hi = sb_r("blockT_hi", [P, 2, KT, P], nc.sbuf_base - HEADS * 2 * P * 4)
        mixer = sb("mixer", [P, PIECES * PIECE + 2 * KT * P])
        w1_hi = sb_r("w1_hi", [P, PIECES, PIECE], nc.sbuf_base - (PIECES * PIECE + 2 * KT * P) * 4)
        blockT_lo = sb_r("blockT_lo", [P, 2, KT, P], nc.sbuf_base - 2 * KT * P * 4)
        u_pad = sb("u_pad", [P, SEQ + CONV_K - 1])
        conv_y = sb("conv_y", [P, SEQ])
        attn_sq = sb("attn_sq", [P, AW])
        attn_sqs = sb("attn_sqs", [P, SEQ])
        bias_split = sb("bias_split", [3 * E, 2 * FF + D], BF16)
        expert_sel = sb("expert_sel", [3 * E, E], BF16)
        bias_sel = sb("bias_sel", [3 * E, 2, P], BF16)
        ident = sb("ident", [P, P])
        earlier = sb("earlier", [P, P], BF16)
        ones_bf = sb("ones_bf", [P, P], BF16)
        ones_col = sb("ones_col", [P, 1])
        ones_row = sb("ones_row", [1, P])
        upto = sb("upto", [E, E], BF16)
        ident_bf = sb("ident_bf", [E, E], BF16)
        iota_e = sb("iota_e", [P, TOPK, E])
        iota_o = sb("iota_o", [OVF_ROWS, 1])
        eps_col = sb("eps_col", [P, 1])
        w_rt = sb("w_rt", [P, KT, E])
        b_rt = sb("b_rt", [1, E])
        conv_wc = sb("conv_wc", [P, CONV_K, CT])
        g_conv = sb("g_conv", [P, CT])
        g_attn = sb("g_attn", [P, CT])
        sink_b = sb("sink_b", [P, HEADS])
        stat = sb("stat", [P, 80])
        r_group = sb("r_group", [P, 2, TB])
        smax = sb("smax", [P, 6, HEADS])
        esink = sb("esink", [P, HEADS])
        logit = sb("logit", [P, 2, E])
        top8 = sb("top8", [P, 2, 8])
        top8_i = sb("top8_i", [P, 2, 8], U32)
        top_e = sb("top_e", [P, 2, TOPK])
        top_x = sb("top_x", [P, 2, TOPK])
        rt_small = sb("rt_small", [P, 2, 4])
        onehot = sb("onehot", [P, 2, TOPK, E])
        chosen = sb("chosen", [P, TB, E], BF16)
        chosen_cum = sb("chosen_cum", [P, TB + 1, E], BF16)
        rankrow = sb("rankrow", [P, 2, E])
        row_f = sb("row_f", [P, 2, TOPK])
        row_i = sb("row_i", [P, TB, TOPK], I32)
        entry = sb("entry", [P, TB, TOPK, 2], I32)
        slots = sb("slots", [P, LIST_BLOCKS, E, 2], I32)
        slot_tok = sb("slot_tok", [P, LIST_BLOCKS * E], I32)
        cur_slot = sb("cur_slot", [P, 2, 2], I32)
        cur_tok = sb("cur_tok", [P, 2, 1], I32)
        ovf_f = sb("ovf_f", [OVF_ROWS, 6])
        ovf_m = sb("ovf_m", [OVF_ROWS, 3, E])
        ovf_nb = sb("ovf_nb", [E, 4])
        ovf_nb16 = sb("ovf_nb16", [E, OVF_ROWS], BF16)
        ovf_tab = sb("ovf_tab", [OVF_ROWS, 4], I32)
        ovf_row = sb("ovf_row", [1, OVF_ROWS * 4], I32)

        ps = ctx.enter_context(nc.psum_tensor("ps", [P, 8, 512], F32))

        w_conv_sb = ring1[:, 0:KT * CONV_COLS].rearrange("p (k c) -> p k c", k=KT)
        w_lo_qkv = ring2_r[:, 0:KT * QKV].rearrange("p (k c) -> p k c", k=KT)
        w_lo_conv = w1_lo[:, :, :, :].rearrange("p s q c -> p (s q c)")[:, 0:KT * CONV_COLS].rearrange("p (k c) -> p k c", k=KT)

        def weight_tile(m):
            if m < QKV_TILES:
                c0 = (AW, 0, P, 2 * P, 3 * P, AW + P)[m]
                raw, low, at = w_qkv_sb, w_lo_qkv, KT * QKV + (m % 2) * KT * P
            else:
                n, part = (m - QKV_TILES) // 3, (m - QKV_TILES) % 3
                c0 = (1, 2, 0)[part] * CW + n * P
                raw, low, at = w_conv_sb, w_lo_conv, ((n % 2) * 3 + part) * KT * P
            return raw[:, :, c0:c0 + P], low[:, :, c0:c0 + P], ring2_r[:, at:at + KT * P].rearrange("p (k c) -> p k c", k=KT)

        spare = KT * CONV_COLS
        alibi = ring1[:, spare:spare + HEADS * 2 * P].rearrange("p (h s) -> p h s", h=HEADS)
        bias_raw = ring1[0:3 * E, spare + HEADS * 2 * P:spare + HEADS * 2 * P + 2 * FF]
        w_qkv_sb = ring2[:, 0:KT * QKV].rearrange("p (k c) -> p k c", k=KT)
        w_out_sb = ring2[:, :].rearrange("p (k n) -> p k n", k=KT)
        ring1_v = ring1[:, :].rearrange("p (s k h c) -> p s k h c", s=STEPS, k=KT, h=2)
        ring2_v = ring2[:, :].rearrange("p (s k n) -> p s k n", s=STEPS, k=FK)
        list_fill = slots[:, :, :, :].rearrange("p b e w -> p (b e w)")
        conv_sq = normed[:, :, :].rearrange("p a (c t) -> p (a c) t", c=2)
        qT = mixer[:, 0:4 * SEQ].rearrange("p (a t) -> p a t", a=HEADS // 2)
        kT = mixer[:, 4 * SEQ:6 * SEQ].rearrange("p (g t) -> p g t", g=KV_HEADS)
        v_sb = mixer[:, 6 * SEQ:7 * SEQ].rearrange("p (t d) -> p t d", t=TB)
        c_gate = mixer[:, 7 * SEQ:8 * SEQ]
        convT = mixer[:, 8 * SEQ:12 * SEQ].rearrange("p (c t) -> p c t", c=CT)
        attnT = qT
        conv_sqs = u_pad[:, 0:SEQ]
        picked = attn_sq[:, 0:TOPK * E].rearrange("p (k e) -> p k e", k=TOPK)
        gathered = scores[:, :, :].rearrange("p (b c) s -> p b (c s)", b=2)
        gated_y = normed
        step_v = xnT[:, :, :].rearrange("p k t -> p (k t)")
        glu_c = step_v[:, 0:2 * FC].rearrange("p (b c) -> p b c", b=2)
        lin_c = step_v[:, 2 * FC:4 * FC].rearrange("p (b c) -> p b c", b=2)
        sig = step_v[:, 4 * FC:6 * FC].rearrange("p (b c) -> p b c", b=2)
        prod = step_v[:, 6 * FC:8 * FC].rearrange("p (b c) -> p b c", b=2)
        act_v = step_v[:, 8 * FC:10 * FC].rearrange("p (b c) -> p b c", b=2)
        actT = step_v[:, 10 * FC:12 * FC].rearrange("p (b k t) -> p b k t", b=2, k=FK)
        y_rows = ring1[:, :].rearrange("p (t k n) -> p t k n", t=TB, k=TOPK)

        X_SUM, X_STD, X_R, A_STD, C_STD, H_SUM, H_STD, H_R, F_SUM, F_STD, F_R = range(0, 11 * TB, TB)

        B_H, B_Y, B_T, B_X = 0, 2, 4, 5
        ps_y = ps[:, B_Y:B_Y + 2, :].rearrange("p b n -> p (b n)")

        x_in = [sem(f"x_in{t}") for t in range(TB)]
        gains_in, small_in = sem("gains_in"), sem("small_in")
        qkv_in, conv_in, wout_early, wout_late = sem("qkv_in"), sem("conv_in"), sem("wout_early"), sem("wout_late")
        bias1_in, bias2_in, gfinal_in = sem("bias1_in"), sem("bias2_in"), sem("gfinal_in")
        w1_in = [sem(f"w1_in{j}") for j in range(STEPS)]
        w2_in = [sem(f"w2_in{j}") for j in range(STEPS)]
        dve_step, act_step, pool_step = sem("dve_step"), sem("act_step"), sem("pool_step")
        consts_ready, alibi_ready, biases_ready = sem("consts_ready"), sem("alibi_ready"), sem("biases_ready")
        std_ready, xn_ready, xn_turned = sem("std_ready"), sem("xn_ready"), sem("xn_turned")
        xn_hi, xn_lo = sem("xn_hi"), sem("xn_lo")
        tile_hi, tile_lo = sem("tile_hi"), sem("tile_lo")
        x_again = [sem(f"x_again{t}") for t in range(TB)]
        k_ready, k_doubled = sem("k_ready"), sem("k_doubled")
        proj_done, proj_act, proj_dve = sem("proj_done"), sem("proj_act"), sem("proj_dve")
        scores_done, scores_read = sem("scores_done"), sem("scores_read")
        negmax_ready, exp_done = sem("negmax_ready"), sem("exp_done")
        part_done, c_ready, u_ready, conv_read = sem("part_done"), sem("c_ready"), sem("u_ready"), sem("conv_read")
        convy_ready, sq_ready, convT_ready = sem("convy_ready"), sem("sq_ready"), sem("convT_ready")
        probs_turned, pT_act, pT_dve = sem("probs_turned"), sem("pT_act"), sem("pT_dve")
        vT_ready, vT_turned, probs_ready = sem("vT_ready"), sem("vT_turned"), sem("probs_ready")
        pv_done, osq_ready, o_ready, osqs_ready, csqs_ready = sem("pv_done"), sem("osq_ready"), sem("o_ready"), sem("osqs_ready"), sem("csqs_ready")
        sums_done, gstd_ready = sem("sums_done"), sem("gstd_ready")
        oproj_done, x2_half, std2_ready, h2_ready = sem("oproj_done"), sem("x2_half"), sem("std2_ready"), sem("h2_ready")
        h2_turned, h2_stored = sem("h2_turned"), sem("h2_stored")
        h2T_a, h2T_b = sem("h2T_a"), sem("h2T_b")
        logits_done, negtop_ready, gexp_ready = sem("logits_done"), sem("negtop_ready"), sem("gexp_ready")
        chosen_ready, rank_done, placed, entries_ready = sem("chosen_ready"), sem("rank_done"), sem("placed"), sem("entries_ready")
        counts_done, nb_ready, prefix_done, ovf_ready, ovf_in = sem("counts_done"), sem("nb_ready"), sem("prefix_done"), sem("ovf_ready"), sem("ovf_in")
        ovf_stored = sem("ovf_stored")
        list_filled, list_written, slots_in, tok_ready = sem("list_filled"), sem("list_written"), sem("slots_in"), sem("tok_ready")
        cur_copied, cur_ready = sem("cur_copied"), sem("cur_ready")
        rows_in = [sem(f"rows_in{b}") for b in range(2)]
        rows_cleared = sem("rows_cleared")
        rows_turned, rows_hi, rows_lo = sem("rows_turned"), sem("rows_hi"), sem("rows_lo")
        hi_ready, lo_ready, w1_used, slot_ready = sem("hi_ready"), sem("lo_ready"), sem("w1_used"), sem("slot_ready")
        h_read, glu_ready, sig_ready = sem("h_read"), sem("glu_ready"), sem("sig_ready")
        prod_ready, actv_ready, act_turned, actT_ready = sem("prod_ready"), sem("actv_ready"), sem("act_turned"), sem("actT_ready")
        w2_done, y_ready = sem("w2_done"), sem("y_ready")
        scatter_begun = sem("scatter_begun")
        y_out = [sem(f"y_out{b}") for b in range(2)]
        rows_ovf, y_ovf = sem("rows_ovf"), sem("y_ovf")
        all_scattered = sem("all_scattered")
        yrow_in = [sem(f"yrow_in{t}_{pair}") for t in range(TB) for pair in range(2)]
        sum_ready, fstd_ready, fin_ready, out_written = sem("sum_ready"), sem("fstd_ready"), sem("fin_ready"), sem("out_written")
        dve_final, act_final = sem("dve_final"), sem("act_final")

        def raw_piece(j, q):
            return ring1_v[:, j, q * PK:(q + 1) * PK, :, :].rearrange("p k h c -> p (k h c)")

        block = ctx.enter_context(nc.Block())

        def expert_blocks(eng, run):
            run(0, 0)
            run(1, 1)
            with eng.Fori(2, E - 2, 2) as i:
                run(i, 0)
                run(i + 1, 1)
            run(E - 2, 0)
            run(E - 1, 1)

        def overflow_blocks(eng, run):
            eng.wait_ge(ovf_in, 16)
            n_ovf = eng.value_load(ovf_row[0:1, 2:3], min_val=0, max_val=MAX_OVERFLOW)
            with eng.If(n_ovf > 0):
                with eng.Fori(0, MAX_OVERFLOW) as o:
                    with eng.If(n_ovf > o):
                        run(o, o + E)

        @block.sync
        def _(sp):
            with nc.allow_non_contiguous_dma(reason="small parameter columns"):
                for t in range(TB):
                    sp.dma_start(X[:, t, :], x[0, t * P:(t + 1) * P, :]).then_inc(x_in[t], 16)
                    if t == 0:
                        sp.dma_start(gain_a[:, :], g_mix[0].partition_broadcast(P)).then_inc(gains_in, 16)
                w_in_v = w_in[0].rearrange("(k p) c -> p k c", p=P)
                for k in range(0, KT, 2):
                    sp.dma_start(w_qkv_sb[:, k:k + 2, :], w_in_v[:, k:k + 2, 0:QKV]).then_inc(qkv_in, 16)
                for odd in range(2):
                    sp.dma_start(sink_b[:, odd * HEADS // 2:(odd + 1) * HEADS // 2],
                                 sinks[0].rearrange("(a b) -> b a", b=2)[odd].partition_broadcast(P)).then_inc(small_in, 16)
                sp.dma_start(g_attn[:, :], g_attn_out[0].rearrange("(c p) -> p c", p=P)).then_inc(small_in, 16)
                sp.dma_start(conv_wc[:, :, :], conv_w[0].rearrange("w (c p) -> p w c", p=P)).then_inc(small_in, 16)
                sp.dma_start(g_conv[:, :], g_conv_out[0].rearrange("(c p) -> p c", p=P)).then_inc(small_in, 16)
                for k in range(KT):
                    sp.dma_start(w_conv_sb[:, k, :], w_in_v[:, k, QKV:]).then_inc(conv_in, 16)
                sp.dma_start(gain_ffn[:, :], g_ffn[0].partition_broadcast(P)).then_inc(small_in, 16)
                sp.dma_start(w_rt[:, :, :], w_router[0].rearrange("(k p) e -> p k e", p=P)).then_inc(small_in, 16)
                sp.dma_start(b_rt[:, :], b_router).then_inc(small_in, 16)
            for g in range(3):
                sp.dma_start(bias_raw[g * E:(g + 1) * E, :], b1[0]).then_inc(bias1_in, 16)
            sp.wait_ge(xn_ready, TB)
            sp.dma_start(gain_a[:, :], g_final.partition_broadcast(P)).then_inc(gfinal_in, 16)
            sp.wait_ge(k_ready, 2)
            sp.dma_start(kT[HD:P, 0, :], kT[0:HD, 0, :]).then_inc(k_doubled, 16)
            sp.dma_start(kT[0:HD, 1, :], kT[HD:P, 1, :]).then_inc(k_doubled, 16)
            sp.wait_ge(biases_ready, 1)
            for g in range(3):
                sp.dma_start(bias_raw[g * E:(g + 1) * E, 0:D], b2[0]).then_inc(bias2_in, 16)

            w_out_v = w_out[0].rearrange("(k p) n -> p k n", p=P)
            sp.wait_ge(part_done, 3 * (CT - 1))
            for k in W_OUT_EARLY:
                sp.dma_start(w_out_sb[:, k, :], w_out_v[:, k, :]).then_inc(wout_early, 16)
            for part, k in enumerate(W_OUT_LATE):
                sp.wait_ge(part_done, 3 * (CT - 1) + part + 1)
                sp.dma_start(w_out_sb[:, k, :], w_out_v[:, k, :]).then_inc(wout_late, 16)
            for t in range(TB):
                sp.dma_start(X[:, t, :], x[0, t * P:(t + 1) * P, :]).then_inc(x_again[t], 16)

            def load_w1(j, e):
                src = w1[0, e].rearrange("(k p) (h c) -> p k h c", p=P, h=2)
                for h in range(2):
                    sp.dma_start(ring1_v[:, j, :, h, :], src[:, :, h, j * FC:(j + 1) * FC]).then_inc(w1_in[j], 16)

            def load_w2(j, e):
                src = w2[0, e].rearrange("(s k p) n -> p s k n", p=P, k=FK)
                sp.dma_start(ring2_v[:, j, :, :], src[:, j, :, :]).then_inc(w2_in[j], 16)

            def load(i, _parity):
                for j in range(STEPS):
                    if isinstance(i, int) and i == 0:
                        if j == 0:
                            sp.wait_ge(part_done, 3 * CT)
                        if j == STEPS - 1:
                            sp.wait_ge(scores_read, TB)
                            sp.wait_ge(biases_ready, 2)
                        load_w1(j, i)
                        continue
                    sp.wait_ge(w1_used, ((i - 1) * STEPS + j + 1) * PIECES)
                    load_w1(j, i)
                    sp.wait_ge(w2_done, (i - 1) * STEPS + j + 1)
                    load_w2(j, i)
                if isinstance(i, int) and i == 0:
                    sp.wait_ge(oproj_done, 2 * TB)
                    for j in range(STEPS):
                        load_w2(j, i)

            expert_blocks(sp, load)

            def load_overflow(o, i):
                e = sp.value_load(ovf_row[0:1, bass.ds(o * 4, 1)], min_val=0, max_val=E - 1)
                for j in range(STEPS):
                    sp.wait_ge(w1_used, ((i - 1) * STEPS + j + 1) * PIECES)
                    load_w1(j, e)
                    sp.wait_ge(w2_done, (i - 1) * STEPS + j + 1)
                    load_w2(j, e)

            overflow_blocks(sp, load_overflow)

            sp.wait_ge(all_scattered, 1)
            y_dram_v = y_dram.rearrange("(t p k) n -> t p k n", p=P, k=TOPK)
            for t in range(TB):
                for pair in range(2):
                    sp.dma_start(y_rows[:, t, 2 * pair:2 * pair + 2, :], y_dram_v[t, :, 2 * pair:2 * pair + 2, :]).then_inc(yrow_in[2 * t + pair], 16)
            for t in range(TB):
                sp.wait_ge(fin_ready, t + 1)
                sp.dma_start(out[0, t * P:(t + 1) * P, :], y_rows[:, t, 0, :]).then_inc(out_written, 16)
            sp.wait_ge(out_written, 16 * TB)

        @block.tensor
        def _(pe):
            mm = pe.matmul

            def turn_rows(src, bank):
                for k in range(KT):
                    ins = pe.transpose(ps[:, bank + k // 4, (k % 4) * P:(k % 4 + 1) * P],
                                       src[:, k * P:(k + 1) * P], ident[:, :])
                return ins

            pe.wait_ge(consts_ready, 1)
            for t in range(TB):
                pe.wait_ge(xn_ready, t + 1)
                if t >= 2:
                    pe.wait_ge(xn_lo, 2 * (t - 1))
                turn_rows(normed[:, t % 2, :], 2 * (t % 2)).then_inc(xn_turned, 1)

            def project(m, bank, done):
                pe.wait_ge(tile_lo, m + 1)
                _, low, high = weight_tile(m)
                for k in range(KT):
                    mm(ps[:, bank, :], high[:, k, :], xnT_hi[:, k, :], start=(k == 0), stop=False)
                    mm(ps[:, bank, :], high[:, k, :], xnT_lo[:, :, k, :], start=False, stop=False)
                    ins = mm(ps[:, bank, :], low[:, k, :], xnT_hi[:, k, :], start=False, stop=(k == KT - 1))
                if done:
                    ins.then_inc(done, 1)

            pe.wait_ge(xn_lo, 2 * TB)
            for m in range(QKV_TILES):
                if m == 4:
                    pe.wait_ge(proj_dve, 1)
                if m == 5:
                    pe.wait_ge(proj_act, 1)
                project(m, 4 + m % 4, proj_done)

            def scores_of(n, odd):
                k0 = 0 if n else 1
                if n == 0 and not odd:
                    pe.wait_ge(proj_dve, 3)
                    pe.wait_ge(proj_act, 2)
                    pe.wait_ge(k_doubled, 32)
                if n and not odd:
                    pe.wait_ge(u_ready, n)
                if n and odd:
                    pe.wait_ge(conv_read, n)
                for h in range(odd, HEADS, 2):
                    g, half, at = h // GRP, (h % 2) * HD, head_place(h)
                    ins = mm(ps[:, at // 2, (at % 2) * 2 * P + k0 * P:(at % 2 + 1) * 2 * P],
                             qT[half:half + HD, h // 2, n * P:(n + 1) * P],
                             kT[half:half + HD, g, (n - 1 + k0) * P:(n + 1) * P], start=True, stop=True)
                if odd:
                    ins.then_inc(scores_done, 1)

            def turn_probs(n, c):
                q = GRP * n + c
                if q >= 2:
                    pe.wait_ge(pT_dve if c % 2 else pT_act, q // 2)
                for h in (2 * c, 2 * c + 1):
                    for kb in range(0 if n else 1, 2):
                        ins = pe.transpose(ps[:, 4 + c % 2, ((h % 2) * 2 + kb) * P:((h % 2) * 2 + kb + 1) * P],
                                           scores[:, h, kb * P:(kb + 1) * P], ident[:, :])
                ins.then_inc(probs_turned, 1)

            def attend(n):
                k0 = 0 if n else 1
                pe.wait_ge(pT_act, 2 * (n + 1))
                pe.wait_ge(pT_dve, 2 * (n + 1))
                if n == 0:
                    pe.wait_ge(proj_act, 4)
                if n >= 2:
                    pe.wait_ge(o_ready, n - 1)
                for odd in range(2):
                    for g in range(KV_HEADS):
                        at = odd * (HEADS // 2) + 2 * g
                        for kb in range(k0, 2):
                            ins = mm(ps[odd * HD:(odd + 1) * HD, 6 + n % 2, 2 * g * P:2 * (g + 1) * P],
                                     v_sb[:, n - 1 + kb, g * HD:(g + 1) * HD], probsT[:, at:at + 2, kb, :],
                                     start=(kb == k0), stop=(kb == 1))
                ins.then_inc(pv_done, 1)

            scores_of(0, 0)
            scores_of(0, 1)
            pe.wait_ge(vT_ready, 1)
            for t in range(TB):
                ins = pe.transpose(ps[:, 6, t * P:(t + 1) * P], c_gate[:, t * P:(t + 1) * P], ident[:, :])
            ins.then_inc(vT_turned, 1)
            for n in range(TB):
                pe.wait_ge(scores_read, n + 1)
                project(QKV_TILES + 3 * n, 0, part_done)
                if n:
                    attend(n - 1)
                project(QKV_TILES + 3 * n + 1, 1, part_done)
                project(QKV_TILES + 3 * n + 2, 2, part_done)
                pe.wait_ge(probs_ready, n + 1)
                turn_probs(n, 0)
                turn_probs(n, 1)
                if n < TB - 1:
                    scores_of(n + 1, 0)
                turn_probs(n, 2)
                turn_probs(n, 3)
                if n < TB - 1:
                    scores_of(n + 1, 1)

            def out_proj(t, n):
                if t == 0 and n == 0:
                    pe.wait_ge(wout_early, 16 * len(W_OUT_EARLY))
                    pe.wait_ge(convT_ready, CT)
                    pe.wait_ge(u_ready, CT)
                if t == 0 and n == 1:
                    pe.wait_ge(conv_read, CT)
                if n == 0:
                    pe.wait_ge(o_ready, t + 1)
                if t:
                    pe.wait_ge(x2_half, 2 * (t - 1) + n + 1)
                for k in W_OUT_EARLY + W_OUT_LATE:
                    if t == 0 and n == 0 and k == W_OUT_LATE[0]:
                        pe.wait_ge(wout_late, 16 * len(W_OUT_LATE))
                    half, c = k // CT, k % CT
                    ins = mm(ps[:, 2 * n + half, :], (attnT, convT)[half][:, c, t * P:(t + 1) * P],
                             w_out_sb[:, k, n * 512:(n + 1) * 512],
                             start=(k in (0, W_OUT_LATE[-1] + 1)), stop=(k in (CT - 1, W_OUT_LATE[-1])))
                ins.then_inc(oproj_done, 1)

            def group_sums():
                pe.wait_ge(osqs_ready, TB)
                pe.wait_ge(csqs_ready, 1)
                for half, src in enumerate((attn_sqs, conv_sqs)):
                    for t in range(TB):
                        ins = mm(ps[:, 4, half * TB + t:half * TB + t + 1], src[:, t * P:(t + 1) * P], ones_col[:, :],
                                 start=True, stop=True)
                ins.then_inc(sums_done, 1)

            def turn_h2(t):
                pe.wait_ge(h2_ready, t + 1)
                if t == 0:
                    pe.wait_ge(gstd_ready, 1)
                else:
                    pe.wait_ge(h2T_a, t)
                    pe.wait_ge(h2T_b, t)
                turn_rows(normed[:, t % 2, :], 4).then_inc(h2_turned, 1)

            def router(t):
                pe.wait_ge(h2T_a, t + 1)
                pe.wait_ge(h2T_b, t + 1)
                if t == 0:
                    pe.wait_ge(small_in, 16 * 8)
                else:
                    pe.wait_ge(chosen_ready, t)
                mm(ps[:, 6, 0:E], ones_row[:, :], b_rt[:, :], start=True, stop=False)
                for k in range(KT):
                    ins = mm(ps[:, 6, 0:E], xnT[:, k, t * P:(t + 1) * P], w_rt[:, k, :],
                             start=False, stop=(k == KT - 1))
                ins.then_inc(logits_done, 1)

            def rank(t):
                pe.wait_ge(chosen_ready, t + 1)
                if t == 0:
                    pe.wait_ge(consts_ready, 2)
                else:
                    pe.wait_ge(placed, t)
                ins = mm(ps[:, 7, 0:E], earlier[:, :], chosen[:, t, :], start=True, stop=(t == 0))
                if t:
                    ins = mm(ps[:, 7, 0:E], ones_bf[:, :], chosen_cum[:, t, :], start=False, stop=True)
                ins.then_inc(rank_done, 1)

            out_proj(0, 0)
            attend(TB - 1)
            out_proj(0, 1)
            group_sums()
            for t in range(1, TB):
                out_proj(t, 0)
                turn_h2(t - 1)
                if t >= 2:
                    rank(t - 2)
                out_proj(t, 1)
                router(t - 1)
            turn_h2(TB - 1)
            rank(TB - 2)
            router(TB - 1)
            rank(TB - 1)
            mm(ps[0:E, 0, 0:1], chosen_cum[:, TB, :], ones_bf[:, 0:1], start=True, stop=True).then_inc(counts_done, 1)
            pe.wait_ge(nb_ready, 1)
            mm(ps[0:OVF_ROWS, 1, 0:E], ovf_nb16[:, :], upto[:, :], start=True, stop=True)
            mm(ps[0:OVF_ROWS, 1, E:2 * E], ovf_nb16[:, :], ident_bf[:, :], start=True, stop=True).then_inc(prefix_done, 1)

            def turn_block(i, parity):
                pe.wait_ge(rows_in[parity], 16 * (i // 2 + 1) if isinstance(i, int) else half_up(i, parity) * 16)
                if not (isinstance(i, int) and i == 0):
                    pe.wait_ge(rows_lo, i * 2)
                turn_rows(gathered[:, parity, :], B_X).then_inc(rows_turned, 1)

            def half_up(i, parity):
                return (i + 2 - parity) // 2

            def w1_step(i, j, parity):
                s = i * STEPS + j
                if j == 0:
                    pe.wait_ge(rows_lo, (i + 1) * 2)
                    pe.wait_ge(cur_ready, i + 1)
                if not isinstance(s, int) or s >= 2:
                    pe.wait_ge(h_read, s - 1)
                h = ps[:, B_H + j % 2, :]
                mm(h, bias_sel[:, parity, :], bias_split[:, 0:2 * FF].rearrange("p (h c) -> p h c", h=2)[:, :, j * FC:(j + 1) * FC],
                   start=True, stop=False)
                for q in range(PIECES):
                    pe.wait_ge(lo_ready, s * PIECES + q + 1)
                    for k in range(q * PK, (q + 1) * PK):
                        cols = slice((k % PK) * 2 * FC, (k % PK + 1) * 2 * FC)
                        x_hi, x_lo = blockT_hi[:, parity, k, :], blockT_lo[:, parity, k, :]
                        mm(h, x_hi, w1_hi[:, q, cols], start=False, stop=False)
                        mm(h, x_hi, w1_lo[:, j, q, cols], start=False, stop=False)
                        ins = mm(h, x_lo, w1_hi[:, q, cols], start=False, stop=(k == KT - 1))
                    ins.then_inc(w1_used, 1)

            def turn_act(i, j):
                s = i * STEPS + j
                pe.wait_ge(actv_ready, s + 1)
                if not isinstance(s, int) or s >= 1:
                    pe.wait_ge(actT_ready, s)
                for k in range(FK):
                    ins = pe.transpose(ps[:, B_T, k * P:(k + 1) * P], act_v[:, j % 2, k * P:(k + 1) * P], ident[:, :])
                ins.then_inc(act_turned, 1)

            def w2_step(i, j, parity):
                s = i * STEPS + j
                pe.wait_ge(actT_ready, s + 1)
                pe.wait_ge(w2_in[j], (i + 1) * 16)
                if j == 0:
                    if not (isinstance(i, int) and i == 0):
                        pe.wait_ge(y_ready, i)
                    for n in range(2):
                        mm(ps[:, B_Y + n, :], bias_sel[:, parity, :], bias_split[:, 2 * FF + n * 512:2 * FF + (n + 1) * 512],
                           start=True, stop=False)
                for k in range(FK):
                    for n in range(2):
                        ins = mm(ps[:, B_Y + n, :], actT[:, j % 2, k, :], ring2_v[:, j, k, n * 512:(n + 1) * 512],
                                 start=False, stop=(j == STEPS - 1 and k == FK - 1))
                ins.then_inc(w2_done, 1)

            def compute(i, parity):
                first = isinstance(i, int) and i == 0
                last = isinstance(i, int) and i == E - 1
                w1_step(i, 0, parity)
                if not first:
                    turn_act(i - 1, 3)
                    w2_step(i - 1, 2, 1 - parity)
                w1_step(i, 1, parity)
                turn_act(i, 0)
                if not first:
                    w2_step(i - 1, 3, 1 - parity)
                w1_step(i, 2, parity)
                turn_act(i, 1)
                w2_step(i, 0, parity)
                if not last:
                    turn_block(i + 1, 1 - parity)
                w1_step(i, 3, parity)
                turn_act(i, 2)
                w2_step(i, 1, parity)

            def drain(i, parity):
                turn_act(i, 3)
                w2_step(i, 2, parity)
                w2_step(i, 3, parity)

            pe.wait_ge(biases_ready, 2)
            pe.wait_ge(ovf_ready, 1)
            turn_block(0, 0)
            expert_blocks(pe, compute)
            drain(E - 1, 1)

            def overflow(o, i):
                pe.wait_ge(rows_ovf, (o + 1) * 16)
                pe.wait_ge(rows_lo, i * 2)
                turn_rows(gathered[:, 0, :], B_X).then_inc(rows_turned, 1)
                for j in range(STEPS):
                    w1_step(i, j, 0)
                    if j >= 1:
                        turn_act(i, j - 1)
                    if j >= 2:
                        w2_step(i, j - 2, 0)
                drain(i, 0)

            overflow_blocks(pe, overflow)

        @block.vector
        def _(dve):
            v = nc.vector
            chain = [0]

            def then(ins):
                chain[0] += 1
                ins.then_inc(dve_step, 1)
                dve.wait_ge(dve_step, chain[0])

            def norm(src, dst, gain, std_col, r_col, done):
                then(v.reciprocal(stat[:, r_col:r_col + 1], stat[:, std_col:std_col + 1]))
                return v.scalar_tensor_tensor(out=dst, in0=src, scalar=stat[:, r_col:r_col + 1], in1=gain,
                                              op0=ALU.mult, op1=ALU.mult).then_inc(done, 1)

            def low_tile(m):
                dve.wait_ge(tile_hi, m + 1)
                raw, low, high = weight_tile(m)
                v.tensor_tensor(low, raw, high.bitcast(F32), ALU.subtract).then_inc(tile_lo, 1)

            def low_xn(t):
                for b in range(2):
                    dve.wait_ge(xn_hi, 2 * t + b + 1)
                    half = slice(4 * b, 4 * b + 4)
                    v.tensor_tensor(xnT_lo[:, t, half, :], ps[:, 2 * (t % 2) + b, :].rearrange("p (k t) -> p k t", k=4),
                                    xnT_hi[:, half, t * P:(t + 1) * P].bitcast(F32), ALU.subtract).then_inc(xn_lo, 1)

            v.memset(u_pad[:, 0:CONV_K - 1], 0.0)
            then(v.memset(chosen_cum[:, 0, :], 0.0))

            dve.wait_ge(gains_in, 16)
            for t in range(TB):
                dve.wait_ge(std_ready, t + 1)
                if t >= 2:
                    dve.wait_ge(xn_turned, t - 1)
                norm(X[:, t, :], normed[:, t % 2, :], gain_a[:, :], X_STD + t, X_R + t, xn_ready)
                if t >= 1:
                    low_xn(t - 1)
            low_xn(TB - 1)

            low_tile(0)
            low_tile(1)
            dve.wait_ge(proj_done, 1)
            v.tensor_copy(kT[0:HD, 0, :], ps[0:HD, 4, :]).then_inc(k_ready, 1)
            v.tensor_copy(kT[HD:P, 1, :], ps[HD:P, 4, :]).then_inc(k_ready, 1)
            dve.wait_ge(k_ready, 2)
            dve.sem_inc(proj_dve, 1)
            low_tile(2)
            low_tile(3)
            dve.wait_ge(proj_done, 3)
            v.tensor_copy(qT[:, 1, :], ps[:, 6, :]).then_inc(proj_dve, 1)
            low_tile(4)
            low_tile(5)
            dve.wait_ge(proj_done, 5)
            v.tensor_copy(qT[:, 3, :], ps[:, 4, :]).then_inc(proj_dve, 1)
            for part in range(3):
                low_tile(QKV_TILES + part)

            def attended(n):
                dve.wait_ge(osq_ready, n + 1)
                v.tensor_tensor(attnT[:, :, n * P:(n + 1) * P], ps[:, 6 + n % 2, :].rearrange("p (c t) -> p c t", c=CT),
                                g_attn[:, :].unsqueeze(2).to_broadcast([P, CT, P]), ALU.mult).then_inc(o_ready, 1)
                v.tensor_reduce(attn_sqs[:, n * P:(n + 1) * P], attn_sq[:, :].rearrange("p (c t) -> p t c", c=CT), AX_X, ALU.add).then_inc(osqs_ready, 1)

            dve.wait_ge(alibi_ready, 1)
            dve.wait_ge(small_in, 16 * 8)
            for n in range(TB):
                k0 = 0 if n else 1
                s0 = k0 * P
                dve.wait_ge(scores_done, n + 1)
                if n >= 1:
                    dve.wait_ge(probs_turned, GRP * n)
                then(v.scalar_tensor_tensor(out=scores[:, :, s0:], in0=ps[:, 0:4, :].rearrange("p b (h s) -> p (b h) s", h=2)[:, :, s0:],
                                            scalar=HD ** -0.5, in1=alibi[:, :, s0:], op0=ALU.mult, op1=ALU.add))
                dve.sem_inc(scores_read, 1)
                then(v.tensor_reduce(smax[:, 0, :], scores[:, :, s0:], AX_X, ALU.max))
                then(v.tensor_tensor(smax[:, 1, :], smax[:, 0, :], sink_b[:, :], ALU.max))
                then(v.tensor_scalar(smax[:, 2, :], smax[:, 1, :], -1.0, None, ALU.mult))
                v.tensor_tensor(smax[:, 3, :], smax[:, 2, :], sink_b[:, :], ALU.add).then_inc(negmax_ready, 1)
                if n < TB - 1:
                    for part in range(3):
                        low_tile(QKV_TILES + 3 * (n + 1) + part)
                dve.wait_ge(exp_done, n + 1)
                then(v.tensor_tensor(smax[:, 5, :], smax[:, 4, :], esink[:, :], ALU.add))
                then(v.reciprocal(smax[:, 5, :], smax[:, 5, :]))
                v.tensor_tensor(scores[:, :, s0:], scores[:, :, s0:], smax[:, 5, :].unsqueeze(2).to_broadcast([P, HEADS, 2 * P - s0]),
                                ALU.mult).then_inc(probs_ready, 1)
                dve.wait_ge(c_ready, n + 1)
                dve.wait_ge(part_done, 3 * n + 2)
                then(v.tensor_tensor(u_pad[:, CONV_K - 1:], c_gate, ps[:, 1, :], ALU.mult))
                dve.sem_inc(u_ready, 1)
                if n >= 1:
                    dve.wait_ge(sq_ready, n)
                then(v.tensor_scalar(conv_y[:, :], u_pad[:, 0:SEQ], conv_wc[:, 0, n:n + 1], None, ALU.mult))
                for w in range(1, CONV_K):
                    then(v.scalar_tensor_tensor(out=conv_y[:, :], in0=u_pad[:, w:w + SEQ], scalar=conv_wc[:, w, n:n + 1],
                                                in1=conv_y[:, :], op0=ALU.mult, op1=ALU.add))
                if n >= 1:
                    attended(n - 1)
                dve.wait_ge(part_done, 3 * n + 3)
                then(v.tensor_tensor(conv_y[:, :], conv_y[:, :], ps[:, 2, :], ALU.mult))
                dve.sem_inc(conv_read, 1)
                dve.sem_inc(convy_ready, 1)
                for c in (1, 3):
                    dve.wait_ge(probs_turned, GRP * n + c + 1)
                    if c == 1 and n >= 1:
                        dve.wait_ge(pv_done, n)
                    v.tensor_copy(probsT[:, 2 * c:2 * c + 2, k0:2, :],
                                  ps[:, 5, :].rearrange("p (h k t) -> p h k t", h=2, k=2)[:, :, k0:2, :]).then_inc(pT_dve, 1)
                    if c == 1:
                        v.tensor_scalar(convT[:, n, :], conv_y[:, :], g_conv[:, n:n + 1], None, ALU.mult).then_inc(convT_ready, 1)
            dve.wait_ge(sq_ready, CT)
            v.tensor_reduce(conv_sqs[:, :], conv_sq.rearrange("p c t -> p t c"), AX_X, ALU.add).then_inc(csqs_ready, 1)
            attended(TB - 1)

            dve.wait_ge(gstd_ready, 1)
            then(v.reciprocal(r_group[:, :, :].rearrange("p g t -> p (g t)"), stat[:, A_STD:A_STD + 2 * TB]))

            def residual(t, n):
                dve.wait_ge(oproj_done, 2 * t + n + 1)
                if n == 0:
                    dve.wait_ge(x_again[t], 16)
                xt = X[:, t, n * 512:(n + 1) * 512]
                then(v.scalar_tensor_tensor(out=xt, in0=ps[:, 2 * n, :], scalar=r_group[:, 0, t:t + 1], in1=xt, op0=ALU.mult, op1=ALU.add))
                v.scalar_tensor_tensor(out=xt, in0=ps[:, 2 * n + 1, :], scalar=r_group[:, 1, t:t + 1],
                                       in1=xt, op0=ALU.mult, op1=ALU.add).then_inc(x2_half, 1)

            def second_norm(t):
                dve.wait_ge(std2_ready, t + 1)
                if t >= 2:
                    dve.wait_ge(h2_turned, t - 1)
                    dve.wait_ge(h2_stored, 16 * t)
                norm(X[:, t, :], normed[:, t % 2, :], gain_ffn[:, :], H_STD + t, H_R + t, h2_ready)

            def turned_h2(t):
                dve.wait_ge(h2_turned, t + 1)
                v.tensor_copy(xnT[:, 4:8, t * P:(t + 1) * P],
                              ps[:, 5, :].rearrange("p (k t) -> p k t", k=4)).then_inc(h2T_b, 1)

            def select(t):
                b = t % 2
                dve.wait_ge(logits_done, t + 1)
                then(v.tensor_copy(logit[:, b, :], ps[:, 6, 0:E]))
                then(v.max(top8[:, b, :], logit[:, b, :]))
                v.tensor_scalar(rt_small[:, b, 0:1], top8[:, b, 0:1], -1.0, None, ALU.mult).then_inc(negtop_ready, 1)
                then(v.max_index(top8_i[:, b, :], top8[:, b, :], logit[:, b, :]))
                then(v.tensor_copy(top_e[:, b, :], top8_i[:, b, 0:TOPK]))
                then(v.tensor_tensor(onehot[:, b, :, :], iota_e[:, :, :], top_e[:, b, :].unsqueeze(2).to_broadcast([P, TOPK, E]), ALU.is_equal))
                with nc.allow_low_precision(reason="sums of zeros and ones, at most 4"):
                    then(v.tensor_reduce(chosen[:, t, :], onehot[:, b, :, :].rearrange("p k e -> p e k"), AX_X, ALU.add))
                    v.tensor_tensor(chosen_cum[:, t + 1, :], chosen_cum[:, t, :], chosen[:, t, :], ALU.add).then_inc(chosen_ready, 1)

            def gates(t):
                b = t % 2
                dve.wait_ge(gexp_ready, t + 1)
                then(v.reciprocal(rt_small[:, b, 2:3], rt_small[:, b, 1:2]))
                then(v.tensor_scalar(entry[:, t, :, 1:2].bitcast(F32), top_x[:, b, :].unsqueeze(2), rt_small[:, b, 2:3], None, ALU.mult))
                dve.sem_inc(entries_ready, 1)

            def place(t):
                b = t % 2
                dve.wait_ge(rank_done, t + 1)
                then(v.scalar_tensor_tensor(out=rankrow[:, b, :], in0=ps[:, 7, 0:E], scalar=float(E), in1=iota_e[:, 0, :],
                                            op0=ALU.mult, op1=ALU.add))
                then(v.tensor_tensor(picked[:, :, :], onehot[:, b, :, :], rankrow[:, b, :].unsqueeze(1).to_broadcast([P, TOPK, E]), ALU.mult))
                then(v.tensor_reduce(row_f[:, b, :], picked[:, :, :], AX_X, ALU.add))
                v.tensor_copy(row_i[:, t, :], row_f[:, b, :]).then_inc(placed, 1)
                dve.wait_ge(placed, t + 1)

            residual(0, 0)
            residual(0, 1)
            second_norm(0)
            for t in range(1, TB):
                residual(t, 0)
                turned_h2(t - 1)
                if t >= 2:
                    place(t - 2)
                    gates(t - 2)
                residual(t, 1)
                second_norm(t)
                select(t - 1)
            turned_h2(TB - 1)
            place(TB - 2)
            gates(TB - 2)
            select(TB - 1)
            place(TB - 1)
            gates(TB - 1)

            dve.wait_ge(counts_done, 1)
            then(v.tensor_copy(ovf_nb[:, 0:1], ps[0:E, 0, 0:1]))
            then(v.tensor_scalar(ovf_nb[:, 1:2], ovf_nb[:, 0:1], float(P), None, ALU.is_gt))
            for n in range(2, LIST_BLOCKS):
                then(v.tensor_scalar(ovf_nb[:, 2:3], ovf_nb[:, 0:1], float(n * P), None, ALU.is_gt))
                then(v.tensor_tensor(ovf_nb[:, 1:2], ovf_nb[:, 1:2], ovf_nb[:, 2:3], ALU.add))
            v.tensor_copy(ovf_nb16[:, :], ovf_nb[:, 1:2].to_broadcast([E, OVF_ROWS])).then_inc(nb_ready, 1)
            dve.wait_ge(prefix_done, 1)
            then(v.tensor_copy(ovf_m[:, 0:2, :].rearrange("p a e -> p (a e)"), ps[0:OVF_ROWS, 1, 0:2 * E]))
            dve.sem_inc(ovf_ready, 1)
            then(v.tensor_scalar(ovf_m[:, 2, :], ovf_m[:, 0, :], iota_o[:, 0:1], None, ALU.is_le))
            then(v.tensor_reduce(ovf_f[:, 0:1], ovf_m[:, 2, :], AX_X, ALU.add))
            then(v.tensor_scalar(ovf_f[:, 0:1], ovf_f[:, 0:1], float(E - 1), None, ALU.min))
            then(v.tensor_tensor(ovf_m[:, 1, :], ovf_m[:, 1, :], ovf_m[:, 2, :], ALU.mult))
            then(v.tensor_reduce(ovf_f[:, 1:2], ovf_m[:, 1, :], AX_X, ALU.add))
            then(v.tensor_tensor(ovf_f[:, 2:3], iota_o[:, :], ovf_f[:, 1:2], ALU.subtract))
            then(v.tensor_scalar(ovf_f[:, 2:3], ovf_f[:, 2:3], 1.0, float(E), ALU.add, ALU.mult))
            then(v.tensor_tensor(ovf_f[:, 1:2], ovf_f[:, 2:3], ovf_f[:, 0:1], ALU.add))
            then(v.tensor_scalar(ovf_f[:, 1:2], ovf_f[:, 1:2], float(LIST_BLOCKS * E - 1), 0.0, ALU.min, ALU.max))
            v.tensor_copy(ovf_f[:, 2:3], ovf_m[:, 0, E - 1:E])
            then(v.memset(ovf_f[:, 3:4], 0.0))
            v.tensor_copy(ovf_tab[:, :], ovf_f[:, 0:4]).then_inc(ovf_ready, 1)
            def low_rows(i, parity):
                for b in range(2):
                    dve.wait_ge(rows_hi, i * 2 + b + 1)
                    half = slice(4 * b, 4 * b + 4)
                    v.tensor_tensor(blockT_lo[:, parity, half, :], ps[:, B_X + b, :].rearrange("p (k t) -> p k t", k=4),
                                    blockT_hi[:, parity, half, :].bitcast(F32), ALU.subtract).then_inc(rows_lo, 1)

            def low_piece(i, j, q):
                dve.wait_ge(hi_ready, (i * STEPS + j) * PIECES + q + 1)
                v.tensor_tensor(w1_lo[:, j, q, :], raw_piece(j, q), w1_hi[:, q, :].bitcast(F32), ALU.subtract).then_inc(lo_ready, 1)

            def swiglu(i, j, after):
                if after:
                    for q in range(PIECES - 1):
                        low_piece(*after, q)
                s = i * STEPS + j
                b = j % 2
                h = ps[:, B_H + b, :]
                dve.wait_ge(w1_used, (s + 1) * PIECES)
                v.tensor_scalar(glu_c[:, b, :], h[:, 0:FC], LIMIT, None, ALU.min).then_inc(glu_ready, 1)
                v.tensor_scalar(lin_c[:, b, :], h[:, FC:2 * FC], LIMIT, -LIMIT, ALU.min, ALU.max).then_inc(h_read, 1)
                if after:
                    low_piece(*after, PIECES - 1)
                dve.wait_ge(glu_ready, s + 1)
                dve.wait_ge(h_read, s + 1)
                v.scalar_tensor_tensor(out=prod[:, b, :], in0=lin_c[:, b, :], scalar=1.0, in1=glu_c[:, b, :],
                                       op0=ALU.add, op1=ALU.mult).then_inc(prod_ready, 1)
                dve.wait_ge(prod_ready, s + 1)
                dve.wait_ge(sig_ready, s + 1)
                if not isinstance(s, int) or s >= 2:
                    dve.wait_ge(act_turned, s - 1)
                v.tensor_tensor(act_v[:, b, :], prod[:, b, :], sig[:, b, :], ALU.mult).then_inc(actv_ready, 1)

            def elementwise(i, parity):
                last = isinstance(i, int) and i == E - 1
                for j in range(STEPS):
                    swiglu(i, j, (i, j + 1) if j < STEPS - 1 else None if last else (i + 1, 0))
                    if j == 2 and not last:
                        if not (isinstance(i, int) and i == 0):
                            dve.wait_ge(w1_used, i * STEPS * PIECES)
                        low_rows(i + 1, 1 - parity)

            for q in range(PIECES - 1):
                low_piece(0, 0, q)
            dve.wait_ge(slots_in, 16)
            v.tensor_scalar(slot_tok[:, :].unsqueeze(2), slots[:, :, :, :].rearrange("p b e w -> p (b e) w")[:, :, 0:1],
                            2, None, ALU.logical_shift_right).then_inc(tok_ready, 1)
            low_piece(0, 0, PIECES - 1)
            low_rows(0, 0)
            expert_blocks(dve, elementwise)

            def overflow(o, i):
                low_rows(i, 0)
                for q in range(PIECES):
                    low_piece(i, 0, q)
                for j in range(STEPS):
                    swiglu(i, j, (i, j + 1) if j < STEPS - 1 else None)

            overflow_blocks(dve, overflow)

            dve.wait_ge(gfinal_in, 16)
            def add_pair(t, pair):
                n = 4 * t + 2 * pair
                y = y_rows[:, t, :, :]
                dve.wait_ge(yrow_in[2 * t + pair], 16)
                v.tensor_tensor(y[:, 2 * pair, :], y[:, 2 * pair, :], y[:, 2 * pair + 1, :], ALU.add).then_inc(sum_ready, 1)
                dve.wait_ge(sum_ready, n + 1)
                v.tensor_tensor(X[:, t, :], X[:, t, :], y[:, 2 * pair, :], ALU.add).then_inc(sum_ready, 1)
                dve.wait_ge(sum_ready, n + 2)

            def last_norm(t):
                dve.wait_ge(fstd_ready, t + 1)
                v.reciprocal(stat[:, F_R + t:F_R + t + 1], stat[:, F_STD + t:F_STD + t + 1]).then_inc(dve_final, 1)
                dve.wait_ge(dve_final, t + 1)
                v.scalar_tensor_tensor(out=y_rows[:, t, 0, :], in0=X[:, t, :], scalar=stat[:, F_R + t:F_R + t + 1], in1=gain_a[:, :],
                                       op0=ALU.mult, op1=ALU.mult).then_inc(fin_ready, 1)

            for t in range(TB):
                add_pair(t, 0)
                if t >= 1:
                    last_norm(t - 1)
                add_pair(t, 1)
            last_norm(TB - 1)

        @block.scalar
        def _(act):
            a = nc.scalar
            chain = [0]

            def then(ins):
                chain[0] += 1
                ins.then_inc(act_step, 1)
                act.wait_ge(act_step, chain[0])

            def row_std(src, junk, n, total, col, done):
                then(a.activation(junk, src, ACT.Square, accum_out=stat[:, total:total + 1]))
                a.activation(stat[:, col:col + 1], stat[:, total:total + 1], ACT.Sqrt, scale=1.0 / n, bias=eps_col[:, :]).then_inc(done, 1)

            def high_tile(m):
                if m == 0:
                    act.wait_ge(qkv_in, 16 * KT // 2)
                elif 2 <= m < QKV_TILES:
                    act.wait_ge(proj_done, m - 1)
                elif m == QKV_TILES:
                    act.wait_ge(conv_in, 16 * KT)
                    act.wait_ge(proj_done, QKV_TILES)
                elif m >= QKV_TILES + 6:
                    act.wait_ge(part_done, 3 * ((m - QKV_TILES) // 3 - 1))
                raw, _, high = weight_tile(m)
                a.activation(high, raw, ACT.Copy).then_inc(tile_hi, 1)

            def high_xn(t):
                act.wait_ge(xn_turned, t + 1)
                for b in range(2):
                    a.activation(xnT_hi[:, 4 * b:4 * b + 4, t * P:(t + 1) * P], ps[:, 2 * (t % 2) + b, :].rearrange("p (k t) -> p k t", k=4),
                                 ACT.Copy).then_inc(xn_hi, 1)

            act.wait_ge(consts_ready, 1)
            waste = probsT[:, 0:4, :, :].rearrange("p h k s -> p (h k s)")
            for t in range(TB):
                act.wait_ge(x_in[t], 16)
                row_std(X[:, t, :], waste, D, X_SUM + t, X_STD + t, std_ready)
                if t >= 1:
                    high_xn(t - 1)
            high_xn(TB - 1)

            high_tile(0)
            high_tile(1)
            high_tile(2)
            act.wait_ge(proj_done, 2)
            a.activation(qT[:, 0, :], ps[:, 5, :], ACT.Copy).then_inc(proj_act, 1)
            high_tile(3)
            high_tile(4)
            act.wait_ge(proj_done, 4)
            a.activation(qT[:, 2, :], ps[:, 7, :], ACT.Copy).then_inc(proj_act, 1)
            high_tile(5)
            act.wait_ge(proj_done, 6)
            a.activation(c_gate, ps[:, 5, :], ACT.Copy).then_inc(vT_ready, 1)
            act.sem_inc(proj_act, 1)
            for part in range(3):
                high_tile(QKV_TILES + part)
            act.wait_ge(vT_turned, 1)
            a.activation(v_sb, ps[:, 6, :].rearrange("p (t d) -> p t d", t=TB), ACT.Copy).then_inc(proj_act, 1)

            def square_attended(n):
                act.wait_ge(pv_done, n + 1)
                if n >= 1:
                    act.wait_ge(osqs_ready, n)
                a.activation(attn_sq[:, :], ps[:, 6 + n % 2, :], ACT.Square).then_inc(osq_ready, 1)

            for n in range(TB):
                k0 = 0 if n else 1
                if n < TB - 1:
                    for part in range(3):
                        high_tile(QKV_TILES + 3 * (n + 1) + part)
                act.wait_ge(negmax_ready, n + 1)
                for h in range(HEADS):
                    a.activation(scores[:, h, k0 * P:], scores[:, h, k0 * P:], ACT.Exp, bias=smax[:, 2, h:h + 1],
                                 accum_out=smax[:, 4, h:h + 1])
                a.activation(esink[:, :], smax[:, 3, :], ACT.Exp).then_inc(exp_done, 1)
                act.wait_ge(part_done, 3 * n + 1)
                if n >= 1:
                    act.wait_ge(u_ready, n)
                a.activation(c_gate, ps[:, 0, :], ACT.Copy).then_inc(c_ready, 1)
                if n >= 1:
                    square_attended(n - 1)
                for c in (0, 2):
                    act.wait_ge(probs_turned, GRP * n + c + 1)
                    if c == 0 and n >= 1:
                        act.wait_ge(pv_done, n)
                    a.activation(probsT[:, 2 * c:2 * c + 2, k0:2, :],
                                 ps[:, 4, :].rearrange("p (h k t) -> p h k t", h=2, k=2)[:, :, k0:2, :], ACT.Copy).then_inc(pT_act, 1)
                act.wait_ge(convy_ready, n + 1)
                a.activation(conv_sq[:, n, :], conv_y[:, :], ACT.Square).then_inc(sq_ready, 1)
            square_attended(TB - 1)

            act.wait_ge(sums_done, 1)
            a.activation(stat[:, A_STD:A_STD + 2 * TB], ps[:, 4, 0:2 * TB], ACT.Sqrt, scale=1.0 / CW, bias=eps_col[:, :]).then_inc(gstd_ready, 1)

            def turned_h2(t):
                act.wait_ge(h2_turned, t + 1)
                a.activation(xnT[:, 0:4, t * P:(t + 1) * P], ps[:, 4, :].rearrange("p (k t) -> p k t", k=4),
                             ACT.Copy).then_inc(h2T_a, 1)

            def gate_exp(t):
                act.wait_ge(negtop_ready, t + 1)
                b = t % 2
                a.activation(top_x[:, b, :], top8[:, b, 0:TOPK], ACT.Exp, bias=rt_small[:, b, 0:1],
                             accum_out=rt_small[:, b, 1:2]).then_inc(gexp_ready, 1)

            for t in range(TB):
                if t >= 1:
                    turned_h2(t - 1)
                act.wait_ge(x2_half, 2 * (t + 1))
                row_std(X[:, t, :], waste, D, H_SUM + t, H_STD + t, std2_ready)
                if t >= 1:
                    gate_exp(t - 1)
                act.wait_ge(h2_ready, t + 1)
                act.dma_start(h2_dram[t * P:(t + 1) * P, :], normed[:, t % 2, :]).then_inc(h2_stored, 16)
            turned_h2(TB - 1)
            gate_exp(TB - 1)

            def high_rows(i, parity):
                act.wait_ge(rows_turned, i + 1)
                for b in range(2):
                    a.activation(blockT_hi[:, parity, 4 * b:4 * b + 4, :], ps[:, B_X + b, :].rearrange("p (k t) -> p k t", k=4),
                                 ACT.Copy).then_inc(rows_hi, 1)

            def high_piece(i, j, q):
                n = (i * STEPS + j) * PIECES + q
                act.wait_ge(w1_in[j], (i + 1) * 32)
                if not isinstance(n, int) or n >= PIECES:
                    act.wait_ge(w1_used, n - PIECES + 1)
                a.activation(w1_hi[:, q, :], raw_piece(j, q), ACT.Copy).then_inc(hi_ready, 1)

            def turned_act(i, j):
                s = i * STEPS + j
                act.wait_ge(act_turned, s + 1)
                if not isinstance(s, int) or s >= 2:
                    act.wait_ge(w2_done, s - 1)
                a.activation(actT[:, j % 2, :, :], ps[:, B_T, 0:FC].rearrange("p (k t) -> p k t", k=FK),
                             ACT.Copy).then_inc(actT_ready, 1)

            def sigmoid(i, j):
                s = i * STEPS + j
                act.wait_ge(glu_ready, s + 1)
                if not isinstance(s, int) or s >= 2:
                    act.wait_ge(actv_ready, s - 1)
                a.activation(sig[:, j % 2, :], glu_c[:, j % 2, :], ACT.Sigmoid, scale=ALPHA).then_inc(sig_ready, 1)

            def result(i, parity):
                act.wait_ge(w2_done, (i + 1) * STEPS)
                act.wait_ge(slot_ready, i + 1)
                if isinstance(i, int):
                    if i >= 2:
                        act.wait_ge(y_out[parity], 16 * (i // 2))
                else:
                    act.wait_ge(y_out[parity], (i - parity) // 2 * 16)
                a.activation(gated_y[:, parity, :], ps_y, ACT.Copy,
                             scale=cur_slot[:, parity, 1:2].bitcast(F32)).then_inc(y_ready, 1)

            def step(i, j, before, after):
                if after:
                    for q in range(PIECES - 1):
                        high_piece(*after, q)
                if before:
                    turned_act(*before)
                sigmoid(i, j)
                if after:
                    high_piece(*after, PIECES - 1)

            def evacuate(i, parity):
                first = isinstance(i, int) and i == 0
                last = isinstance(i, int) and i == E - 1
                for j in range(STEPS):
                    step(i, j, (i, j - 1) if j else None if first else (i - 1, STEPS - 1),
                         (i, j + 1) if j < STEPS - 1 else None if last else (i + 1, 0))
                    if j == 1 and not first:
                        result(i - 1, 1 - parity)
                    if j == 2 and not last:
                        if not first:
                            act.wait_ge(w1_used, i * STEPS * PIECES)
                        high_rows(i + 1, 1 - parity)

            for q in range(PIECES):
                high_piece(0, 0, q)
            act.wait_ge(h2_stored, 16 * TB)
            high_rows(0, 0)
            expert_blocks(act, evacuate)
            turned_act(E - 1, 3)
            result(E - 1, 1)

            def overflow(o, i):
                high_rows(i, 0)
                for q in range(PIECES):
                    high_piece(i, 0, q)
                for j in range(STEPS):
                    step(i, j, (i, j - 1) if j else None, (i, j + 1) if j < STEPS - 1 else None)
                turned_act(i, STEPS - 1)
                act.wait_ge(w2_done, (i + 1) * STEPS)
                act.wait_ge(slot_ready, i + 1)
                act.wait_ge(y_out[0], 16 * E // 2)
                a.activation(gated_y[:, 0, :], ps_y, ACT.Copy, scale=cur_slot[:, 0, 1:2].bitcast(F32)).then_inc(y_ready, 1)

            overflow_blocks(act, overflow)

            for t in range(TB):
                act.wait_ge(sum_ready, 4 * t + 4)
                a.activation(y_rows[:, t, 1, :], X[:, t, :], ACT.Square, accum_out=stat[:, F_SUM + t:F_SUM + t + 1]).then_inc(act_final, 1)
                act.wait_ge(act_final, t + 1)
                a.activation(stat[:, F_STD + t:F_STD + t + 1], stat[:, F_SUM + t:F_SUM + t + 1], ACT.Sqrt, scale=1.0 / D, bias=eps_col[:, :]).then_inc(fstd_ready, 1)

        @block.gpsimd
        def _(pool):
            g = nc.gpsimd
            chain = [0]

            def then(ins):
                chain[0] += 1
                ins.then_inc(pool_step, 1)
                pool.wait_ge(pool_step, chain[0])

            def keep_unless_zero(view, base, pattern, mult, fill):
                return g.affine_select(out=view, in_=view, compare_op=ALU.not_equal, fill=fill, base=base,
                                       pattern=pattern, channel_multiplier=mult)

            g.memset(eps_col[:, :], EPS)
            g.memset(ones_col[:, :], 1.0)
            g.memset(ones_row[:, :], 1.0)
            g.memset(ones_bf[:, :], 1.0)
            g.memset(earlier[:, :], 1.0)
            g.memset(upto[:, :], 1.0)
            g.memset(ident_bf[:, :], 0.0)
            g.memset(expert_sel[:, :], 0.0)
            then(g.memset(ident[:, :], 0.0))
            then(keep_unless_zero(ident[:, :], 0, [[-1, P]], 1, 1.0))
            pool.sem_inc(consts_ready, 1)
            g.iota(alibi[:, 0, :], [[1, 2 * P]], base=-P, channel_multiplier=-1, allow_small_or_imprecise_dtypes=True)
            then(g.memset(list_fill, UNUSED))
            then(g.affine_select(out=alibi[:, 0, :], in_=alibi[:, 0, :], compare_op=ALU.is_ge, fill=NEG, base=P,
                                 pattern=[[-1, 2 * P]], channel_multiplier=1))
            then(g.affine_select(out=alibi[:, 0, :], in_=alibi[:, 0, :], compare_op=ALU.is_gt, fill=NEG, base=0,
                                 pattern=[[1, 2 * P]], channel_multiplier=-1))
            for h in range(HEADS - 1, -1, -1):
                then(g.tensor_scalar(alibi[:, h, :], alibi[:, 0, :], 2.0 ** (-8.0 * (place_head(h) + 1) / HEADS), None, ALU.mult))
            pool.sem_inc(alibi_ready, 1)
            g.dma_start(list_dram.rearrange("(p r) w -> p (r w)", p=P), list_fill).then_inc(list_filled, 16)
            then(keep_unless_zero(ident_bf[:, :], 0, [[-1, E]], 1, 1.0))
            then(g.affine_select(out=earlier[:, :], in_=earlier[:, :], compare_op=ALU.is_gt, fill=0.0, base=0,
                                 pattern=[[1, P]], channel_multiplier=-1))
            then(g.affine_select(out=upto[:, :], in_=upto[:, :], compare_op=ALU.is_ge, fill=0.0, base=0,
                                 pattern=[[1, E]], channel_multiplier=-1))
            for s in range(3):
                then(keep_unless_zero(expert_sel[:, :], -s * E, [[-1, E]], 1, 1.0))
            g.iota(iota_e[:, :, :], [[0, TOPK], [1, E]], base=0, channel_multiplier=0, allow_small_or_imprecise_dtypes=True)
            g.iota(iota_o[:, :], [[0, 1]], base=0, channel_multiplier=1, allow_small_or_imprecise_dtypes=True)
            then(g.iota(entry[:, :, :, 0:1], [[P * TOPK, TB], [1, TOPK], [0, 1]], base=0, channel_multiplier=TOPK))
            pool.sem_inc(consts_ready, 1)

            def split(cols, n):
                raw = bias_raw[:, 0:n]
                for s in range(3):
                    for q in range(s, 3):
                        then(g.tensor_copy(bias_split[q * E:(q + 1) * E, cols:cols + n], raw[q * E:(q + 1) * E, :]))
                    if s < 2:
                        for q in range(s + 1, 3):
                            then(g.tensor_tensor(raw[q * E:(q + 1) * E, :], raw[q * E:(q + 1) * E, :],
                                                 bias_split[q * E:(q + 1) * E, cols:cols + n], ALU.subtract))

            pool.wait_ge(bias1_in, 48)
            split(0, 2 * FF)
            pool.sem_inc(biases_ready, 1)
            pool.wait_ge(bias2_in, 48)
            split(2 * FF, D)
            pool.sem_inc(biases_ready, 1)

            pool.wait_ge(probs_turned, GRP * TB)
            g.memset(gathered[:, :, :], 0.0).then_inc(rows_cleared, 1)

            pool.wait_ge(list_filled, 16)
            for t in range(TB):
                pool.wait_ge(entries_ready, t + 1)
                for k in range(TOPK):
                    g.indirect_dma_start(list_dram, bass.IndirectOffsetOnAxis(row_i[:, t, k:k + 1], 0), entry[:, t, k, :], None,
                                         bounds_check=SEQ * E - 1, oob_is_err=False).then_inc(list_written, 16)
            pool.wait_ge(list_written, 16 * TB * TOPK)
            g.dma_start(slots[:, :, :, :].rearrange("p b e w -> p b (e w)"),
                        list_dram.rearrange("(b p e) w -> p b (e w)", p=P, e=E)).then_inc(slots_in, 16)
            pool.wait_ge(slots_in, 16)
            pool.wait_ge(tok_ready, 1)
            pool.wait_ge(rows_cleared, 1)

            last_token, last_row = pool.to_reg(SEQ - 1), pool.to_reg(ROWS - 1)
            slots_flat = slots[:, :, :, :].rearrange("p b e w -> p (b e) w")

            def fetch(i, parity, expert, column, done):
                g.tensor_copy(cur_tok[:, parity, :], slot_tok[:, bass.ds(column, 1)])
                g.tensor_copy(bias_sel[:, parity, :], expert_sel[:, bass.ds(expert, 1)].to_broadcast([3 * E, P])).then_inc(cur_copied, 1)
                pool.wait_ge(cur_copied, i + 1)
                pool.sem_inc(cur_ready, 1)
                g.indirect_dma_start(gathered[:, parity, :], None, h2_dram, bass.IndirectOffsetOnAxis(cur_tok[:, parity, :], 0),
                                     bounds_check=last_token, oob_is_err=False).then_inc(done, 16)

            def prepare(i, parity):
                if not isinstance(i, int) or i >= 2:
                    pool.wait_ge(rows_turned, i - 1)
                    pool.wait_ge(w1_used, (i - 1) * STEPS * PIECES)
                fetch(i, parity, i, i, rows_in[parity])

            def take_slots(parity, column):
                g.tensor_copy(cur_slot[:, parity, :].unsqueeze(1), slots_flat[:, bass.ds(column, 1), :]).then_inc(slot_ready, 1)

            def scatter(i, parity, done):
                pool.wait_ge(slot_ready, i + 1)
                pool.wait_ge(y_ready, i + 1)
                pool.sem_inc(scatter_begun, 1)
                g.indirect_dma_start(y_dram, bass.IndirectOffsetOnAxis(cur_slot[:, parity, 0:1], 0), gated_y[:, parity, :], None,
                                     bounds_check=last_row, oob_is_err=False).then_inc(done, 16)

            def move(i, parity):
                if not (isinstance(i, int) and i == E - 1):
                    prepare(i + 1, 1 - parity)
                if not isinstance(i, int):
                    pool.wait_ge(y_out[parity], (i - parity) // 2 * 16)
                elif i >= 2:
                    pool.wait_ge(y_out[parity], 16 * (i // 2))
                take_slots(parity, i)
                if not (isinstance(i, int) and i == 0):
                    scatter(i - 1, 1 - parity, y_out[1 - parity])

            pool.wait_ge(h2_stored, 16 * TB)
            prepare(0, 0)
            pool.wait_ge(ovf_ready, 2)
            g.dma_start(ovf_dram, ovf_tab[:, :]).then_inc(ovf_stored, 16)
            pool.wait_ge(ovf_stored, 16)
            g.dma_start(ovf_row[0:1, :], ovf_dram.rearrange("(a o) w -> a (o w)", a=1)).then_inc(ovf_in, 16)
            expert_blocks(pool, move)
            scatter(E - 1, 1, y_out[1])
            for b in range(2):
                pool.wait_ge(y_out[b], 16 * E // 2)

            def overflow(o, i):
                e = pool.value_load(ovf_row[0:1, bass.ds(o * 4, 1)], min_val=0, max_val=E - 1)
                column = pool.value_load(ovf_row[0:1, bass.ds(o * 4 + 1, 1)], min_val=0, max_val=LIST_BLOCKS * E - 1)
                fetch(i, 0, e, column, rows_ovf)
                take_slots(0, column)
                scatter(i, 0, y_ovf)
                pool.wait_ge(y_ovf, (o + 1) * 16)

            overflow_blocks(pool, overflow)
            pool.sem_inc(all_scattered, 1)


_INS = ["x", "g_mix", "w_in", "conv_w", "sinks", "g_attn_out", "g_conv_out", "w_out",
        "g_ffn", "w_router", "b_router", "w1", "b1", "w2", "b2", "g_final"]


def kernel(**inputs):
    import numpy as _np
    import concourse.bacc as _bacc
    from concourse import mybir as _mybir
    from concourse.bass_utils import run_bass_kernel_spmd as _run

    nc = _bacc.Bacc("TRN2", target_bir_lowering=False, num_devices=1)
    arrays, args = {}, []
    for name in _INS:
        a = _np.ascontiguousarray(inputs[name])
        arrays[f"in_{name}"] = a
        args.append(nc.dram_tensor(f"in_{name}", a.shape, _mybir.dt.from_np(a.dtype), kind="ExternalInput").ap())
    args.append(nc.dram_tensor("out", (1, SEQ, D), F32, kind="ExternalOutput").ap())
    layer_kernel(nc, *args)
    r = _run(nc, [arrays], core_ids=[0])
    return r.results[0]["out"]
```

```python
from contextlib import ExitStack

import concourse.bass as bass
from concourse import mybir

F32 = mybir.dt.float32
F32R = mybir.dt.float32r
BF16 = mybir.dt.bfloat16
I32 = mybir.dt.int32
U32 = mybir.dt.uint32
ALU = mybir.AluOpType
ACT = mybir.ActivationFunctionType
AX_X = mybir.AxisListType.X

P = 128
D = 1024
SEQ = 512
TB = SEQ // P
KT = D // P
HEADS, KV_HEADS, HD = 8, 2, 64
GRP = HEADS // KV_HEADS
AW = HEADS * HD
CW = D - AW
CT = CW // P
CONV_K = 3
QKV = (HEADS + 2 * KV_HEADS) * HD
CONV_COLS = 3 * CW
QKV_TILES = QKV // P
E = 32
TOPK = 4
FF = 1024
STEPS = 4
FC = FF // STEPS
FK = FC // P
PIECES = 4
PK = KT // PIECES
PIECE = PK * 2 * FC
ALPHA = 1.702
LIMIT = 7.0
EPS = 1e-5
NEG = -1e30
UNUSED = 1 << 20
ROWS = SEQ * TOPK
LIST_BLOCKS = SEQ // P
MAX_OVERFLOW = ROWS // (P + 1)
OVF_ROWS = 16
W_OUT_LATE = (3, 4, 5)
W_OUT_EARLY = tuple(k for k in range(KT) if k not in W_OUT_LATE)
W_OUT_PLACES = dict(zip(W_OUT_EARLY + W_OUT_LATE, (6, 7, 4, 5, 0, 1, 2, 3)))


def head_place(h):
    return (h % 2) * (HEADS // 2) + h // 2


def place_head(at):
    return (at % (HEADS // 2)) * 2 + at // (HEADS // 2)


def layer_kernel(nc, x, g_mix, w_in, conv_w, sinks, g_attn_out, g_conv_out, w_out,
                 g_ffn, w_router, b_router, w1, b1, w2, b2, g_final, out):
    ctx = ExitStack()
    with ctx:
        def sb(name, shape, dt=F32):
            return ctx.enter_context(nc.sbuf_tensor(name, shape, dt))

        def sb_r(name, shape, offset):
            return nc.alloc_sbuf_tensor_at(name, shape, F32R, offset=offset)

        def sem(name):
            return ctx.enter_context(nc.semaphore(name))

        h2_dram = nc.dram_tensor("h2_rows", (SEQ, D), F32).ap()
        list_dram = nc.dram_tensor("slot_list", (SEQ * E, 2), I32).ap()
        y_dram = nc.dram_tensor("expert_rows", (ROWS, D), F32).ap()

        ovf_dram = nc.dram_tensor("overflow_table", (OVF_ROWS, 4), I32).ap()

        X = sb("X", [P, TB, D])
        xnT_lo = sb_r("xnT_lo", [P, TB, KT, P], nc.sbuf_base - TB * D * 4)
        gain_a = sb("gain_a", [P, D])
        gain_ffn = sb("gain_ffn", [P, D])
        ring1 = sb("ring1", [P, STEPS * KT * 2 * FC])
        w1_lo = sb_r("w1_lo", [P, STEPS, PIECES, PIECE], nc.sbuf_base - STEPS * KT * 2 * FC * 4)
        ring2 = sb("ring2", [P, STEPS * FK * D])
        ring2_r = sb_r("ring2_r", [P, STEPS * FK * D], nc.sbuf_base - STEPS * FK * D * 4)
        xnT = sb("xnT", [P, KT, SEQ])
        xnT_hi = sb_r("xnT_hi", [P, KT, SEQ], nc.sbuf_base - KT * SEQ * 4)
        normed = sb("normed", [P, 2, D])
        scores = sb("scores", [P, HEADS, 2 * P])
        probsT = sb("probsT", [P, HEADS, 2, P])
        blockT_hi = sb_r("blockT_hi", [P, 2, KT, P], nc.sbuf_base - HEADS * 2 * P * 4)
        mixer = sb("mixer", [P, PIECES * PIECE + 2 * KT * P])
        w1_hi = sb_r("w1_hi", [P, PIECES, PIECE], nc.sbuf_base - (PIECES * PIECE + 2 * KT * P) * 4)
        blockT_lo = sb_r("blockT_lo", [P, 2, KT, P], nc.sbuf_base - 2 * KT * P * 4)
        early = sb("early", [P, 4 * SEQ + CONV_K - 1])
        w2_hi = sb_r("w2_hi", [P, 2, D], nc.sbuf_base - (4 * SEQ + CONV_K - 1) * 4)
        bias_split = sb("bias_split", [3 * E, 2 * FF + D], BF16)
        expert_sel = sb("expert_sel", [3 * E, E], BF16)
        bias_sel = sb("bias_sel", [3 * E, 2, P], BF16)
        ident = sb("ident", [P, P])
        earlier = sb("earlier", [P, P], BF16)
        ones_bf = sb("ones_bf", [P, P], BF16)
        ones_col = sb("ones_col", [P, 1])
        ones_row = sb("ones_row", [1, P])
        upto = sb("upto", [E, E], BF16)
        ident_bf = sb("ident_bf", [E, E], BF16)
        iota_e = sb("iota_e", [P, TOPK, E])
        iota_o = sb("iota_o", [OVF_ROWS, 1])
        eps_col = sb("eps_col", [P, 1])
        table_use = sb("table_use", [P, 1])
        w_rt = sb("w_rt", [P, KT, E])
        b_rt = sb("b_rt", [1, E])
        conv_wc = sb("conv_wc", [P, CONV_K, CT])
        g_conv = sb("g_conv", [P, CT])
        g_attn = sb("g_attn", [P, CT])
        sink_b = sb("sink_b", [P, HEADS])
        stat = sb("stat", [P, 80])
        r_group = sb("r_group", [P, 2, TB])
        smax = sb("smax", [P, 6, HEADS])
        esink = sb("esink", [P, HEADS])
        logit = sb("logit", [P, 2, E])
        top8 = sb("top8", [P, 2, 8])
        top8_i = sb("top8_i", [P, 2, 8], U32)
        top_e = sb("top_e", [P, 2, TOPK])
        top_x = sb("top_x", [P, 2, TOPK])
        rt_small = sb("rt_small", [P, 2, 4])
        onehot = sb("onehot", [P, 2, TOPK, E])
        chosen = sb("chosen", [P, TB, E], BF16)
        chosen_cum = sb("chosen_cum", [P, TB + 1, E], BF16)
        rankrow = sb("rankrow", [P, 2, E])
        row_f = sb("row_f", [P, 2, TOPK])
        first_row = sb("first_row", [P, TB])
        smaller = sb("smaller", [P, TOPK, TOPK])
        row_i = sb("row_i", [P, TB, TOPK], I32)
        entry = sb("entry", [P, TB, TOPK, 2], I32)
        slots = sb("slots", [P, LIST_BLOCKS, E, 2], I32)
        slot_tok = sb("slot_tok", [P, LIST_BLOCKS * E], I32)
        cur_slot = sb("cur_slot", [P, 2, 2], I32)
        cur_tok = sb("cur_tok", [P, 2, 1], I32)
        ovf_f = sb("ovf_f", [OVF_ROWS, 6])
        ovf_m = sb("ovf_m", [OVF_ROWS, 3, E])
        ovf_nb = sb("ovf_nb", [E, 4])
        ovf_nb16 = sb("ovf_nb16", [E, OVF_ROWS], BF16)
        ovf_tab = sb("ovf_tab", [OVF_ROWS, 4], I32)
        ovf_row = sb("ovf_row", [1, OVF_ROWS * 4], I32)

        ps = ctx.enter_context(nc.psum_tensor("ps", [P, 8, 512], F32))

        w_conv_sb = ring1[:, 0:KT * CONV_COLS].rearrange("p (k c) -> p k c", k=KT)
        w_lo_qkv = ring2_r[:, 0:KT * QKV].rearrange("p (k c) -> p k c", k=KT)
        w_lo_conv = w1_lo[:, :, :, :].rearrange("p s q c -> p (s q c)")[:, 0:KT * CONV_COLS].rearrange("p (k c) -> p k c", k=KT)

        def weight_tile(m):
            if m < QKV_TILES:
                c0 = (AW, 0, P, 2 * P, 3 * P, AW + P)[m]
                raw, low, at = w_qkv_sb, w_lo_qkv, KT * QKV + (m % 2) * KT * P
            else:
                n, part = (m - QKV_TILES) // 3, (m - QKV_TILES) % 3
                c0 = (1, 2, 0)[part] * CW + n * P
                raw, low, at = w_conv_sb, w_lo_conv, ((n % 2) * 3 + part) * KT * P
            return raw[:, :, c0:c0 + P], low[:, :, c0:c0 + P], ring2_r[:, at:at + KT * P].rearrange("p (k c) -> p k c", k=KT)

        spare = KT * CONV_COLS
        alibi = ring1[:, spare:spare + HEADS * 2 * P].rearrange("p (h s) -> p h s", h=HEADS)
        bias_raw = ring1[0:3 * E, spare + HEADS * 2 * P:spare + HEADS * 2 * P + 2 * FF]
        w_qkv_sb = ring2[:, 0:KT * QKV].rearrange("p (k c) -> p k c", k=KT)
        w_out_sb = ring2[:, :].rearrange("p (k n) -> p k n", k=KT)
        w_out_lo = ring2_r[:, :].rearrange("p (k n) -> p k n", k=KT)
        w_out_hi = w1_lo[:, 2:4, :, :].rearrange("p s q c -> p (s q) c")
        ring1_v = ring1[:, :].rearrange("p (s k h c) -> p s k h c", s=STEPS, k=KT, h=2)
        ring2_v = ring2[:, :].rearrange("p (s k n) -> p s k n", s=STEPS, k=FK)
        list_fill = slots[:, :, :, :].rearrange("p b e w -> p (b e w)")
        conv_sq = normed[:, :, :].rearrange("p a (c t) -> p (a c) t", c=2)
        qT = mixer[:, 0:4 * SEQ].rearrange("p (a t) -> p a t", a=HEADS // 2)
        kT = mixer[:, 4 * SEQ:6 * SEQ].rearrange("p (g t) -> p g t", g=KV_HEADS)
        v_sb = mixer[:, 6 * SEQ:7 * SEQ].rearrange("p (t d) -> p t d", t=TB)
        c_gate = mixer[:, 7 * SEQ:8 * SEQ]
        convT = mixer[:, 8 * SEQ:12 * SEQ].rearrange("p (c t) -> p c t", c=CT)
        attnT = qT
        mixT_hi = xnT_hi
        attnT_lo = w1_hi[:, :, :].rearrange("p q c -> p (q c)")[:, 0:CT * SEQ].rearrange("p (c t) -> p c t", c=CT)
        convT_lo = blockT_lo[:, :, :, :].rearrange("p b k t -> p (b k t)").rearrange("p (c t) -> p c t", c=CT)
        attn_sq, attn_sqs, conv_y = (early[:, n * SEQ:(n + 1) * SEQ] for n in range(3))
        u_pad = early[:, 3 * SEQ:]
        conv_sqs = u_pad[:, 0:SEQ]
        picked = attn_sq[:, 0:TOPK * E].rearrange("p (k e) -> p k e", k=TOPK)
        gathered = scores[:, :, :].rearrange("p (b c) s -> p b (c s)", b=2)
        gated_y = normed
        step_v = xnT[:, :, :].rearrange("p k t -> p (k t)")
        glu_c = step_v[:, 0:2 * FC].rearrange("p (b c) -> p b c", b=2)
        lin_c = step_v[:, 2 * FC:4 * FC].rearrange("p (b c) -> p b c", b=2)
        sig = step_v[:, 4 * FC:6 * FC].rearrange("p (b c) -> p b c", b=2)
        prod = step_v[:, 6 * FC:8 * FC].rearrange("p (b c) -> p b c", b=2)
        act_v = step_v[:, 8 * FC:10 * FC].rearrange("p (b c) -> p b c", b=2)
        actT = step_v[:, 10 * FC:11 * FC].rearrange("p (b t) -> p b t", b=2)
        split_act = xnT_hi[:, :, :].rearrange("p k t -> p (k t)")[:, 11 * FC:13 * FC].rearrange("p (w b t) -> p w b t", w=2, b=2)
        actT_hi, actT_lo = split_act[:, 0], split_act[:, 1]
        y_rows = ring1[:, :].rearrange("p (k t n) -> p k t n", t=TB, k=TOPK)

        X_SUM, X_STD, X_R, A_STD, C_STD, H_SUM, H_STD, H_R, F_SUM, F_STD, F_R = range(0, 11 * TB, TB)

        B_H, B_Y, B_T, B_X = 0, 2, 4, 5
        ps_y = ps[:, B_Y:B_Y + 2, :].rearrange("p b n -> p (b n)")

        x_in = [sem(f"x_in{t}") for t in range(TB)]
        gains_in, small_in = sem("gains_in"), sem("small_in")
        qkv_in, conv_in, wout_early, wout_late = sem("qkv_in"), sem("conv_in"), sem("wout_early"), sem("wout_late")
        bias1_in, bias2_in, gfinal_in = sem("bias1_in"), sem("bias2_in"), sem("gfinal_in")
        w1_in = [sem(f"w1_in{j}") for j in range(STEPS)]
        w2_in = [sem(f"w2_in{j}") for j in range(STEPS)]
        dve_step, act_step, pool_step = sem("dve_step"), sem("act_step"), sem("pool_step")
        consts_ready, alibi_ready, biases_ready = sem("consts_ready"), sem("alibi_ready"), sem("biases_ready")
        std_ready, xn_ready, xn_turned = sem("std_ready"), sem("xn_ready"), sem("xn_turned")
        xn_hi, xn_lo = sem("xn_hi"), sem("xn_lo")
        tile_hi, tile_lo = sem("tile_hi"), sem("tile_lo")
        x_again = [sem(f"x_again{t}") for t in range(TB)]
        k_ready, k_doubled = sem("k_ready"), sem("k_doubled")
        proj_done, proj_act, proj_dve = sem("proj_done"), sem("proj_act"), sem("proj_dve")
        scores_done, scores_read = sem("scores_done"), sem("scores_read")
        negmax_ready, exp_done = sem("negmax_ready"), sem("exp_done")
        part_done, c_ready, u_ready, conv_read = sem("part_done"), sem("c_ready"), sem("u_ready"), sem("conv_read")
        convy_ready, sq_ready, convT_ready = sem("convy_ready"), sem("sq_ready"), sem("convT_ready")
        probs_turned, pT_act, pT_dve = sem("probs_turned"), sem("pT_act"), sem("pT_dve")
        vT_ready, vT_turned, probs_ready = sem("vT_ready"), sem("vT_turned"), sem("probs_ready")
        pv_done, osq_ready, o_ready, osqs_ready, csqs_ready = sem("pv_done"), sem("osq_ready"), sem("o_ready"), sem("osqs_ready"), sem("csqs_ready")
        sums_done, gstd_ready = sem("sums_done"), sem("gstd_ready")
        wout_hi, wout_lo, mix_hi, mix_lo = sem("wout_hi"), sem("wout_lo"), sem("mix_hi"), sem("mix_lo")
        oproj_done, x2_half, std2_ready, h2_ready = sem("oproj_done"), sem("x2_half"), sem("std2_ready"), sem("h2_ready")
        h2_turned, h2_stored = sem("h2_turned"), sem("h2_stored")
        h2T_a, h2T_b = sem("h2T_a"), sem("h2T_b")
        logits_done, negtop_ready, gexp_ready = sem("logits_done"), sem("negtop_ready"), sem("gexp_ready")
        chosen_ready, rank_done, placed, entries_ready = sem("chosen_ready"), sem("rank_done"), sem("placed"), sem("entries_ready")
        counts_done, nb_ready, prefix_done, ovf_ready, ovf_in = sem("counts_done"), sem("nb_ready"), sem("prefix_done"), sem("ovf_ready"), sem("ovf_in")
        ovf_stored = sem("ovf_stored")
        list_filled, list_written, slots_in, tok_ready = sem("list_filled"), sem("list_written"), sem("slots_in"), sem("tok_ready")
        cur_copied, cur_ready = sem("cur_copied"), sem("cur_ready")
        rows_in = [sem(f"rows_in{b}") for b in range(2)]
        rows_cleared = sem("rows_cleared")
        rows_turned, rows_hi, rows_lo = sem("rows_turned"), sem("rows_hi"), sem("rows_lo")
        hi_ready, lo_ready, w1_used, slot_ready = sem("hi_ready"), sem("lo_ready"), sem("w1_used"), sem("slot_ready")
        h_read, glu_ready, sig_ready = sem("h_read"), sem("glu_ready"), sem("sig_ready")
        prod_ready, actv_ready, act_turned = sem("prod_ready"), sem("actv_ready"), sem("act_turned")
        actT_hi_ready, actT_lo_ready = sem("actT_hi_ready"), sem("actT_lo_ready")
        w2_hi_ready, w2_lo_ready = sem("w2_hi_ready"), sem("w2_lo_ready")
        w2_done, y_ready = sem("w2_done"), sem("y_ready")
        scatter_begun = sem("scatter_begun")
        y_out = [sem(f"y_out{b}") for b in range(2)]
        rows_ovf, y_ovf = sem("rows_ovf"), sem("y_ovf")
        all_scattered = sem("all_scattered")
        yrow_in = [[sem(f"yrow{k}_in{t}") for t in range(TB)] for k in range(TOPK)]
        sum_ready, fstd_ready, fin_ready, out_written = sem("sum_ready"), sem("fstd_ready"), sem("fin_ready"), sem("out_written")
        dve_final, act_final = sem("dve_final"), sem("act_final")

        w2_lo = ring2_r[:, :].rearrange("p (s k n) -> p s k n", s=STEPS, k=FK)[:, :, FK - 1, :]

        def raw_piece(j, q):
            return ring1_v[:, j, q * PK:(q + 1) * PK, :, :].rearrange("p k h c -> p (k h c)")

        block = ctx.enter_context(nc.Block())

        def expert_blocks(eng, run):
            run(0, 0)
            run(1, 1)
            with eng.Fori(2, E - 2, 2) as i:
                run(i, 0)
                run(i + 1, 1)
            run(E - 2, 0)
            run(E - 1, 1)

        def overflow_count(eng):
            eng.wait_ge(ovf_in, 16)
            return eng.value_load(ovf_row[0:1, 2:3], min_val=0, max_val=MAX_OVERFLOW)

        def overflow_blocks(eng, n_ovf, run, finish=None):
            with eng.If(n_ovf > 0):
                with eng.Fori(0, MAX_OVERFLOW) as o:
                    with eng.If(n_ovf > o):
                        run(o, o + E)
                if finish:
                    finish()

        @block.sync
        def _(sp):
            with nc.allow_non_contiguous_dma(reason="small parameter columns"):
                for t in range(TB):
                    sp.dma_start(X[:, t, :], x[0, t * P:(t + 1) * P, :]).then_inc(x_in[t], 16)
                    if t == 0:
                        sp.dma_start(gain_a[:, :], g_mix[0].partition_broadcast(P)).then_inc(gains_in, 16)
                w_in_v = w_in[0].rearrange("(k p) c -> p k c", p=P)
                for k in range(0, KT, 2):
                    sp.dma_start(w_qkv_sb[:, k:k + 2, :], w_in_v[:, k:k + 2, 0:QKV]).then_inc(qkv_in, 16)
                for odd in range(2):
                    sp.dma_start(sink_b[:, odd * HEADS // 2:(odd + 1) * HEADS // 2],
                                 sinks[0].rearrange("(a b) -> b a", b=2)[odd].partition_broadcast(P)).then_inc(small_in, 16)
                sp.dma_start(g_attn[:, :], g_attn_out[0].rearrange("(c p) -> p c", p=P)).then_inc(small_in, 16)
                sp.dma_start(conv_wc[:, :, :], conv_w[0].rearrange("w (c p) -> p w c", p=P)).then_inc(small_in, 16)
                sp.dma_start(g_conv[:, :], g_conv_out[0].rearrange("(c p) -> p c", p=P)).then_inc(small_in, 16)
                for k in range(KT):
                    sp.dma_start(w_conv_sb[:, k, :], w_in_v[:, k, QKV:]).then_inc(conv_in, 16)
                sp.dma_start(gain_ffn[:, :], g_ffn[0].partition_broadcast(P)).then_inc(small_in, 16)
                sp.dma_start(w_rt[:, :, :], w_router[0].rearrange("(k p) e -> p k e", p=P)).then_inc(small_in, 16)
                sp.dma_start(b_rt[:, :], b_router).then_inc(small_in, 16)
            for g in range(3):
                sp.dma_start(bias_raw[g * E:(g + 1) * E, :], b1[0]).then_inc(bias1_in, 16)
            sp.wait_ge(xn_ready, TB)
            sp.dma_start(gain_a[:, :], g_final.partition_broadcast(P)).then_inc(gfinal_in, 16)
            sp.wait_ge(k_ready, 2)
            sp.dma_start(kT[HD:P, 0, :], kT[0:HD, 0, :]).then_inc(k_doubled, 16)
            sp.dma_start(kT[0:HD, 1, :], kT[HD:P, 1, :]).then_inc(k_doubled, 16)
            sp.wait_ge(biases_ready, 1)
            for g in range(3):
                sp.dma_start(bias_raw[g * E:(g + 1) * E, 0:D], b2[0]).then_inc(bias2_in, 16)

            w_out_v = w_out[0].rearrange("(k p) n -> p k n", p=P)
            sp.wait_ge(part_done, 3 * (CT - 1))
            for k in W_OUT_EARLY:
                sp.dma_start(w_out_sb[:, k, :], w_out_v[:, k, :]).then_inc(wout_early, 16)
            for part, k in enumerate(W_OUT_LATE):
                sp.wait_ge(part_done, 3 * (CT - 1) + part + 1)
                sp.dma_start(w_out_sb[:, k, :], w_out_v[:, k, :]).then_inc(wout_late, 16)
            for t in range(TB):
                sp.dma_start(X[:, t, :], x[0, t * P:(t + 1) * P, :]).then_inc(x_again[t], 16)

            def load_w1(j, e):
                src = w1[0, e].rearrange("(k p) (h c) -> p k h c", p=P, h=2)
                for h in range(2):
                    sp.dma_start(ring1_v[:, j, :, h, :], src[:, :, h, j * FC:(j + 1) * FC]).then_inc(w1_in[j], 16)

            def load_w2(j, e):
                src = w2[0, e].rearrange("(s k p) n -> p s k n", p=P, k=FK)
                sp.dma_start(ring2_v[:, j, :, :], src[:, j, :, :]).then_inc(w2_in[j], 16)

            def load(i, _parity):
                for j in range(STEPS):
                    if isinstance(i, int) and i == 0:
                        if j == 0:
                            sp.wait_ge(part_done, 3 * CT)
                        if j == 2:
                            sp.wait_ge(oproj_done, 2 * TB)
                        load_w1(j, i)
                        continue
                    sp.wait_ge(w1_used, ((i - 1) * STEPS + j + 1) * PIECES)
                    load_w1(j, i)
                    if j >= 2:
                        sp.wait_ge(w2_done, (i - 1) * STEPS + j - 1)
                        load_w2(j - 2, i)
                    elif not (isinstance(i, int) and i == 1):
                        sp.wait_ge(w2_done, (i - 2) * STEPS + j + 3)
                        load_w2(j + 2, i - 1)
                if isinstance(i, int) and i == 0:
                    sp.wait_ge(rows_in[0], 16)
                    for j in range(STEPS):
                        load_w2(j, i)

            expert_blocks(sp, load)
            for j in range(2, STEPS):
                sp.wait_ge(w2_done, (E - 2) * STEPS + j + 1)
                load_w2(j, E - 1)

            y_dram_v = y_dram.rearrange("(t p k) n -> k p t n", p=P, k=TOPK)

            def load_row(k):
                for t in range(TB):
                    sp.dma_start(y_rows[:, k, t, :], y_dram_v[k][:, t, :]).then_inc(yrow_in[k][t], 16)

            n_ovf = overflow_count(sp)
            with sp.If(n_ovf < 1):
                for k in range(TOPK - 1):
                    sp.wait_ge(w1_used, ((E - 1) * STEPS + k + 1) * PIECES)
                    for b in range(2):
                        sp.wait_ge(y_out[b], 16 * ((E - TOPK + k + 2 - b) // 2))
                    load_row(k)

            def load_overflow(o, i):
                e = sp.value_load(ovf_row[0:1, bass.ds(o * 4, 1)], min_val=0, max_val=E - 1)
                for j in range(STEPS):
                    sp.wait_ge(w1_used, ((i - 1) * STEPS + j + 1) * PIECES)
                    load_w1(j, e)
                    sp.wait_ge(w2_done, (i - 1) * STEPS + j + 1)
                    load_w2(j, e)

            def finish_overflow():
                sp.wait_ge(all_scattered, 1)
                for k in range(TOPK - 1):
                    load_row(k)

            overflow_blocks(sp, n_ovf, load_overflow, finish_overflow)

            sp.wait_ge(all_scattered, 1)
            load_row(TOPK - 1)
            for t in range(TB):
                sp.wait_ge(fin_ready, t + 1)
                sp.dma_start(out[0, t * P:(t + 1) * P, :], y_rows[:, 0, t, :]).then_inc(out_written, 16)
            sp.wait_ge(out_written, 16 * TB)

        @block.tensor
        def _(pe):
            mm = pe.matmul

            def turn_rows(src, bank):
                for k in range(KT):
                    ins = pe.transpose(ps[:, bank + k // 4, (k % 4) * P:(k % 4 + 1) * P],
                                       src[:, k * P:(k + 1) * P], ident[:, :])
                return ins

            pe.wait_ge(consts_ready, 1)
            for t in range(TB):
                pe.wait_ge(xn_ready, t + 1)
                if t >= 2:
                    pe.wait_ge(xn_lo, 2 * (t - 1))
                turn_rows(normed[:, t % 2, :], 2 * (t % 2)).then_inc(xn_turned, 1)

            def project(m, bank, done):
                pe.wait_ge(tile_lo, m + 1)
                _, low, high = weight_tile(m)
                for k in range(KT):
                    mm(ps[:, bank, :], high[:, k, :], xnT_hi[:, k, :], start=(k == 0), stop=False)
                    mm(ps[:, bank, :], high[:, k, :], xnT_lo[:, :, k, :], start=False, stop=False)
                    ins = mm(ps[:, bank, :], low[:, k, :], xnT_hi[:, k, :], start=False, stop=(k == KT - 1))
                if done:
                    ins.then_inc(done, 1)

            pe.wait_ge(xn_lo, 2 * TB)
            for m in range(QKV_TILES):
                if m == 4:
                    pe.wait_ge(proj_dve, 1)
                if m == 5:
                    pe.wait_ge(proj_act, 1)
                project(m, 4 + m % 4, proj_done)

            def scores_of(n, odd):
                k0 = 0 if n else 1
                if n == 0 and not odd:
                    pe.wait_ge(proj_dve, 3)
                    pe.wait_ge(proj_act, 2)
                    pe.wait_ge(k_doubled, 32)
                if n and not odd:
                    pe.wait_ge(u_ready, n)
                if n and odd:
                    pe.wait_ge(conv_read, n)
                for h in range(odd, HEADS, 2):
                    g, half, at = h // GRP, (h % 2) * HD, head_place(h)
                    ins = mm(ps[:, at // 2, (at % 2) * 2 * P + k0 * P:(at % 2 + 1) * 2 * P],
                             qT[half:half + HD, h // 2, n * P:(n + 1) * P],
                             kT[half:half + HD, g, (n - 1 + k0) * P:(n + 1) * P], start=True, stop=True)
                ins.then_inc(scores_done, 1)

            def turn_probs(n, c):
                q = GRP * n + c
                if q >= 2:
                    pe.wait_ge(pT_dve if c % 2 else pT_act, q // 2)
                for h in (2 * c, 2 * c + 1):
                    for kb in range(0 if n else 1, 2):
                        ins = pe.transpose(ps[:, 4 + c % 2, ((h % 2) * 2 + kb) * P:((h % 2) * 2 + kb + 1) * P],
                                           scores[:, h, kb * P:(kb + 1) * P], ident[:, :])
                ins.then_inc(probs_turned, 1)

            def attend(n):
                k0 = 0 if n else 1
                pe.wait_ge(pT_act, 2 * (n + 1))
                pe.wait_ge(pT_dve, 2 * (n + 1))
                if n == 0:
                    pe.wait_ge(proj_act, 4)
                if n >= 2:
                    pe.wait_ge(o_ready, n - 1)
                for odd in range(2):
                    for g in range(KV_HEADS):
                        at = odd * (HEADS // 2) + 2 * g
                        for kb in range(k0, 2):
                            ins = mm(ps[odd * HD:(odd + 1) * HD, 6 + n % 2, 2 * g * P:2 * (g + 1) * P],
                                     v_sb[:, n - 1 + kb, g * HD:(g + 1) * HD], probsT[:, at:at + 2, kb, :],
                                     start=(kb == k0), stop=(kb == 1))
                ins.then_inc(pv_done, 1)

            scores_of(0, 0)
            scores_of(0, 1)
            pe.wait_ge(vT_ready, 1)
            for t in range(TB):
                ins = pe.transpose(ps[:, 6, t * P:(t + 1) * P], c_gate[:, t * P:(t + 1) * P], ident[:, :])
            ins.then_inc(vT_turned, 1)
            for n in range(TB):
                pe.wait_ge(scores_read, 2 * n + 1)
                project(QKV_TILES + 3 * n, 0, part_done)
                if n:
                    attend(n - 1)
                project(QKV_TILES + 3 * n + 1, 1, part_done)
                pe.wait_ge(scores_read, 2 * n + 2)
                project(QKV_TILES + 3 * n + 2, 2, part_done)
                pe.wait_ge(probs_ready, n + 1)
                turn_probs(n, 0)
                turn_probs(n, 1)
                if n < TB - 1:
                    scores_of(n + 1, 0)
                turn_probs(n, 2)
                turn_probs(n, 3)
                if n < TB - 1:
                    scores_of(n + 1, 1)

            def out_proj(t, n):
                if t == 0 and n == 0:
                    pe.wait_ge(u_ready, CT)
                if t == 0 and n == 1:
                    pe.wait_ge(conv_read, CT)
                if n == 0:
                    pe.wait_ge(mix_lo, t + 1)
                if t:
                    pe.wait_ge(x2_half, 2 * (t - 1) + n + 1)
                cols = slice(n * 512, (n + 1) * 512)
                for order, k in enumerate(W_OUT_EARLY + W_OUT_LATE):
                    if t == 0 and n == 0:
                        pe.wait_ge(wout_lo, order + 1)
                    half, c = k // CT, k % CT
                    bank = ps[:, 2 * n + half, :]
                    high, low = mixT_hi[:, k, t * P:(t + 1) * P], (attnT_lo, convT_lo)[half][:, c, t * P:(t + 1) * P]
                    w_high = w_out_hi[:, W_OUT_PLACES[k], cols]
                    mm(bank, high, w_high, start=(k in (0, W_OUT_LATE[-1] + 1)), stop=False)
                    mm(bank, high, w_out_lo[:, k, cols], start=False, stop=False)
                    ins = mm(bank, low, w_high, start=False, stop=(k in (CT - 1, W_OUT_LATE[-1])))
                ins.then_inc(oproj_done, 1)

            def group_sums():
                pe.wait_ge(osqs_ready, TB)
                pe.wait_ge(csqs_ready, 1)
                for half, src in enumerate((attn_sqs, conv_sqs)):
                    for t in range(TB):
                        ins = mm(ps[:, 4, half * TB + t:half * TB + t + 1], src[:, t * P:(t + 1) * P], ones_col[:, :],
                                 start=True, stop=True)
                ins.then_inc(sums_done, 1)

            def turn_h2(t):
                pe.wait_ge(h2_ready, t + 1)
                if t == 0:
                    pe.wait_ge(gstd_ready, 1)
                else:
                    pe.wait_ge(h2T_a, t)
                    pe.wait_ge(h2T_b, t)
                turn_rows(normed[:, t % 2, :], 4).then_inc(h2_turned, 1)

            def router(t):
                pe.wait_ge(h2T_a, t + 1)
                pe.wait_ge(h2T_b, t + 1)
                if t == 0:
                    pe.wait_ge(small_in, 16 * 8)
                else:
                    pe.wait_ge(chosen_ready, t)
                mm(ps[:, 6, 0:E], ones_row[:, :], b_rt[:, :], start=True, stop=False)
                for k in range(KT):
                    ins = mm(ps[:, 6, 0:E], xnT[:, k, t * P:(t + 1) * P], w_rt[:, k, :],
                             start=False, stop=(k == KT - 1))
                ins.then_inc(logits_done, 1)

            def rank(t):
                pe.wait_ge(chosen_ready, t + 1)
                if t == 0:
                    pe.wait_ge(consts_ready, 2)
                else:
                    pe.wait_ge(placed, t)
                ins = mm(ps[:, 7, 0:E], earlier[:, :], chosen[:, t, :], start=True, stop=(t == 0))
                if t:
                    ins = mm(ps[:, 7, 0:E], ones_bf[:, :], chosen_cum[:, t, :], start=False, stop=True)
                ins.then_inc(rank_done, 1)

            attend(TB - 1)
            out_proj(0, 0)
            out_proj(0, 1)
            group_sums()
            for t in range(1, TB):
                out_proj(t, 0)
                turn_h2(t - 1)
                if t >= 2:
                    rank(t - 2)
                out_proj(t, 1)
                router(t - 1)
            turn_h2(TB - 1)
            rank(TB - 2)
            router(TB - 1)
            rank(TB - 1)
            mm(ps[0:E, 0, 0:1], chosen_cum[:, TB, :], ones_bf[:, 0:1], start=True, stop=True).then_inc(counts_done, 1)
            pe.wait_ge(nb_ready, 1)
            mm(ps[0:OVF_ROWS, 1, 0:E], ovf_nb16[:, :], upto[:, :], start=True, stop=True)
            mm(ps[0:OVF_ROWS, 1, E:2 * E], ovf_nb16[:, :], ident_bf[:, :], start=True, stop=True).then_inc(prefix_done, 1)

            def turn_block(i, parity):
                pe.wait_ge(rows_in[parity], 16 * (i // 2 + 1) if isinstance(i, int) else half_up(i, parity) * 16)
                if not (isinstance(i, int) and i == 0):
                    pe.wait_ge(rows_lo, i * 2)
                turn_rows(gathered[:, parity, :], B_X).then_inc(rows_turned, 1)

            def half_up(i, parity):
                return (i + 2 - parity) // 2

            def w1_step(i, j, parity):
                s = i * STEPS + j
                if j == 0:
                    pe.wait_ge(rows_lo, (i + 1) * 2)
                    pe.wait_ge(cur_ready, i + 1)
                if not isinstance(s, int) or s >= 2:
                    pe.wait_ge(h_read, s - 1)
                h = ps[:, B_H + j % 2, :]
                mm(h, bias_sel[:, parity, :], bias_split[:, 0:2 * FF].rearrange("p (h c) -> p h c", h=2)[:, :, j * FC:(j + 1) * FC],
                   start=True, stop=False)
                for q in range(PIECES):
                    pe.wait_ge(lo_ready, s * PIECES + q + 1)
                    for k in range(q * PK, (q + 1) * PK):
                        cols = slice((k % PK) * 2 * FC, (k % PK + 1) * 2 * FC)
                        x_hi, x_lo = blockT_hi[:, parity, k, :], blockT_lo[:, parity, k, :]
                        mm(h, x_hi, w1_hi[:, q, cols], start=False, stop=False)
                        mm(h, x_hi, w1_lo[:, j, q, cols], start=False, stop=False)
                        ins = mm(h, x_lo, w1_hi[:, q, cols], start=False, stop=(k == KT - 1))
                    ins.then_inc(w1_used, 1)

            def turn_act(i, j):
                s = i * STEPS + j
                pe.wait_ge(actv_ready, s + 1)
                if not isinstance(s, int) or s >= 1:
                    pe.wait_ge(actT_lo_ready, s)
                for k in range(FK):
                    ins = pe.transpose(ps[:, B_T, k * P:(k + 1) * P], act_v[:, j % 2, k * P:(k + 1) * P], ident[:, :])
                ins.then_inc(act_turned, 1)

            def w2_step(i, j, parity):
                s = i * STEPS + j
                pe.wait_ge(actT_lo_ready, s + 1)
                pe.wait_ge(w2_lo_ready, s + 1)
                if j == 0:
                    if not (isinstance(i, int) and i == 0):
                        pe.wait_ge(y_ready, i)
                    for n in range(2):
                        mm(ps[:, B_Y + n, :], bias_sel[:, parity, :], bias_split[:, 2 * FF + n * 512:2 * FF + (n + 1) * 512],
                           start=True, stop=False)
                b, last = j % 2, j == STEPS - 1
                for n in range(2):
                    cols = slice(n * 512, (n + 1) * 512)
                    mm(ps[:, B_Y + n, :], actT[:, b, :], ring2_v[:, j, 0, cols], start=False, stop=False)
                for n in range(2):
                    cols = slice(n * 512, (n + 1) * 512)
                    mm(ps[:, B_Y + n, :], actT_hi[:, b, :], w2_hi[:, b, cols], start=False, stop=False)
                    mm(ps[:, B_Y + n, :], actT_hi[:, b, :], w2_lo[:, j, cols], start=False, stop=False)
                    ins = mm(ps[:, B_Y + n, :], actT_lo[:, b, :], w2_hi[:, b, cols], start=False, stop=last)
                ins.then_inc(w2_done, 1)

            def compute(i, parity):
                first = isinstance(i, int) and i == 0
                last = isinstance(i, int) and i == E - 1
                w1_step(i, 0, parity)
                if not first:
                    turn_act(i - 1, 3)
                    w2_step(i - 1, 2, 1 - parity)
                w1_step(i, 1, parity)
                turn_act(i, 0)
                if not first:
                    w2_step(i - 1, 3, 1 - parity)
                w1_step(i, 2, parity)
                turn_act(i, 1)
                w2_step(i, 0, parity)
                if not last:
                    turn_block(i + 1, 1 - parity)
                w1_step(i, 3, parity)
                turn_act(i, 2)
                w2_step(i, 1, parity)

            def drain(i, parity):
                turn_act(i, 3)
                w2_step(i, 2, parity)
                w2_step(i, 3, parity)

            pe.wait_ge(biases_ready, 2)
            pe.wait_ge(ovf_ready, 1)
            turn_block(0, 0)
            expert_blocks(pe, compute)
            drain(E - 1, 1)

            def overflow(o, i):
                pe.wait_ge(rows_ovf, (o + 1) * 16)
                pe.wait_ge(rows_lo, i * 2)
                turn_rows(gathered[:, 0, :], B_X).then_inc(rows_turned, 1)
                for j in range(STEPS):
                    w1_step(i, j, 0)
                    if j >= 1:
                        turn_act(i, j - 1)
                    if j >= 2:
                        w2_step(i, j - 2, 0)
                drain(i, 0)

            overflow_blocks(pe, overflow_count(pe), overflow)

        @block.vector
        def _(dve):
            v = nc.vector
            chain = [0]

            def then(ins):
                chain[0] += 1
                ins.then_inc(dve_step, 1)
                dve.wait_ge(dve_step, chain[0])

            def norm(src, dst, gain, std_col, r_col, done):
                then(v.reciprocal(stat[:, r_col:r_col + 1], stat[:, std_col:std_col + 1]))
                return v.scalar_tensor_tensor(out=dst, in0=src, scalar=stat[:, r_col:r_col + 1], in1=gain,
                                              op0=ALU.mult, op1=ALU.mult).then_inc(done, 1)

            def low_tile(m):
                dve.wait_ge(tile_hi, m + 1)
                raw, low, high = weight_tile(m)
                v.tensor_tensor(low, raw, high.bitcast(F32), ALU.subtract).then_inc(tile_lo, 1)

            def low_xn(t):
                for b in range(2):
                    dve.wait_ge(xn_hi, 2 * t + b + 1)
                    half = slice(4 * b, 4 * b + 4)
                    v.tensor_tensor(xnT_lo[:, t, half, :], ps[:, 2 * (t % 2) + b, :].rearrange("p (k t) -> p k t", k=4),
                                    xnT_hi[:, half, t * P:(t + 1) * P].bitcast(F32), ALU.subtract).then_inc(xn_lo, 1)

            v.memset(u_pad[:, 0:CONV_K - 1], 0.0)
            then(v.memset(chosen_cum[:, 0, :], 0.0))

            dve.wait_ge(gains_in, 16)
            for t in range(TB):
                dve.wait_ge(std_ready, t + 1)
                if t >= 2:
                    dve.wait_ge(xn_turned, t - 1)
                norm(X[:, t, :], normed[:, t % 2, :], gain_a[:, :], X_STD + t, X_R + t, xn_ready)
                if t >= 1:
                    low_xn(t - 1)
            low_xn(TB - 1)

            low_tile(0)
            low_tile(1)
            dve.wait_ge(proj_done, 1)
            v.tensor_copy(kT[0:HD, 0, :], ps[0:HD, 4, :]).then_inc(k_ready, 1)
            v.tensor_copy(kT[HD:P, 1, :], ps[HD:P, 4, :]).then_inc(k_ready, 1)
            dve.wait_ge(k_ready, 2)
            dve.sem_inc(proj_dve, 1)
            low_tile(2)
            low_tile(3)
            dve.wait_ge(proj_done, 3)
            v.tensor_copy(qT[:, 1, :], ps[:, 6, :]).then_inc(proj_dve, 1)
            low_tile(4)
            low_tile(5)
            dve.wait_ge(proj_done, 5)
            v.tensor_copy(qT[:, 3, :], ps[:, 4, :]).then_inc(proj_dve, 1)
            for part in range(3):
                low_tile(QKV_TILES + part)

            def attended(n):
                dve.wait_ge(osq_ready, n + 1)
                v.tensor_tensor(attnT[:, :, n * P:(n + 1) * P], ps[:, 6 + n % 2, :].rearrange("p (c t) -> p c t", c=CT),
                                g_attn[:, :].unsqueeze(2).to_broadcast([P, CT, P]), ALU.mult).then_inc(o_ready, 1)
                v.tensor_reduce(attn_sqs[:, n * P:(n + 1) * P], attn_sq[:, :].rearrange("p (c t) -> p t c", c=CT), AX_X, ALU.add).then_inc(osqs_ready, 1)

            def biased_scores(n, odd):
                s0 = 0 if n else P
                at = slice(odd * HEADS // 2, (odd + 1) * HEADS // 2)
                dve.wait_ge(scores_done, 2 * n + odd + 1)
                if n >= 1:
                    dve.wait_ge(probs_turned, GRP * (n - 1) + 2 * (odd + 1))
                then(v.scalar_tensor_tensor(out=scores[:, at, s0:], in0=ps[:, 2 * odd:2 * odd + 2, :].rearrange("p b (h s) -> p (b h) s", h=2)[:, :, s0:],
                                            scalar=HD ** -0.5, in1=alibi[:, at, s0:], op0=ALU.mult, op1=ALU.add))
                dve.sem_inc(scores_read, 1)

            def low_w_out(order):
                dve.wait_ge(wout_hi, order + 1)
                k = (W_OUT_EARLY + W_OUT_LATE)[order]
                v.tensor_tensor(w_out_lo[:, k, :], w_out_sb[:, k, :], w_out_hi[:, W_OUT_PLACES[k], :].bitcast(F32), ALU.subtract).then_inc(wout_lo, 1)

            def low_mix(t):
                dve.wait_ge(mix_hi, t + 1)
                rows = slice(t * P, (t + 1) * P)
                v.tensor_tensor(attnT_lo[:, :, rows], attnT[:, :, rows], mixT_hi[:, 0:CT, rows].bitcast(F32), ALU.subtract)
                v.tensor_tensor(convT_lo[:, :, rows], convT[:, :, rows], mixT_hi[:, CT:KT, rows].bitcast(F32), ALU.subtract).then_inc(mix_lo, 1)

            dve.wait_ge(alibi_ready, 1)
            dve.wait_ge(small_in, 16 * 8)
            for n in range(TB):
                k0 = 0 if n else 1
                s0 = k0 * P
                if n == 0:
                    biased_scores(0, 0)
                biased_scores(n, 1)
                then(v.tensor_reduce(smax[:, 0, :], scores[:, :, s0:], AX_X, ALU.max))
                then(v.tensor_tensor(smax[:, 1, :], smax[:, 0, :], sink_b[:, :], ALU.max))
                then(v.tensor_scalar(smax[:, 2, :], smax[:, 1, :], -1.0, None, ALU.mult))
                v.tensor_tensor(smax[:, 3, :], smax[:, 2, :], sink_b[:, :], ALU.add).then_inc(negmax_ready, 1)
                if n < TB - 1:
                    for part in range(3):
                        low_tile(QKV_TILES + 3 * (n + 1) + part)
                else:
                    low_w_out(0)
                    low_w_out(1)
                dve.wait_ge(exp_done, n + 1)
                then(v.tensor_tensor(smax[:, 5, :], smax[:, 4, :], esink[:, :], ALU.add))
                then(v.reciprocal(smax[:, 5, :], smax[:, 5, :]))
                v.tensor_tensor(scores[:, :, s0:], scores[:, :, s0:], smax[:, 5, :].unsqueeze(2).to_broadcast([P, HEADS, 2 * P - s0]),
                                ALU.mult).then_inc(probs_ready, 1)
                dve.wait_ge(c_ready, n + 1)
                dve.wait_ge(part_done, 3 * n + 2)
                then(v.tensor_tensor(u_pad[:, CONV_K - 1:], c_gate, ps[:, 1, :], ALU.mult))
                dve.sem_inc(u_ready, 1)
                if n >= 1:
                    dve.wait_ge(sq_ready, n)
                then(v.tensor_scalar(conv_y[:, :], u_pad[:, 0:SEQ], conv_wc[:, 0, n:n + 1], None, ALU.mult))
                for w in range(1, CONV_K):
                    then(v.scalar_tensor_tensor(out=conv_y[:, :], in0=u_pad[:, w:w + SEQ], scalar=conv_wc[:, w, n:n + 1],
                                                in1=conv_y[:, :], op0=ALU.mult, op1=ALU.add))
                if n >= 1:
                    attended(n - 1)
                if n == TB - 1:
                    low_w_out(2)
                    low_w_out(3)
                dve.wait_ge(part_done, 3 * n + 3)
                then(v.tensor_tensor(conv_y[:, :], conv_y[:, :], ps[:, 2, :], ALU.mult))
                dve.sem_inc(conv_read, 1)
                dve.sem_inc(convy_ready, 1)
                for c in (1, 3):
                    dve.wait_ge(probs_turned, GRP * n + c + 1)
                    if c == 1 and n >= 1:
                        dve.wait_ge(pv_done, n)
                    v.tensor_copy(probsT[:, 2 * c:2 * c + 2, k0:2, :],
                                  ps[:, 5, :].rearrange("p (h k t) -> p h k t", h=2, k=2)[:, :, k0:2, :]).then_inc(pT_dve, 1)
                    if c == 1:
                        v.tensor_scalar(convT[:, n, :], conv_y[:, :], g_conv[:, n:n + 1], None, ALU.mult).then_inc(convT_ready, 1)
                        if n < TB - 1:
                            biased_scores(n + 1, 0)
            for order in range(4, KT):
                low_w_out(order)
                if order == 4:
                    low_mix(0)
            attended(TB - 1)
            dve.wait_ge(sq_ready, CT)
            v.tensor_reduce(conv_sqs[:, :], conv_sq.rearrange("p c t -> p t c"), AX_X, ALU.add).then_inc(csqs_ready, 1)
            low_mix(1)

            dve.wait_ge(gstd_ready, 1)
            then(v.reciprocal(r_group[:, :, :].rearrange("p g t -> p (g t)"), stat[:, A_STD:A_STD + 2 * TB]))

            def residual(t, n):
                dve.wait_ge(oproj_done, 2 * t + n + 1)
                if n == 0:
                    dve.wait_ge(x_again[t], 16)
                xt = X[:, t, n * 512:(n + 1) * 512]
                then(v.scalar_tensor_tensor(out=xt, in0=ps[:, 2 * n, :], scalar=r_group[:, 0, t:t + 1], in1=xt, op0=ALU.mult, op1=ALU.add))
                v.scalar_tensor_tensor(out=xt, in0=ps[:, 2 * n + 1, :], scalar=r_group[:, 1, t:t + 1],
                                       in1=xt, op0=ALU.mult, op1=ALU.add).then_inc(x2_half, 1)

            def second_norm(t):
                dve.wait_ge(std2_ready, t + 1)
                if t >= 2:
                    dve.wait_ge(h2_turned, t - 1)
                    dve.wait_ge(h2_stored, 16 * t)
                norm(X[:, t, :], normed[:, t % 2, :], gain_ffn[:, :], H_STD + t, H_R + t, h2_ready)

            def turned_h2(t):
                dve.wait_ge(h2_turned, t + 1)
                v.tensor_copy(xnT[:, 4:8, t * P:(t + 1) * P],
                              ps[:, 5, :].rearrange("p (k t) -> p k t", k=4)).then_inc(h2T_b, 1)

            def select(t):
                b = t % 2
                dve.wait_ge(logits_done, t + 1)
                then(v.tensor_copy(logit[:, b, :], ps[:, 6, 0:E]))
                then(v.max(top8[:, b, :], logit[:, b, :]))
                v.tensor_scalar(rt_small[:, b, 0:1], top8[:, b, 0:1], -1.0, None, ALU.mult).then_inc(negtop_ready, 1)
                then(v.max_index(top8_i[:, b, :], top8[:, b, :], logit[:, b, :]))
                then(v.tensor_copy(top_e[:, b, :], top8_i[:, b, 0:TOPK]))
                then(v.tensor_tensor(onehot[:, b, :, :], iota_e[:, :, :], top_e[:, b, :].unsqueeze(2).to_broadcast([P, TOPK, E]), ALU.is_equal))
                with nc.allow_low_precision(reason="sums of zeros and ones, at most 4"):
                    then(v.tensor_reduce(chosen[:, t, :], onehot[:, b, :, :].rearrange("p k e -> p e k"), AX_X, ALU.add))
                    v.tensor_tensor(chosen_cum[:, t + 1, :], chosen_cum[:, t, :], chosen[:, t, :], ALU.add).then_inc(chosen_ready, 1)

            def gates(t):
                b = t % 2
                then(v.tensor_tensor(smaller[:, :, :], top_e[:, b, :].unsqueeze(2).to_broadcast([P, TOPK, TOPK]),
                                     top_e[:, b, :].unsqueeze(1).to_broadcast([P, TOPK, TOPK]), ALU.is_gt))
                then(v.tensor_reduce(row_f[:, b, :], smaller[:, :, :], AX_X, ALU.add))
                v.tensor_scalar(entry[:, t, :, 0:1], row_f[:, b, :].unsqueeze(2), first_row[:, t:t + 1], None, ALU.add)
                dve.wait_ge(gexp_ready, t + 1)
                then(v.reciprocal(rt_small[:, b, 2:3], rt_small[:, b, 1:2]))
                then(v.tensor_scalar(entry[:, t, :, 1:2].bitcast(F32), top_x[:, b, :].unsqueeze(2), rt_small[:, b, 2:3], None, ALU.mult))
                dve.sem_inc(entries_ready, 1)

            def place(t):
                b = t % 2
                dve.wait_ge(rank_done, t + 1)
                then(v.scalar_tensor_tensor(out=rankrow[:, b, :], in0=ps[:, 7, 0:E], scalar=float(E), in1=iota_e[:, 0, :],
                                            op0=ALU.mult, op1=ALU.add))
                then(v.tensor_tensor(picked[:, :, :], onehot[:, b, :, :], rankrow[:, b, :].unsqueeze(1).to_broadcast([P, TOPK, E]), ALU.mult))
                then(v.tensor_reduce(row_f[:, b, :], picked[:, :, :], AX_X, ALU.add))
                v.tensor_copy(row_i[:, t, :], row_f[:, b, :]).then_inc(placed, 1)
                dve.wait_ge(placed, t + 1)

            residual(0, 0)
            low_mix(2)
            residual(0, 1)
            low_mix(3)
            second_norm(0)
            for t in range(1, TB):
                residual(t, 0)
                turned_h2(t - 1)
                if t >= 2:
                    place(t - 2)
                    gates(t - 2)
                residual(t, 1)
                second_norm(t)
                select(t - 1)
            turned_h2(TB - 1)
            place(TB - 2)
            gates(TB - 2)
            select(TB - 1)
            place(TB - 1)
            gates(TB - 1)

            dve.wait_ge(counts_done, 1)
            then(v.tensor_copy(ovf_nb[:, 0:1], ps[0:E, 0, 0:1]))
            then(v.tensor_scalar(ovf_nb[:, 1:2], ovf_nb[:, 0:1], float(P), None, ALU.is_gt))
            for n in range(2, LIST_BLOCKS):
                then(v.tensor_scalar(ovf_nb[:, 2:3], ovf_nb[:, 0:1], float(n * P), None, ALU.is_gt))
                then(v.tensor_tensor(ovf_nb[:, 1:2], ovf_nb[:, 1:2], ovf_nb[:, 2:3], ALU.add))
            v.tensor_copy(ovf_nb16[:, :], ovf_nb[:, 1:2].to_broadcast([E, OVF_ROWS])).then_inc(nb_ready, 1)
            dve.wait_ge(prefix_done, 1)
            then(v.tensor_copy(ovf_m[:, 0:2, :].rearrange("p a e -> p (a e)"), ps[0:OVF_ROWS, 1, 0:2 * E]))
            dve.sem_inc(ovf_ready, 1)
            then(v.tensor_scalar(ovf_m[:, 2, :], ovf_m[:, 0, :], iota_o[:, 0:1], None, ALU.is_le))
            then(v.tensor_reduce(ovf_f[:, 0:1], ovf_m[:, 2, :], AX_X, ALU.add))
            then(v.tensor_scalar(ovf_f[:, 0:1], ovf_f[:, 0:1], float(E - 1), None, ALU.min))
            then(v.tensor_tensor(ovf_m[:, 1, :], ovf_m[:, 1, :], ovf_m[:, 2, :], ALU.mult))
            then(v.tensor_reduce(ovf_f[:, 1:2], ovf_m[:, 1, :], AX_X, ALU.add))
            then(v.tensor_tensor(ovf_f[:, 2:3], iota_o[:, :], ovf_f[:, 1:2], ALU.subtract))
            then(v.tensor_scalar(ovf_f[:, 2:3], ovf_f[:, 2:3], 1.0, float(E), ALU.add, ALU.mult))
            then(v.tensor_tensor(ovf_f[:, 1:2], ovf_f[:, 2:3], ovf_f[:, 0:1], ALU.add))
            then(v.tensor_scalar(ovf_f[:, 1:2], ovf_f[:, 1:2], float(LIST_BLOCKS * E - 1), 0.0, ALU.min, ALU.max))
            v.tensor_copy(ovf_f[:, 2:3], ovf_m[:, 0, E - 1:E])
            then(v.memset(ovf_f[:, 3:4], 0.0))
            v.tensor_copy(ovf_tab[:, :], ovf_f[:, 0:4]).then_inc(ovf_ready, 1)
            def low_rows(i, parity):
                for b in range(2):
                    dve.wait_ge(rows_hi, i * 2 + b + 1)
                    half = slice(4 * b, 4 * b + 4)
                    v.tensor_tensor(blockT_lo[:, parity, half, :], ps[:, B_X + b, :].rearrange("p (k t) -> p k t", k=4),
                                    blockT_hi[:, parity, half, :].bitcast(F32), ALU.subtract).then_inc(rows_lo, 1)

            def low_piece(i, j, q):
                dve.wait_ge(hi_ready, (i * STEPS + j) * PIECES + q + 1)
                v.tensor_tensor(w1_lo[:, j, q, :], raw_piece(j, q), w1_hi[:, q, :].bitcast(F32), ALU.subtract).then_inc(lo_ready, 1)

            def low_w2(i, j):
                dve.wait_ge(w2_hi_ready, i * STEPS + j + 1)
                v.tensor_tensor(w2_lo[:, j, :], ring2_v[:, j, FK - 1, :], w2_hi[:, j % 2, :].bitcast(F32), ALU.subtract).then_inc(w2_lo_ready, 1)

            def low_act(i, j):
                dve.wait_ge(actT_hi_ready, i * STEPS + j + 1)
                v.tensor_tensor(actT_lo[:, j % 2, :], ps[:, B_T, FC - P:FC], actT_hi[:, j % 2, :].bitcast(F32),
                                ALU.subtract).then_inc(actT_lo_ready, 1)

            def swiglu(i, j, before, after):
                if after:
                    for q in range(PIECES - 1):
                        low_piece(*after, q)
                s = i * STEPS + j
                b = j % 2
                h = ps[:, B_H + b, :]
                dve.wait_ge(w1_used, (s + 1) * PIECES)
                v.tensor_scalar(glu_c[:, b, :], h[:, 0:FC], LIMIT, None, ALU.min).then_inc(glu_ready, 1)
                v.tensor_scalar(lin_c[:, b, :], h[:, FC:2 * FC], LIMIT, -LIMIT, ALU.min, ALU.max).then_inc(h_read, 1)
                if before:
                    low_act(*before)
                if after:
                    low_piece(*after, PIECES - 1)
                dve.wait_ge(glu_ready, s + 1)
                dve.wait_ge(h_read, s + 1)
                v.scalar_tensor_tensor(out=prod[:, b, :], in0=lin_c[:, b, :], scalar=1.0, in1=glu_c[:, b, :],
                                       op0=ALU.add, op1=ALU.mult).then_inc(prod_ready, 1)
                dve.wait_ge(prod_ready, s + 1)
                dve.wait_ge(sig_ready, s + 1)
                if not isinstance(s, int) or s >= 2:
                    dve.wait_ge(act_turned, s - 1)
                v.tensor_tensor(act_v[:, b, :], prod[:, b, :], sig[:, b, :], ALU.mult).then_inc(actv_ready, 1)
                if before:
                    low_w2(*before)

            def elementwise(i, parity):
                first = isinstance(i, int) and i == 0
                last = isinstance(i, int) and i == E - 1
                for j in range(STEPS):
                    swiglu(i, j, (i, j - 1) if j else None if first else (i - 1, STEPS - 1), (i, j + 1) if j < STEPS - 1 else None if last else (i + 1, 0))
                    if j == 2 and not last:
                        if not first:
                            dve.wait_ge(w1_used, i * STEPS * PIECES)
                        low_rows(i + 1, 1 - parity)

            for q in range(PIECES - 1):
                low_piece(0, 0, q)
            dve.wait_ge(slots_in, 16)
            v.tensor_scalar(slot_tok[:, :].unsqueeze(2), slots[:, :, :, :].rearrange("p b e w -> p (b e) w")[:, :, 0:1],
                            2, None, ALU.logical_shift_right).then_inc(tok_ready, 1)
            low_piece(0, 0, PIECES - 1)
            low_rows(0, 0)
            expert_blocks(dve, elementwise)
            low_act(E - 1, STEPS - 1)
            low_w2(E - 1, STEPS - 1)

            def add_rows():
                for k in range(TOPK - 1):
                    for t in range(TB):
                        add_row(k, t)

            def add_row(k, t):
                dve.wait_ge(yrow_in[k][t], 16)
                if k:
                    dve.wait_ge(sum_ready, (k - 1) * TB + t + 1)
                v.tensor_tensor(X[:, t, :], X[:, t, :], y_rows[:, k, t, :], ALU.add).then_inc(sum_ready, 1)

            n_ovf = overflow_count(dve)
            with dve.If(n_ovf < 1):
                add_rows()

            def overflow(o, i):
                low_rows(i, 0)
                for q in range(PIECES):
                    low_piece(i, 0, q)
                for j in range(STEPS):
                    swiglu(i, j, (i, j - 1) if j else None, (i, j + 1) if j < STEPS - 1 else None)
                low_act(i, STEPS - 1)
                low_w2(i, STEPS - 1)

            overflow_blocks(dve, n_ovf, overflow, add_rows)

            dve.wait_ge(gfinal_in, 16)

            def last_norm(t):
                dve.wait_ge(fstd_ready, t + 1)
                v.reciprocal(stat[:, F_R + t:F_R + t + 1], stat[:, F_STD + t:F_STD + t + 1]).then_inc(dve_final, 1)
                dve.wait_ge(dve_final, t + 1)
                v.scalar_tensor_tensor(out=y_rows[:, 0, t, :], in0=X[:, t, :], scalar=stat[:, F_R + t:F_R + t + 1], in1=gain_a[:, :],
                                       op0=ALU.mult, op1=ALU.mult).then_inc(fin_ready, 1)

            for t in range(TB):
                add_row(TOPK - 1, t)
                dve.wait_ge(sum_ready, (TOPK - 1) * TB + t + 1)
                if t:
                    last_norm(t - 1)
            last_norm(TB - 1)

        @block.scalar
        def _(act):
            a = nc.scalar
            chain = [0]

            def then(ins):
                chain[0] += 1
                ins.then_inc(act_step, 1)
                act.wait_ge(act_step, chain[0])

            def row_std(src, junk, n, total, col, done):
                then(a.activation(junk, src, ACT.Square, accum_out=stat[:, total:total + 1]))
                a.activation(stat[:, col:col + 1], stat[:, total:total + 1], ACT.Sqrt, scale=1.0 / n, bias=eps_col[:, :]).then_inc(done, 1)

            def load_sqrt():
                a.activation(table_use[:, :], eps_col[:, :], ACT.Sqrt)

            def high_tile(m):
                if m == 0:
                    act.wait_ge(qkv_in, 16 * KT // 2)
                elif 2 <= m < QKV_TILES:
                    act.wait_ge(proj_done, m - 1)
                elif m == QKV_TILES:
                    act.wait_ge(conv_in, 16 * KT)
                    act.wait_ge(proj_done, QKV_TILES)
                elif m >= QKV_TILES + 6:
                    act.wait_ge(part_done, 3 * ((m - QKV_TILES) // 3 - 1))
                raw, _, high = weight_tile(m)
                a.activation(high, raw, ACT.Copy).then_inc(tile_hi, 1)

            def high_xn(t):
                act.wait_ge(xn_turned, t + 1)
                for b in range(2):
                    a.activation(xnT_hi[:, 4 * b:4 * b + 4, t * P:(t + 1) * P], ps[:, 2 * (t % 2) + b, :].rearrange("p (k t) -> p k t", k=4),
                                 ACT.Copy).then_inc(xn_hi, 1)

            act.wait_ge(consts_ready, 1)
            load_sqrt()
            waste = probsT[:, 0:4, :, :].rearrange("p h k s -> p (h k s)")
            for t in range(TB):
                act.wait_ge(x_in[t], 16)
                row_std(X[:, t, :], waste, D, X_SUM + t, X_STD + t, std_ready)
                if t >= 1:
                    high_xn(t - 1)
            high_xn(TB - 1)

            high_tile(0)
            high_tile(1)
            high_tile(2)
            act.wait_ge(proj_done, 2)
            a.activation(qT[:, 0, :], ps[:, 5, :], ACT.Copy).then_inc(proj_act, 1)
            high_tile(3)
            high_tile(4)
            act.wait_ge(proj_done, 4)
            a.activation(qT[:, 2, :], ps[:, 7, :], ACT.Copy).then_inc(proj_act, 1)
            high_tile(5)
            act.wait_ge(proj_done, 6)
            a.activation(c_gate, ps[:, 5, :], ACT.Copy).then_inc(vT_ready, 1)
            act.sem_inc(proj_act, 1)
            for part in range(3):
                high_tile(QKV_TILES + part)
            act.wait_ge(vT_turned, 1)
            a.activation(v_sb, ps[:, 6, :].rearrange("p (t d) -> p t d", t=TB), ACT.Copy).then_inc(proj_act, 1)

            def square_attended(n):
                act.wait_ge(pv_done, n + 1)
                if n >= 1:
                    act.wait_ge(osqs_ready, n)
                a.activation(attn_sq[:, :], ps[:, 6 + n % 2, :], ACT.Square).then_inc(osq_ready, 1)

            def high_w_out(order):
                if order == 0:
                    act.wait_ge(wout_early, 16 * len(W_OUT_EARLY))
                    act.wait_ge(biases_ready, 2)
                elif order == 2:
                    act.wait_ge(scores_read, 2 * TB)
                elif order == 4:
                    act.wait_ge(part_done, 3 * CT)
                elif order == len(W_OUT_EARLY):
                    act.wait_ge(wout_late, 16 * len(W_OUT_LATE))
                k = (W_OUT_EARLY + W_OUT_LATE)[order]
                a.activation(w_out_hi[:, W_OUT_PLACES[k], :], w_out_sb[:, k, :], ACT.Copy).then_inc(wout_hi, 1)

            def high_mix(t):
                act.wait_ge(o_ready, t + 1)
                act.wait_ge(convT_ready, CT)
                rows = slice(t * P, (t + 1) * P)
                a.activation(mixT_hi[:, 0:CT, rows], attnT[:, :, rows], ACT.Copy)
                a.activation(mixT_hi[:, CT:KT, rows], convT[:, :, rows], ACT.Copy).then_inc(mix_hi, 1)

            for n in range(TB):
                k0 = 0 if n else 1
                if n < TB - 1:
                    for part in range(3):
                        high_tile(QKV_TILES + 3 * (n + 1) + part)
                else:
                    high_w_out(0)
                    high_w_out(1)
                act.wait_ge(negmax_ready, n + 1)
                for h in range(HEADS):
                    a.activation(scores[:, h, k0 * P:], scores[:, h, k0 * P:], ACT.Exp, bias=smax[:, 2, h:h + 1],
                                 accum_out=smax[:, 4, h:h + 1])
                a.activation(esink[:, :], smax[:, 3, :], ACT.Exp).then_inc(exp_done, 1)
                act.wait_ge(part_done, 3 * n + 1)
                if n >= 1:
                    act.wait_ge(u_ready, n)
                a.activation(c_gate, ps[:, 0, :], ACT.Copy).then_inc(c_ready, 1)
                if n >= 1:
                    square_attended(n - 1)
                if n == TB - 1:
                    high_w_out(2)
                    high_w_out(3)
                for c in (0, 2):
                    act.wait_ge(probs_turned, GRP * n + c + 1)
                    if c == 0 and n >= 1:
                        act.wait_ge(pv_done, n)
                    a.activation(probsT[:, 2 * c:2 * c + 2, k0:2, :],
                                 ps[:, 4, :].rearrange("p (h k t) -> p h k t", h=2, k=2)[:, :, k0:2, :], ACT.Copy).then_inc(pT_act, 1)
                act.wait_ge(convy_ready, n + 1)
                a.activation(conv_sq[:, n, :], conv_y[:, :], ACT.Square).then_inc(sq_ready, 1)
                if n == TB - 1:
                    for order in range(4, KT):
                        high_w_out(order)
                        if order == 4:
                            high_mix(0)
            square_attended(TB - 1)
            for t in range(1, TB):
                high_mix(t)

            act.wait_ge(sums_done, 1)
            a.activation(stat[:, A_STD:A_STD + 2 * TB], ps[:, 4, 0:2 * TB], ACT.Sqrt, scale=1.0 / CW, bias=eps_col[:, :]).then_inc(gstd_ready, 1)

            def turned_h2(t):
                act.wait_ge(h2_turned, t + 1)
                a.activation(xnT[:, 0:4, t * P:(t + 1) * P], ps[:, 4, :].rearrange("p (k t) -> p k t", k=4),
                             ACT.Copy).then_inc(h2T_a, 1)

            def gate_exp(t):
                act.wait_ge(negtop_ready, t + 1)
                b = t % 2
                a.activation(top_x[:, b, :], top8[:, b, 0:TOPK], ACT.Exp, bias=rt_small[:, b, 0:1],
                             accum_out=rt_small[:, b, 1:2]).then_inc(gexp_ready, 1)

            for t in range(TB):
                if t >= 1:
                    turned_h2(t - 1)
                load_sqrt()
                act.wait_ge(x2_half, 2 * (t + 1))
                row_std(X[:, t, :], waste, D, H_SUM + t, H_STD + t, std2_ready)
                if t >= 1:
                    gate_exp(t - 1)
                act.wait_ge(h2_ready, t + 1)
                act.dma_start(h2_dram[t * P:(t + 1) * P, :], normed[:, t % 2, :]).then_inc(h2_stored, 16)
            turned_h2(TB - 1)
            gate_exp(TB - 1)

            def high_rows(i, parity):
                act.wait_ge(rows_turned, i + 1)
                for b in range(2):
                    a.activation(blockT_hi[:, parity, 4 * b:4 * b + 4, :], ps[:, B_X + b, :].rearrange("p (k t) -> p k t", k=4),
                                 ACT.Copy).then_inc(rows_hi, 1)

            def high_piece(i, j, q):
                n = (i * STEPS + j) * PIECES + q
                act.wait_ge(w1_in[j], (i + 1) * 32)
                if not isinstance(n, int) or n >= PIECES:
                    act.wait_ge(w1_used, n - PIECES + 1)
                a.activation(w1_hi[:, q, :], raw_piece(j, q), ACT.Copy).then_inc(hi_ready, 1)

            def turned_act(i, j):
                s = i * STEPS + j
                act.wait_ge(act_turned, s + 1)
                if not isinstance(s, int) or s >= 2:
                    act.wait_ge(w2_done, s - 1)
                a.activation(actT[:, j % 2, :], ps[:, B_T, 0:P], ACT.Copy)
                a.activation(actT_hi[:, j % 2, :], ps[:, B_T, FC - P:FC], ACT.Copy).then_inc(actT_hi_ready, 1)

            def high_w2(i, j):
                s = i * STEPS + j
                act.wait_ge(w2_in[j], (i + 1) * 16)
                if not isinstance(s, int) or s >= 2:
                    act.wait_ge(w2_done, s - 1)
                a.activation(w2_hi[:, j % 2, :], ring2_v[:, j, FK - 1, :], ACT.Copy).then_inc(w2_hi_ready, 1)

            def sigmoid(i, j):
                s = i * STEPS + j
                act.wait_ge(glu_ready, s + 1)
                if not isinstance(s, int) or s >= 2:
                    act.wait_ge(actv_ready, s - 1)
                a.activation(sig[:, j % 2, :], glu_c[:, j % 2, :], ACT.Sigmoid, scale=ALPHA).then_inc(sig_ready, 1)

            def result(i, parity):
                act.wait_ge(w2_done, (i + 1) * STEPS)
                act.wait_ge(slot_ready, i + 1)
                if isinstance(i, int):
                    if i >= 2:
                        act.wait_ge(y_out[parity], 16 * (i // 2))
                else:
                    act.wait_ge(y_out[parity], (i - parity) // 2 * 16)
                a.activation(gated_y[:, parity, :], ps_y, ACT.Copy,
                             scale=cur_slot[:, parity, 1:2].bitcast(F32)).then_inc(y_ready, 1)

            def step(i, j, before, after):
                if after:
                    for q in range(PIECES - 1):
                        high_piece(*after, q)
                if before:
                    turned_act(*before)
                sigmoid(i, j)
                if after:
                    high_piece(*after, PIECES - 1)
                if before:
                    high_w2(*before)

            def evacuate(i, parity):
                first = isinstance(i, int) and i == 0
                last = isinstance(i, int) and i == E - 1
                for j in range(STEPS):
                    step(i, j, (i, j - 1) if j else None if first else (i - 1, STEPS - 1),
                         (i, j + 1) if j < STEPS - 1 else None if last else (i + 1, 0))
                    if j == 1 and not first:
                        result(i - 1, 1 - parity)
                    if j == 2 and not last:
                        if not first:
                            act.wait_ge(w1_used, i * STEPS * PIECES)
                        high_rows(i + 1, 1 - parity)

            for q in range(PIECES):
                high_piece(0, 0, q)
            act.wait_ge(h2_stored, 16 * TB)
            high_rows(0, 0)
            expert_blocks(act, evacuate)
            turned_act(E - 1, STEPS - 1)
            high_w2(E - 1, STEPS - 1)
            result(E - 1, 1)

            def overflow(o, i):
                high_rows(i, 0)
                for q in range(PIECES):
                    high_piece(i, 0, q)
                for j in range(STEPS):
                    step(i, j, (i, j - 1) if j else None, (i, j + 1) if j < STEPS - 1 else None)
                turned_act(i, STEPS - 1)
                high_w2(i, STEPS - 1)
                act.wait_ge(w2_done, (i + 1) * STEPS)
                act.wait_ge(slot_ready, i + 1)
                act.wait_ge(y_out[0], 16 * E // 2)
                a.activation(gated_y[:, 0, :], ps_y, ACT.Copy, scale=cur_slot[:, 0, 1:2].bitcast(F32)).then_inc(y_ready, 1)

            overflow_blocks(act, overflow_count(act), overflow)

            load_sqrt()
            for t in range(TB):
                act.wait_ge(sum_ready, (TOPK - 1) * TB + t + 1)
                a.activation(y_rows[:, 1, t, :], X[:, t, :], ACT.Square, accum_out=stat[:, F_SUM + t:F_SUM + t + 1]).then_inc(act_final, 1)
                act.wait_ge(act_final, t + 1)
                a.activation(stat[:, F_STD + t:F_STD + t + 1], stat[:, F_SUM + t:F_SUM + t + 1], ACT.Sqrt, scale=1.0 / D, bias=eps_col[:, :]).then_inc(fstd_ready, 1)

        @block.gpsimd
        def _(pool):
            g = nc.gpsimd
            chain = [0]

            def then(ins):
                chain[0] += 1
                ins.then_inc(pool_step, 1)
                pool.wait_ge(pool_step, chain[0])

            def keep_unless_zero(view, base, pattern, mult, fill):
                return g.affine_select(out=view, in_=view, compare_op=ALU.not_equal, fill=fill, base=base,
                                       pattern=pattern, channel_multiplier=mult)

            g.memset(eps_col[:, :], EPS)
            g.memset(ones_col[:, :], 1.0)
            g.memset(ones_row[:, :], 1.0)
            g.memset(ones_bf[:, :], 1.0)
            g.memset(earlier[:, :], 1.0)
            g.memset(upto[:, :], 1.0)
            g.memset(ident_bf[:, :], 0.0)
            g.memset(expert_sel[:, :], 0.0)
            then(g.memset(ident[:, :], 0.0))
            then(keep_unless_zero(ident[:, :], 0, [[-1, P]], 1, 1.0))
            pool.sem_inc(consts_ready, 1)
            g.iota(alibi[:, 0, :], [[1, 2 * P]], base=-P, channel_multiplier=-1, allow_small_or_imprecise_dtypes=True)
            then(g.memset(list_fill, UNUSED))
            then(g.affine_select(out=alibi[:, 0, :], in_=alibi[:, 0, :], compare_op=ALU.is_ge, fill=NEG, base=P,
                                 pattern=[[-1, 2 * P]], channel_multiplier=1))
            then(g.affine_select(out=alibi[:, 0, :], in_=alibi[:, 0, :], compare_op=ALU.is_gt, fill=NEG, base=0,
                                 pattern=[[1, 2 * P]], channel_multiplier=-1))
            for h in range(HEADS - 1, -1, -1):
                then(g.tensor_scalar(alibi[:, h, :], alibi[:, 0, :], 2.0 ** (-8.0 * (place_head(h) + 1) / HEADS), None, ALU.mult))
            pool.sem_inc(alibi_ready, 1)
            g.dma_start(list_dram.rearrange("(p r) w -> p (r w)", p=P), list_fill).then_inc(list_filled, 16)
            then(keep_unless_zero(ident_bf[:, :], 0, [[-1, E]], 1, 1.0))
            then(g.affine_select(out=earlier[:, :], in_=earlier[:, :], compare_op=ALU.is_gt, fill=0.0, base=0,
                                 pattern=[[1, P]], channel_multiplier=-1))
            then(g.affine_select(out=upto[:, :], in_=upto[:, :], compare_op=ALU.is_ge, fill=0.0, base=0,
                                 pattern=[[1, E]], channel_multiplier=-1))
            for s in range(3):
                then(keep_unless_zero(expert_sel[:, :], -s * E, [[-1, E]], 1, 1.0))
            g.iota(iota_e[:, :, :], [[0, TOPK], [1, E]], base=0, channel_multiplier=0, allow_small_or_imprecise_dtypes=True)
            g.iota(iota_o[:, :], [[0, 1]], base=0, channel_multiplier=1, allow_small_or_imprecise_dtypes=True)
            then(g.iota(first_row[:, :], [[P * TOPK, TB]], base=0, channel_multiplier=TOPK, allow_small_or_imprecise_dtypes=True))
            pool.sem_inc(consts_ready, 1)

            def split(cols, n):
                raw = bias_raw[:, 0:n]
                for s in range(3):
                    for q in range(s, 3):
                        then(g.tensor_copy(bias_split[q * E:(q + 1) * E, cols:cols + n], raw[q * E:(q + 1) * E, :]))
                    if s < 2:
                        for q in range(s + 1, 3):
                            then(g.tensor_tensor(raw[q * E:(q + 1) * E, :], raw[q * E:(q + 1) * E, :],
                                                 bias_split[q * E:(q + 1) * E, cols:cols + n], ALU.subtract))

            pool.wait_ge(bias1_in, 48)
            split(0, 2 * FF)
            pool.sem_inc(biases_ready, 1)
            pool.wait_ge(bias2_in, 48)
            split(2 * FF, D)
            pool.sem_inc(biases_ready, 1)

            pool.wait_ge(probs_turned, GRP * TB)
            g.memset(gathered[:, :, :], 0.0).then_inc(rows_cleared, 1)

            pool.wait_ge(list_filled, 16)
            for t in range(TB):
                pool.wait_ge(entries_ready, t + 1)
                for k in range(TOPK):
                    g.indirect_dma_start(list_dram, bass.IndirectOffsetOnAxis(row_i[:, t, k:k + 1], 0), entry[:, t, k, :], None,
                                         bounds_check=SEQ * E - 1, oob_is_err=False).then_inc(list_written, 16)
            pool.wait_ge(list_written, 16 * TB * TOPK)
            g.dma_start(slots[:, :, :, :].rearrange("p b e w -> p b (e w)"),
                        list_dram.rearrange("(b p e) w -> p b (e w)", p=P, e=E)).then_inc(slots_in, 16)
            pool.wait_ge(slots_in, 16)
            pool.wait_ge(tok_ready, 1)
            pool.wait_ge(rows_cleared, 1)

            last_token, last_row = pool.to_reg(SEQ - 1), pool.to_reg(ROWS - 1)
            slots_flat = slots[:, :, :, :].rearrange("p b e w -> p (b e) w")

            def fetch(i, parity, expert, column, done):
                g.tensor_copy(cur_tok[:, parity, :], slot_tok[:, bass.ds(column, 1)])
                g.tensor_copy(bias_sel[:, parity, :], expert_sel[:, bass.ds(expert, 1)].to_broadcast([3 * E, P])).then_inc(cur_copied, 1)
                pool.wait_ge(cur_copied, i + 1)
                pool.sem_inc(cur_ready, 1)
                g.indirect_dma_start(gathered[:, parity, :], None, h2_dram, bass.IndirectOffsetOnAxis(cur_tok[:, parity, :], 0),
                                     bounds_check=last_token, oob_is_err=False).then_inc(done, 16)

            def prepare(i, parity):
                if not isinstance(i, int) or i >= 2:
                    pool.wait_ge(rows_turned, i - 1)
                    pool.wait_ge(w1_used, (i - 1) * STEPS * PIECES)
                fetch(i, parity, i, i, rows_in[parity])

            def take_slots(parity, column):
                g.tensor_copy(cur_slot[:, parity, :].unsqueeze(1), slots_flat[:, bass.ds(column, 1), :]).then_inc(slot_ready, 1)

            def scatter(i, parity, done):
                pool.wait_ge(slot_ready, i + 1)
                pool.wait_ge(y_ready, i + 1)
                pool.sem_inc(scatter_begun, 1)
                g.indirect_dma_start(y_dram, bass.IndirectOffsetOnAxis(cur_slot[:, parity, 0:1], 0), gated_y[:, parity, :], None,
                                     bounds_check=last_row, oob_is_err=False).then_inc(done, 16)

            def move(i, parity):
                if not (isinstance(i, int) and i == E - 1):
                    prepare(i + 1, 1 - parity)
                if not isinstance(i, int):
                    pool.wait_ge(y_out[parity], (i - parity) // 2 * 16)
                elif i >= 2:
                    pool.wait_ge(y_out[parity], 16 * (i // 2))
                take_slots(parity, i)
                if not (isinstance(i, int) and i == 0):
                    scatter(i - 1, 1 - parity, y_out[1 - parity])

            pool.wait_ge(h2_stored, 16 * TB)
            prepare(0, 0)
            pool.wait_ge(ovf_ready, 2)
            g.dma_start(ovf_dram, ovf_tab[:, :]).then_inc(ovf_stored, 16)
            pool.wait_ge(ovf_stored, 16)
            g.dma_start(ovf_row[0:1, :], ovf_dram.rearrange("(a o) w -> a (o w)", a=1)).then_inc(ovf_in, 16)
            expert_blocks(pool, move)
            scatter(E - 1, 1, y_out[1])
            for b in range(2):
                pool.wait_ge(y_out[b], 16 * E // 2)

            def overflow(o, i):
                e = pool.value_load(ovf_row[0:1, bass.ds(o * 4, 1)], min_val=0, max_val=E - 1)
                column = pool.value_load(ovf_row[0:1, bass.ds(o * 4 + 1, 1)], min_val=0, max_val=LIST_BLOCKS * E - 1)
                fetch(i, 0, e, column, rows_ovf)
                take_slots(0, column)
                scatter(i, 0, y_ovf)
                pool.wait_ge(y_ovf, (o + 1) * 16)

            overflow_blocks(pool, overflow_count(pool), overflow)
            pool.sem_inc(all_scattered, 1)


_INS = ["x", "g_mix", "w_in", "conv_w", "sinks", "g_attn_out", "g_conv_out", "w_out",
        "g_ffn", "w_router", "b_router", "w1", "b1", "w2", "b2", "g_final"]


def kernel(**inputs):
    import numpy as _np
    import concourse.bacc as _bacc
    from concourse import mybir as _mybir
    from concourse.bass_utils import run_bass_kernel_spmd as _run

    nc = _bacc.Bacc("TRN2", target_bir_lowering=False, num_devices=1)
    arrays, args = {}, []
    for name in _INS:
        a = _np.ascontiguousarray(inputs[name])
        arrays[f"in_{name}"] = a
        args.append(nc.dram_tensor(f"in_{name}", a.shape, _mybir.dt.from_np(a.dtype), kind="ExternalInput").ap())
    args.append(nc.dram_tensor("out", (1, SEQ, D), F32, kind="ExternalOutput").ap())
    layer_kernel(nc, *args)
    r = _run(nc, [arrays], core_ids=[0])
    return r.results[0]["out"]
```
